# Optimizing a Trainium2 kernel written in Bass

```python
import math
import jax, jax.numpy as jnp
from jax import lax
import numpy as np

D_MODEL = 1024
BATCH = 1
SEQ = 512
DEPTH = 1

CHUNK = 64
N_META = 16
META_PAD = (CHUNK - N_META % CHUNK) % CHUNK
RMS_EPS = 1e-6
GLA_HEADS = 4
GLA_DK = D_MODEL // 8
GLA_DV = D_MODEL // 4
GLA_GATE_RANK = 16
GLA_GATE_NORM = 16.0
GLA_QK = GLA_HEADS * GLA_DK
GLA_VW = GLA_HEADS * GLA_DV
SSD_D_INNER = 2 * D_MODEL
SSD_HEADDIM = 64
SSD_HEADS = SSD_D_INNER // SSD_HEADDIM
SSD_GROUPS = 4
SSD_HPG = SSD_HEADS // SSD_GROUPS
SSD_STATE = 128
SSD_CONV = 4
SSD_BC = SSD_GROUPS * SSD_STATE
SSD_XBC = SSD_D_INNER + 2 * SSD_BC
PEER_HEADS = 8
PEER_N_KEYS = 128
PEER_N_EXPERTS = PEER_N_KEYS * PEER_N_KEYS
PEER_KEY_DIM = 256
PEER_HALF = PEER_KEY_DIM // 2
PEER_TOPK = 16
PEER_BLOCK = 256
IN_SPLITS = (GLA_QK, GLA_QK, GLA_VW, GLA_VW, GLA_GATE_RANK, SSD_D_INNER, SSD_XBC, SSD_HEADS, D_MODEL, D_MODEL)
IN_WIDTH = GLA_QK * 2 + GLA_VW * 2 + GLA_GATE_RANK + SSD_D_INNER + SSD_XBC + SSD_HEADS + 2 * D_MODEL


def rmsnorm(x, w):
    xf = x.astype(jnp.float32)
    y = xf * lax.rsqrt(jnp.mean(xf * xf, axis=-1, keepdims=True) + RMS_EPS)
    return (y * w.astype(jnp.float32)).astype(x.dtype)

def split_cols(t, sizes):
    out, start = [], 0
    for s in sizes:
        out.append(t[..., start:start + s])
        start += s
    return out

def pad_front(t):
    return jnp.pad(t, [(0, 0), (META_PAD, 0)] + [(0, 0)] * (t.ndim - 2))

def to_chunks(t):
    b, lp = t.shape[:2]
    return jnp.moveaxis(t.reshape(b, lp // CHUNK, CHUNK, *t.shape[2:]), 1, 0)

def from_chunks(t):
    t = jnp.moveaxis(t, 0, 1)
    return t.reshape(t.shape[0], -1, *t.shape[3:])

def causal_dwconv(u, w, b):
    L = u.shape[1]
    up = jnp.pad(u, ((0, 0), (SSD_CONV - 1, 0), (0, 0)))
    return sum(up[:, i:i + L] * w[i] for i in range(SSD_CONV)) + b

def gla_chunk_step(S, inp):
    q, k, v, lg = inp
    G = jnp.cumsum(lg, axis=1)
    eG, eGn = jnp.exp(G), jnp.exp(-G)
    a_causal = jnp.einsum('bthk,bshk->bhts', q * eG, k * eGn)
    a_ahead = jnp.einsum('bthk,bshk->bhts', q * eGn, k * eG)
    tri = jnp.tril(jnp.ones((CHUNK, CHUNK), dtype=bool))
    att = jnp.where(tri, a_causal, a_ahead)
    o = jnp.einsum('bhts,bshv->bthv', att, v) + jnp.einsum('bthk,bhkv->bthv', q * eG, S)
    G_last = G[:, -1]
    S = S * jnp.exp(G_last)[..., None] + jnp.einsum('bshk,bshv->bhkv', k * jnp.exp(G_last[:, None] - G), v)
    return S, o

def gla_chunked(q, k, v, lg):
    S0 = jnp.zeros((q.shape[0], GLA_HEADS, GLA_DK, GLA_DV), jnp.float32)
    _, o = lax.scan(gla_chunk_step, S0, (to_chunks(q), to_chunks(k), to_chunks(v), to_chunks(lg)))
    return from_chunks(o)

def ssd_chunk_step(S, inp):
    xdt, a, Bc, Cc = inp
    acum = jnp.cumsum(a, axis=1)
    seg = jnp.exp(-jnp.abs(acum[:, :, None] - acum[:, None, :]))
    cb = jnp.einsum('btgn,bsgn->btsg', Cc, Bc)
    y = jnp.einsum('btsgr,btsg,bsgrp->btgrp', seg, cb, xdt)
    y = y + jnp.einsum('btgn,bgrpn,btgr->btgrp', Cc, S, jnp.exp(acum))
    to_end = jnp.exp(acum[:, -1:] - acum)
    S = S * jnp.exp(acum[:, -1])[..., None, None] + jnp.einsum('bsgn,bsgr,bsgrp->bgrpn', Bc, to_end, xdt)
    return S, y

def ssd_chunked(xdt, a, Bm, Cm):
    S0 = jnp.zeros((xdt.shape[0], SSD_GROUPS, SSD_HPG, SSD_HEADDIM, SSD_STATE), jnp.float32)
    _, y = lax.scan(ssd_chunk_step, S0, (to_chunks(xdt), to_chunks(a), to_chunks(Bm), to_chunks(Cm)))
    return from_chunks(y)

def hybrid_mixer(hn, w_in, gla_w_gate2, gla_b_gate, gla_norm_w, conv_w, conv_b, dt_bias, a_log, d_skip,
                 ssd_norm_w, w_up_gla, w_up_ssd, w_out):
    Bsz, L, _ = hn.shape
    f32 = jnp.float32
    proj = hn @ w_in
    q, k, v, g_out, g_low, z, xbc, dt_raw, gate_a, gate_b = split_cols(proj, IN_SPLITS)

    log_g = jax.nn.log_sigmoid((g_low @ gla_w_gate2 + gla_b_gate).astype(f32)) / GLA_GATE_NORM
    hd = lambda t, n: t.reshape(Bsz, L, GLA_HEADS, n)
    o = gla_chunked(pad_front(hd(q, GLA_DK) * GLA_DK ** -0.5), pad_front(hd(k, GLA_DK)),
                    pad_front(hd(v, GLA_DV)), pad_front(hd(log_g, GLA_DK)))[:, META_PAD:]
    o = rmsnorm(o, gla_norm_w) * jax.nn.silu(hd(g_out, GLA_DV))
    y_a = o.reshape(Bsz, L, GLA_VW).astype(hn.dtype) @ w_up_gla

    xbc = jax.nn.silu(causal_dwconv(xbc, conv_w, conv_b))
    xs, Bm, Cm = split_cols(xbc, (SSD_D_INNER, SSD_BC, SSD_BC))
    dt = jax.nn.softplus(dt_raw.astype(f32) + dt_bias)
    a = dt * (-jnp.exp(a_log.astype(f32)))
    grp = lambda t: t.reshape(Bsz, L, SSD_GROUPS, SSD_HPG)
    xs_h = xs.reshape(Bsz, L, SSD_GROUPS, SSD_HPG, SSD_HEADDIM)
    y = ssd_chunked(pad_front(xs_h * grp(dt)[..., None]), pad_front(grp(a)),
                    pad_front(Bm.reshape(Bsz, L, SSD_GROUPS, SSD_STATE)),
                    pad_front(Cm.reshape(Bsz, L, SSD_GROUPS, SSD_STATE)))[:, META_PAD:]
    y = y + d_skip.reshape(SSD_GROUPS, SSD_HPG)[:, :, None] * xs_h
    y = y.reshape(Bsz, L, SSD_D_INNER) * jax.nn.silu(z)
    y = rmsnorm(y.reshape(Bsz, L, SSD_GROUPS, SSD_D_INNER // SSD_GROUPS),
                ssd_norm_w.reshape(SSD_GROUPS, -1)).reshape(Bsz, L, SSD_D_INNER)
    y_b = y.astype(hn.dtype) @ w_up_ssd

    mixed = jax.nn.sigmoid(gate_a) * y_a + jax.nn.sigmoid(gate_b) * y_b
    return (mixed @ w_out).astype(hn.dtype)

def peer_ffn(h, w_q, sub_keys, u_tab, v_tab):
    T = h.shape[0]
    pad = (-T) % PEER_BLOCK
    hp = jnp.pad(h, ((0, pad), (0, 0))).reshape(-1, PEER_BLOCK, D_MODEL)

    def block(hb):
        n = hb.shape[0]
        q = (hb @ w_q).reshape(n, PEER_HEADS, 2, PEER_HALF)
        s = jnp.einsum('nhid,hikd->nhik', q, sub_keys).astype(jnp.float32)
        s_top, i_top = lax.top_k(s, PEER_TOPK)
        cand = s_top[:, :, 0, :, None] + s_top[:, :, 1, None, :]
        cand_idx = i_top[:, :, 0, :, None] * PEER_N_KEYS + i_top[:, :, 1, None, :]
        best, pos = lax.top_k(cand.reshape(n, PEER_HEADS, PEER_TOPK * PEER_TOPK), PEER_TOPK)
        idx = jnp.take_along_axis(cand_idx.reshape(n, PEER_HEADS, -1), pos, axis=-1)
        w = jax.nn.softmax(best, axis=-1)
        u = jnp.take(u_tab, idx, axis=0)
        act = jax.nn.gelu(jnp.einsum('nhkd,nd->nhk', u, hb).astype(jnp.float32))
        out = jnp.einsum('nhk,nhkd->nd', w * act, jnp.take(v_tab, idx, axis=0))
        return out.astype(hb.dtype)

    return lax.map(block, hp).reshape(-1, D_MODEL)[:T]

def first_inputs(seed: int = 0) -> dict:
    key = jax.random.key(seed)
    ks = jax.random.split(key, 24)
    f32 = jnp.float32
    nrm = lambda k, shape, std: jax.random.normal(k, shape, f32) * std
    gain = lambda k, shape: 1.0 + 0.02 * jax.random.normal(k, shape, f32)
    Dp = DEPTH
    dt0 = jnp.exp(jax.random.uniform(ks[9], (Dp, SSD_HEADS), f32, math.log(1e-3), math.log(1e-1)))
    dt_bias = dt0 + jnp.log(-jnp.expm1(-dt0))
    a_log = jnp.log(jax.random.uniform(ks[10], (Dp, SSD_HEADS), f32, 1.0, 16.0))
    return {
        'x': nrm(ks[0], (BATCH, SEQ, D_MODEL), 1.0),
        'meta_tokens': nrm(ks[1], (N_META, D_MODEL), 1.0),
        'ln_mix_w': gain(ks[2], (Dp, D_MODEL)),
        'w_in': nrm(ks[3], (Dp, D_MODEL, IN_WIDTH), D_MODEL ** -0.5),
        'gla_w_gate2': nrm(ks[4], (Dp, GLA_GATE_RANK, GLA_QK), GLA_GATE_RANK ** -0.5),
        'gla_b_gate': nrm(ks[5], (Dp, GLA_QK), 0.1),
        'gla_norm_w': gain(ks[6], (Dp, GLA_DV)),
        'ssd_conv_w': nrm(ks[7], (Dp, SSD_CONV, SSD_XBC), SSD_CONV ** -0.5),
        'ssd_conv_b': nrm(ks[8], (Dp, SSD_XBC), 0.02),
        'ssd_dt_bias': dt_bias,
        'ssd_a_log': a_log,
        'ssd_d': gain(ks[11], (Dp, SSD_HEADS)),
        'ssd_norm_w': gain(ks[12], (Dp, SSD_D_INNER)),
        'w_up_gla': nrm(ks[13], (Dp, GLA_VW, D_MODEL), GLA_VW ** -0.5),
        'w_up_ssd': nrm(ks[14], (Dp, SSD_D_INNER, D_MODEL), SSD_D_INNER ** -0.5),
        'w_out': nrm(ks[15], (Dp, D_MODEL, D_MODEL), D_MODEL ** -0.5),
        'ln_ffn_w': gain(ks[16], (Dp, D_MODEL)),
        'peer_w_q': nrm(ks[17], (Dp, D_MODEL, PEER_HEADS * PEER_KEY_DIM), D_MODEL ** -0.5),
        'peer_sub_keys': nrm(ks[18], (Dp, PEER_HEADS, 2, PEER_N_KEYS, PEER_HALF), PEER_HALF ** -0.5),
        'peer_u': nrm(ks[19], (Dp, PEER_N_EXPERTS, D_MODEL), D_MODEL ** -0.5),
        'peer_v': nrm(ks[20], (Dp, PEER_N_EXPERTS, D_MODEL), PEER_HEADS ** -0.5),
        'ln_final_w': gain(ks[21], (D_MODEL,)),
    }

def first_block(x, meta_tokens, ln_mix_w, w_in, gla_w_gate2, gla_b_gate, gla_norm_w, ssd_conv_w, ssd_conv_b,
              ssd_dt_bias, ssd_a_log, ssd_d, ssd_norm_w, w_up_gla, w_up_ssd, w_out, ln_ffn_w,
              peer_w_q, peer_sub_keys, peer_u, peer_v, ln_final_w):
    Bsz = x.shape[0]
    meta = jnp.broadcast_to(meta_tokens[None].astype(x.dtype), (Bsz, N_META, D_MODEL))
    h = jnp.concatenate([meta, x], axis=1)
    for l in range(DEPTH):
        hn = rmsnorm(h, ln_mix_w[l])
        h = h + hybrid_mixer(hn, w_in[l], gla_w_gate2[l], gla_b_gate[l], gla_norm_w[l], ssd_conv_w[l],
                             ssd_conv_b[l], ssd_dt_bias[l], ssd_a_log[l], ssd_d[l], ssd_norm_w[l],
                             w_up_gla[l], w_up_ssd[l], w_out[l])
        if l == DEPTH - 1:
            h = h[:, N_META:]
        hn = rmsnorm(h, ln_ffn_w[l])
        ffn = peer_ffn(hn.reshape(-1, D_MODEL), peer_w_q[l], peer_sub_keys[l], peer_u[l], peer_v[l])
        h = h + ffn.reshape(h.shape)
    return rmsnorm(h, ln_final_w)


MIX_W = D_MODEL
HEAD_DIM = 64
ATTN_W = MIX_W // 2
N_ATTN_HEADS = ATTN_W // HEAD_DIM
N_KV_HEADS = 2
KV_W = N_KV_HEADS * HEAD_DIM
WINDOW = 128
BLOCK = 128
RET_W = MIX_W - ATTN_W
N_RET_HEADS = 4
RET_HEAD_DIM = RET_W // N_RET_HEADS
RET_CHUNK = 128
IN_W = ATTN_W + 2 * KV_W + 4 * RET_W
D_FF = 2816
CONV_WIDTH = 3
GN_EPS = 1e-6
MASK_VALUE = -1e30


def rms_norm(x, w):
    xf = x.astype(jnp.float32)
    y = xf * lax.rsqrt(jnp.mean(xf * xf, axis=-1, keepdims=True) + RMS_EPS)
    return (y * w.astype(jnp.float32)).astype(x.dtype)

def sliding_window_sink_attention(q, k, v, sinks):
    b, s, _ = q.shape
    nb = s // BLOCK
    g = N_ATTN_HEADS // N_KV_HEADS
    qb = q.reshape(b, nb, BLOCK, N_KV_HEADS, g, HEAD_DIM)
    kb = k.reshape(b, nb, BLOCK, N_KV_HEADS, HEAD_DIM)
    vb = v.reshape(b, nb, BLOCK, N_KV_HEADS, HEAD_DIM)
    pad = ((0, 0), (1, 0), (0, 0), (0, 0), (0, 0))
    kk = jnp.concatenate([jnp.pad(kb, pad)[:, :-1], kb], axis=2)
    vv = jnp.concatenate([jnp.pad(vb, pad)[:, :-1], vb], axis=2)
    scores = jnp.einsum('bnqhgd,bnkhd->bnhgqk', qb, kk).astype(jnp.float32) * (HEAD_DIM ** -0.5)
    qpos = jnp.arange(BLOCK)[:, None] + BLOCK
    kpos = jnp.arange(2 * BLOCK)[None, :]
    rel = qpos - kpos
    band = (rel >= 0) & (rel < WINDOW)
    not_pad = (jnp.arange(nb)[:, None, None] > 0) | (kpos >= BLOCK)[None]
    valid = band[None] & not_pad
    scores = jnp.where(valid[None, :, None, None], scores, MASK_VALUE)
    sink = jnp.broadcast_to(
        sinks.astype(jnp.float32).reshape(N_KV_HEADS, g)[None, None, :, :, None, None],
        scores.shape[:-1] + (1,))
    probs = jax.nn.softmax(jnp.concatenate([scores, sink], axis=-1), axis=-1)[..., :-1]
    out = jnp.einsum('bnhgqk,bnkhd->bnqhgd', probs.astype(vv.dtype), vv)
    return out.reshape(b, s, ATTN_W)

def rotate_every_two(x):
    x1 = x[..., ::2]
    x2 = x[..., 1::2]
    return jnp.stack([-x2, x1], axis=-1).reshape(x.shape)

def retention_chunkwise(q, k, v):
    b, s, h, dk = q.shape
    dv = v.shape[-1]
    nc = s // RET_CHUNK
    c = RET_CHUNK
    log_gamma = jnp.log(1.0 - jnp.power(2.0, -5.0 - jnp.arange(h, dtype=jnp.float32)))
    idx = jnp.arange(c, dtype=jnp.float32)
    rel = idx[:, None] - idx[None, :]
    d_intra = jnp.where(rel[None] >= 0,
                        jnp.exp(log_gamma[:, None, None] * jnp.maximum(rel, 0.0)[None]), 0.0)
    xi = jnp.exp(log_gamma[None, :] * (idx[:, None] + 1.0))
    zeta = jnp.exp(log_gamma[None, :] * (c - 1.0 - idx[:, None]))
    chunk_decay = jnp.exp(log_gamma * c)
    qc = q.reshape(b, nc, c, h, dk)
    kc = k.reshape(b, nc, c, h, dk)
    vc = v.reshape(b, nc, c, h, dv)
    inner = jnp.einsum('bnqhd,bnkhd->bnhqk', qc, kc) * d_intra[None, None]
    o_inner = jnp.einsum('bnhqk,bnkhe->bnqhe', inner, vc)
    kv_chunk = jnp.einsum('bnkhd,kh,bnkhe->bnhde', kc, zeta, vc)

    def step(state, kv):
        return chunk_decay[None, :, None, None] * state + kv, state

    _, prev = lax.scan(step, jnp.zeros((b, h, dk, dv), jnp.float32), jnp.moveaxis(kv_chunk, 1, 0))
    prev = jnp.moveaxis(prev, 0, 1)
    o_cross = jnp.einsum('bnqhd,bnhde->bnqhe', qc, prev) * xi[None, None, :, :, None]
    return (o_inner + o_cross).reshape(b, s, h, dv)

def retention_group(q, k, v, gate):
    b, s, _ = q.shape
    dtype = q.dtype
    pos = jnp.arange(s, dtype=jnp.float32)
    angle = 1.0 / jnp.power(10000.0, jnp.linspace(0.0, 1.0, RET_HEAD_DIM // 2, dtype=jnp.float32))
    angle = jnp.repeat(angle, 2)
    sin = jnp.sin(pos[:, None] * angle[None])[None, :, None, :]
    cos = jnp.cos(pos[:, None] * angle[None])[None, :, None, :]
    qf = q.astype(jnp.float32).reshape(b, s, N_RET_HEADS, RET_HEAD_DIM)
    kf = k.astype(jnp.float32).reshape(b, s, N_RET_HEADS, RET_HEAD_DIM) * (RET_HEAD_DIM ** -0.5)
    vf = v.astype(jnp.float32).reshape(b, s, N_RET_HEADS, RET_HEAD_DIM)
    qf = qf * cos + rotate_every_two(qf) * sin
    kf = kf * cos + rotate_every_two(kf) * sin
    o = retention_chunkwise(qf, kf, vf)
    mu = jnp.mean(o, axis=-1, keepdims=True)
    var = jnp.mean(jnp.square(o - mu), axis=-1, keepdims=True)
    o = ((o - mu) * lax.rsqrt(var + GN_EPS)).reshape(b, s, RET_W)
    return (jax.nn.silu(gate.astype(jnp.float32)) * o).astype(dtype)

def causal_depthwise_conv(u, w, bias):
    ch = u.shape[-1]
    y = lax.conv_general_dilated(u, w[:, None, :].astype(u.dtype), window_strides=(1,),
                                 padding=[(CONV_WIDTH - 1, 0)],
                                 dimension_numbers=('NWC', 'WIO', 'NWC'),
                                 feature_group_count=ch)
    return y + bias.astype(u.dtype)

def second_inputs(seed: int = 0) -> dict:
    key = jax.random.key(seed)
    ks = jax.random.split(key, 13)
    f32 = jnp.float32

    def gain(k):
        return 1.0 + 0.02 * jax.random.normal(k, (DEPTH, D_MODEL), f32)

    return {
        "x": jax.random.normal(ks[0], (BATCH, SEQ, D_MODEL), f32),
        "mix_pre_norm": gain(ks[1]),
        "w_in": jax.random.normal(ks[2], (DEPTH, D_MODEL, IN_W), f32) * D_MODEL ** -0.5,
        "attn_sinks": jax.random.normal(ks[3], (DEPTH, N_ATTN_HEADS), f32),
        "w_out": jax.random.normal(ks[4], (DEPTH, MIX_W, D_MODEL), f32) * MIX_W ** -0.5,
        "mix_post_norm": gain(ks[5]),
        "ffn_pre_norm": gain(ks[6]),
        "w_up": jax.random.normal(ks[7], (DEPTH, D_MODEL, 2 * D_FF), f32) * D_MODEL ** -0.5,
        "conv_w": jax.random.normal(ks[8], (DEPTH, CONV_WIDTH, 2 * D_FF), f32) * CONV_WIDTH ** -0.5,
        "conv_b": 0.01 * jax.random.normal(ks[9], (DEPTH, 2 * D_FF), f32),
        "w_down": jax.random.normal(ks[10], (DEPTH, D_FF, D_MODEL), f32) * D_FF ** -0.5,
        "ffn_post_norm": gain(ks[11]),
    }

def second_block(x, mix_pre_norm, w_in, attn_sinks, w_out, mix_post_norm,
              ffn_pre_norm, w_up, conv_w, conv_b, w_down, ffn_post_norm):
    splits = np.cumsum([ATTN_W, KV_W, KV_W, RET_W, RET_W, RET_W]).tolist()
    for l in range(DEPTH):
        h = rms_norm(x, mix_pre_norm[l])
        proj = jnp.einsum('bsd,de->bse', h, w_in[l])
        q_a, k_a, v_a, q_r, k_r, v_r, g_r = jnp.split(proj, splits, axis=-1)
        attn_out = sliding_window_sink_attention(q_a, k_a, v_a, attn_sinks[l])
        ret_out = retention_group(q_r, k_r, v_r, g_r)
        mixed = jnp.einsum('bse,ed->bsd', jnp.concatenate([attn_out, ret_out], axis=-1), w_out[l])
        x = x + rms_norm(mixed, mix_post_norm[l])
        h = rms_norm(x, ffn_pre_norm[l])
        u = causal_depthwise_conv(jnp.einsum('bsd,df->bsf', h, w_up[l]), conv_w[l], conv_b[l])
        u_gate, u_val = jnp.split(u, 2, axis=-1)
        y = jax.nn.gelu(u_gate, approximate=True) * u_val
        y = jnp.einsum('bsf,fd->bsd', y, w_down[l])
        x = x + rms_norm(y, ffn_post_norm[l])
    return x


def setup_inputs(seed=0):
    out = dict(first_inputs(seed))
    for name, value in second_inputs(seed + 1).items():
        if name != "x":
            out[name + "_2"] = value
    return out


def reference(
    x, meta_tokens, ln_mix_w, w_in, gla_w_gate2, gla_b_gate, gla_norm_w, ssd_conv_w, ssd_conv_b,
    ssd_dt_bias, ssd_a_log, ssd_d, ssd_norm_w, w_up_gla, w_up_ssd, w_out, ln_ffn_w, peer_w_q,
    peer_sub_keys, peer_u, peer_v, ln_final_w, mix_pre_norm_2, w_in_2, attn_sinks_2, w_out_2,
    mix_post_norm_2, ffn_pre_norm_2, w_up_2, conv_w_2, conv_b_2, w_down_2, ffn_post_norm_2,
):
    x = first_block(
        x, meta_tokens, ln_mix_w, w_in, gla_w_gate2, gla_b_gate, gla_norm_w, ssd_conv_w,
        ssd_conv_b, ssd_dt_bias, ssd_a_log, ssd_d, ssd_norm_w, w_up_gla, w_up_ssd, w_out,
        ln_ffn_w, peer_w_q, peer_sub_keys, peer_u, peer_v, ln_final_w,
    )
    return second_block(
        x, mix_pre_norm_2, w_in_2, attn_sinks_2, w_out_2, mix_post_norm_2, ffn_pre_norm_2,
        w_up_2, conv_w_2, conv_b_2, w_down_2, ffn_post_norm_2,
    )


_drawn_inputs = setup_inputs


def setup_inputs(seed=0):
    import zlib

    import numpy as np

    out = dict(_drawn_inputs(seed))
    spreads = {}
    factors = {'attn_sinks_2': 5.375,
     'mix_post_norm_2': 3.501,
     'ffn_pre_norm_2': 3.547,
     'conv_b_2': 6.953,
     'ffn_post_norm_2': 4.627}
    for name, (base, spread) in spreads.items():
        noise = np.random.default_rng([zlib.crc32(name.encode()), seed]).standard_normal(out[name].shape)
        drawn = base * np.exp(spread * noise) if base else spread * noise
        out[name] = __import__('jax').numpy.asarray(drawn.astype(out[name].dtype))
    for name, factor in factors.items():
        out[name] = (out[name] * factor).astype(out[name].dtype)
    return out
```

```python
from contextlib import ExitStack

import numpy as np
import concourse.bass as bass
from concourse import mybir

F32 = mybir.dt.float32
F32R = mybir.dt.float32r
U32 = mybir.dt.uint32
ALU = mybir.AluOpType
ACT = mybir.ActivationFunctionType
AX = mybir.AxisListType.X

P = 128
D = 1024
KD = D // P
SEQ = 512
META = 16
L = META + SEQ
NB = SEQ // P
CH = 64
EPS = 1e-6
RING = 4

GLA_HEADS, GLA_DK, GLA_DV, GATE_RANK = 4, 128, 256, 16
SSD_GROUPS, SSD_HPG, SSD_HD = 4, 8, 64
SSD_HEADS = SSD_GROUPS * SSD_HPG
PEER_HEADS, KEYS, TOPK = 8, 128, 16
GROUP = 8
A_HEADS, A_HD, KV_HEADS = 8, 64, 2
R_HEADS = 4
D_FF = 2816
FT = D_FF // P

CONST_W = {"ident": 128, "ones": 128, "tri": 128, "tri16": 128, "same": 128, "half0": 128, "half1": 128, "diag64": 64, "iota": 128, "iota16": 16,
           "causal": 256}
CONST2_W = {"decay": R_HEADS, "band": 256, "rot": 128, "dintra": 512, "xi": 512, "zeta": 512, "cos": 512, "sin": 512}


def places(widths):
    at, out = 0, {}
    for n, w in widths.items():
        out[n] = (at, at + w)
        at += w
    return out


CONST_AT, CONST2_AT = places(CONST_W), places(CONST2_W)
CONST_N, CONST2_N = sum(CONST_W.values()), sum(CONST2_W.values())


def constants():
    c = {}
    i = np.arange(P)
    chunk = i // CH
    same = (chunk[:, None] == chunk[None, :]).astype(np.float32)
    c["ident"] = np.eye(P)
    c["ones"] = np.ones((P, P))
    c["half0"] = np.broadcast_to(chunk[:, None] == 0, (P, P))
    c["half1"] = np.broadcast_to(chunk[:, None] == 1, (P, P))
    c["tri"] = same * (i[:, None] <= i[None, :])
    c["tri16"] = c["tri"] / 16.0
    c["same"] = same
    c["diag64"] = (i[:, None] % CH == np.arange(CH)[None, :])
    c["iota"] = np.broadcast_to(i[None, :], (P, P))
    c["iota16"] = np.broadcast_to(np.arange(16)[None, :], (P, 16))
    c["causal"] = np.tile(i[:, None] % CH <= np.arange(CH)[None, :], (1, NB))
    rel = (i[:, None] + P) - np.arange(2 * P)[None, :]
    c["band"] = np.where((rel >= 0) & (rel < P), 0.0, -1e30)
    rot = np.zeros((P, P))
    rot[i[1::2], i[0::2]] = -1.0
    rot[i[0::2], i[1::2]] = 1.0
    c["rot"] = rot
    f = np.float32
    log_gamma = np.log(f(1.0) - np.power(f(2.0), f(-5.0) - np.arange(R_HEADS, dtype=f)))
    r = (i[None, :] - i[:, None]).astype(f)
    c["dintra"] = np.stack([np.where(r >= 0, np.exp(g * np.maximum(r, 0)), 0) for g in log_gamma], 1).reshape(P, -1)
    c["xi"] = np.stack([np.broadcast_to(np.exp(g * (i + f(1))), (P, P)) for g in log_gamma], 1).reshape(P, -1)
    c["zeta"] = np.stack([np.broadcast_to(np.exp(g * (P - f(1) - i)), (P, P)) for g in log_gamma], 1).reshape(P, -1)
    c["decay"] = np.broadcast_to(np.exp(log_gamma * f(P)), (P, R_HEADS))
    angle = np.repeat(f(1.0) / np.power(f(10000.0), np.linspace(0, 1, P // 2, dtype=f)), 2)
    arg = (np.arange(SEQ, dtype=f)[None, :] * angle[:, None]).astype(f)
    c["cos"], c["sin"] = np.cos(arg), np.sin(arg)
    return [np.ascontiguousarray(np.concatenate([np.asarray(c[n], np.float32).reshape(P, ws[n]) for n in ws], 1))
            for ws in (CONST_W, CONST2_W)]


class Core:

    def __init__(self, nc, ctx):
        self.nc, self.ctx = nc, ctx
        self.banks = ctx.enter_context(nc.psum_tensor("banks", [P, 8, 512], F32))
        self.consts = ctx.enter_context(nc.sbuf_tensor("consts", [P, CONST_N], F32))
        self.consts2 = None
        self.in_use = []

    def sems(self, phase, names):
        self.in_use += [self.nc.alloc_semaphore(name=f"{phase}_{n}") for n in names.split()]
        return self.in_use[-len(names.split()):]

    def reset_sems(self):
        with self.nc.Block() as block:
            @block.sync
            def _(sp):
                for s in self.in_use:
                    sp.sem_clear(s)
        for s in self.in_use:
            self.nc.release_semaphore(s)
        self.in_use = []

    def const(self, name):
        if name in CONST2_AT:
            a, b = CONST2_AT[name]
            return self.consts2[:, a:b]
        a, b = CONST_AT[name]
        return self.consts[:, a:b]


def load_phase(k, name, pairs):
    (loaded,) = k.sems(name, "loaded")
    with k.nc.Block() as block:
        @block.sync
        def _(sp):
            for to, source in pairs:
                sp.dma_start(to, source).then_inc(loaded, 16)
            sp.wait_ge(loaded, 16 * len(pairs))


def store_phase(k, name, to, source):
    (stored,) = k.sems(name, "stored")
    with k.nc.Block() as block:
        @block.sync
        def _(sp):
            sp.dma_start(to, source).then_inc(stored, 16)
            sp.wait_ge(stored, 16)


def norm_phase(k, name, src, dst, weight, groups, tiles, n, add=None, mean_of=None):
    nc = k.nc
    halves = 1 if n <= 512 else 2
    w = n // halves
    squared, square_used, summed, root, recip, scaled = k.sems(name, "squared square_used summed root recip scaled")
    with ExitStack() as ctx:
        sq = ctx.enter_context(nc.sbuf_tensor(f"{name}_sq", [P, 2, n], F32))
        std = ctx.enter_context(nc.sbuf_tensor(f"{name}_std", [P, 2, n], F32))
        rstd = ctx.enter_context(nc.sbuf_tensor(f"{name}_rstd", [P, 2, n], F32))
        eps = ctx.enter_context(nc.sbuf_tensor(f"{name}_eps", [P, 1], F32))
        ones = k.const("ones")
        inv = 1.0 / (tiles * P)
        with nc.Block() as block:
            @block.scalar
            def _(act):
                act.wait_ge(scaled, 1)
                for g in range(groups):
                    for t in range(tiles):
                        m = g * tiles + t
                        if m >= 2:
                            act.wait_ge(square_used, m - 1)
                        nc.scalar.activation(sq[:, m % 2, :], src[:, m, :], ACT.Square).then_inc(squared, 1)
                    act.wait_ge(square_used, (g + 1) * tiles)
                    if g >= 2:
                        act.wait_ge(recip, g - 1)
                    nc.scalar.activation(std[:, g % 2, :].rearrange("p (h n) -> p h n", h=halves),
                                         k.banks[:, 2 * (g % 2):2 * (g % 2) + halves, 0:w],
                                         ACT.Sqrt, bias=eps[:, 0:1], scale=inv).then_inc(root, 1)

            @block.tensor
            def _(pe):
                for g in range(groups):
                    for t in range(tiles):
                        m = g * tiles + t
                        pe.wait_ge(squared, m + 1)
                        if t == 0 and g >= 2:
                            pe.wait_ge(root, g - 1)
                        for h in range(halves):
                            last = nc.tensor.matmul(k.banks[:, 2 * (g % 2) + h, 0:w], ones,
                                                    sq[:, m % 2, h * w:(h + 1) * w],
                                                    start=(t == 0), stop=(t == tiles - 1))
                        last.then_inc(square_used, 1)

            @block.vector
            def _(dve):
                nc.vector.memset(eps[:], EPS).then_inc(scaled, 1)
                done = 1
                for g in range(groups):
                    dve.wait_ge(root, g + 1)
                    if g >= 2:
                        dve.wait_ge(scaled, done)
                    nc.vector.reciprocal(rstd[:, g % 2, :], std[:, g % 2, :]).then_inc(recip, 1)
                    dve.wait_ge(recip, g + 1)
                    for t in range(tiles):
                        m = g * tiles + t
                        if weight is None:
                            nc.vector.tensor_tensor(dst[:, m, :], src[:, m, :], rstd[:, g % 2, :],
                                                    ALU.mult).then_inc(scaled, 1)
                        else:
                            nc.vector.scalar_tensor_tensor(dst[:, m, :], src[:, m, :], weight[:, m:m + 1],
                                                           rstd[:, g % 2, :], ALU.mult, ALU.mult).then_inc(scaled, 1)
                        done += 1
                if add is not None:
                    for m in range(groups * tiles):
                        dve.wait_ge(scaled, 2 + m)
                        nc.vector.tensor_tensor(dst[:, m, :], dst[:, m, :], add[:, m, :], ALU.add).then_inc(summed, 1)


def product3(nc, to, w, x, start, stop):
    nc.tensor.matmul(to, w[0], x[0], start=start, stop=False)
    nc.tensor.matmul(to, w[0], x[1], start=False, stop=False)
    return nc.tensor.matmul(to, w[1], x[0], start=False, stop=stop)


def split_phase(k, name, src, pair, tiles):
    nc = k.nc
    high_done, low_done = k.sems(name, "high_done low_done")
    high, low = pair
    with nc.Block() as block:
        @block.scalar
        def _(act):
            for t in range(tiles):
                nc.scalar.activation(high[:, t, :], src[:, t, :], ACT.Copy).then_inc(high_done, 1)

        @block.vector
        def _(dve):
            for t in range(tiles):
                dve.wait_ge(high_done, t + 1)
                nc.vector.tensor_tensor(low[:, t, :], src[:, t, :], high[:, t, :].bitcast(F32), ALU.subtract).then_inc(low_done, 1)


def product_phase(k, name, w_dram, x, kt, mt, n, finish, dst=None, other=None, at=0):
    nc = k.nc
    halves = 1 if n <= 512 else 2
    w = n // halves
    U = RING
    assert mt % U == 0
    raws = RING if kt <= KD else 2
    per = 4 if halves == 1 else 2
    product, psum_read, gate_out, written, high_done, low_done = k.sems(
        name, "product psum_read gate_out written high_done low_done")
    w_in = k.sems(name, " ".join(f"w_in{r}" for r in range(raws)))
    gated = finish in ("times_silu", "times_gate", "gate_add")
    func = {"silu": ACT.Silu, "times_silu": ACT.Silu, "times_gate": ACT.Sigmoid, "gate_add": ACT.Sigmoid}.get(finish, ACT.Copy)
    with ExitStack() as ctx:
        def sb(nm, shape, dt=F32):
            return ctx.enter_context(nc.sbuf_tensor(f"{name}_{nm}", shape, dt))
        raw = sb("raw", [P, raws, kt * P])
        high, low = sb("high", [P, 2, kt * P], F32R), sb("low", [P, 2, kt * P], F32R)
        temp = sb("t", [P, 2, n]) if gated else None
        temp2 = sb("t2", [P, n]) if finish == "gate_add" else None

        def psum(r):
            return k.banks[:, halves * (r % per):halves * (r % per) + halves, 0:w]

        def tile(a, m):
            return a[:, bass.ds(m, 1), :].rearrange("p a (h n) -> p (a h) n", h=halves)

        def flat(a, m):
            return a[:, bass.ds(m, 1), :].rearrange("p a n -> p (a n)")

        with nc.Block() as block:
            @block.sync
            def _(sp):
                with sp.Fori(0, mt // U) as g:
                    for r in range(U):
                        sp.wait_ge(low_done, g * U + (r + 1))
                        sp.dma_start(raw[:, r % raws, :],
                                     w_dram[bass.ds(g * U + r, 1), :, at:at + kt * P].rearrange("a p n -> (a p) n")
                                     ).then_inc(w_in[r % raws], 16)

            @block.tensor
            def _(pe):
                pe.sem_inc(product, 2)
                with pe.Fori(0, mt // U) as g:
                    for r in range(U):
                        pe.wait_ge(low_done, g * U + (r + 1 + raws))
                        pe.wait_ge(psum_read, g * U + (r + 1))
                        for c in range(kt):
                            cols = slice(c * P, (c + 1) * P)
                            for h in range(halves):
                                last = product3(nc, psum(r)[:, h, :], (high[:, r % 2, cols], low[:, r % 2, cols]),
                                                [a[:, c, h * w:(h + 1) * w] for a in x], c == 0, c == kt - 1)
                        last.then_inc(product, 1)

            def split(dve, g, r):
                dve.wait_ge(w_in[r % raws], g * (16 * U // raws) + (16 * (r // raws) + 16))
                dve.wait_ge(product, g * U + (r + 1))
                nc.vector.tensor_copy(high[:, r % 2, :], raw[:, r % raws, :]).then_inc(high_done, 1)
                dve.wait_ge(high_done, g * U + (r + 1))
                nc.vector.tensor_tensor(low[:, r % 2, :], raw[:, r % raws, :], high[:, r % 2, :].bitcast(F32), ALU.subtract
                                        ).then_inc(low_done, 1)

            def finish_tile(dve, g, r):
                m = g * U + r
                if finish == "add":
                    dve.wait_ge(product, m + 3)
                    nc.vector.tensor_tensor(tile(dst, m), tile(dst, m), psum(r), ALU.add).then_inc(psum_read, 1)
                elif gated:
                    dve.wait_ge(psum_read, m + (1 + per))
                    if finish == "gate_add":
                        nc.vector.tensor_tensor(temp2[:], temp[:, r % 2, :], flat(other, m), ALU.mult).then_inc(gate_out, 1)
                        dve.wait_ge(gate_out, m + 3)
                        nc.vector.tensor_tensor(flat(dst, m), flat(dst, m), temp2[:], ALU.add).then_inc(written, 1)
                        dve.wait_ge(written, m + 1)
                    else:
                        nc.vector.tensor_tensor(flat(dst, m), flat(dst, m), temp[:, r % 2, :], ALU.mult).then_inc(gate_out, 1)

            @block.vector
            def _(dve):
                dve.sem_inc(low_done, raws)
                if gated:
                    dve.sem_inc(gate_out, 2)
                if finish == "add":
                    dve.sem_inc(psum_read, per)

                def turn(g, first):
                    for r in range(U):
                        split(dve, g, r)
                        if r:
                            finish_tile(dve, g, r - 1)
                        elif not first:
                            finish_tile(dve, g - 1, U - 1)
                turn(0, True)
                if mt > U:
                    with dve.Fori(1, mt // U) as g:
                        turn(g, False)
                finish_tile(dve, mt // U - 1, U - 1)

            @block.scalar
            def _(act):
                if finish == "add":
                    return
                act.sem_inc(psum_read, per)
                with act.Fori(0, mt // U) as g:
                    for r in range(U):
                        act.wait_ge(product, g * U + (r + 3))
                        if gated:
                            act.wait_ge(gate_out, g * U + (r + 1))
                            nc.scalar.activation(temp[:, r % 2, :].rearrange("p (h n) -> p h n", h=halves), psum(r), func
                                                 ).then_inc(psum_read, 1)
                        else:
                            nc.scalar.activation(tile(dst, g * U + r), psum(r), func).then_inc(psum_read, 1)


def chunk_cols(c):
    return slice(0, META) if c == 0 else slice(META + (c - 1) * CH, META + c * CH)


def block_cols(b):
    return slice(META + b * P, META + (b + 1) * P)


def small_products_phase(k, name, hn, w_low, low, w_dt, dt_raw):
    nc = k.nc
    done, evicted = k.sems(name, "done evicted")
    with nc.Block() as block:
        @block.tensor
        def _(pe):
            for h in range(2):
                for c in range(KD):
                    last = nc.tensor.matmul(k.banks[0:GATE_RANK, h, 0:264], w_low[:, c, :], hn[:, c, h * 264:h * 264 + 264],
                                            start=(c == 0), stop=(c == KD - 1))
            last.then_inc(done, 1)
            for b in range(NB):
                for c in range(KD):
                    nc.tensor.matmul(k.banks[:, 2, b * 32:b * 32 + 32], hn[:, c, block_cols(b)], w_dt[:, c, :],
                                     start=(c == 0), stop=(c == KD - 1))
            for c in range(KD):
                last = nc.tensor.matmul(k.banks[0:META, 3, 0:32], hn[:, c, 0:META], w_dt[:, c, :],
                                        start=(c == 0), stop=(c == KD - 1))
            last.then_inc(done, 1)

        @block.vector
        def _(dve):
            nc.vector.memset(low[:], 1.0).then_inc(evicted, 1)
            nc.vector.memset(dt_raw[:, NB, :], 0.0).then_inc(evicted, 1)
            dve.wait_ge(evicted, 2)
            dve.wait_ge(done, 1)
            nc.vector.tensor_copy(low[0:GATE_RANK, :].rearrange("p (h n) -> p h n", h=2), k.banks[0:GATE_RANK, 0:2, 0:264]
                                  ).then_inc(evicted, 1)
            dve.wait_ge(done, 2)
            nc.vector.tensor_copy(dt_raw[:, 0:NB, :].rearrange("p b n -> p (b n)"), k.banks[:, 2, 0:NB * 32]).then_inc(evicted, 1)
            nc.vector.tensor_copy(dt_raw[0:META, NB, :], k.banks[0:META, 3, 0:32]).then_inc(evicted, 1)


def gla_phase(k, name, hn, low, gate_w, wq, wk, wv, o):
    nc = k.nc
    SC = GLA_DK ** -0.5
    (q_in, k_in, v_in, q_done, k_done, v_done, gate_done, gate_abs, gate_exp, gate_ln, lg_done, g_done, g_last, e_done, to_last,
     prod, kdt_done, att_done, kdt_ready, v_ready, kv_done, state, att_copy, att_ready, o_done, o_out, head_gate, cleared,
     high_done, low_done) = k.sems(
        name, "q_in k_in v_in q_done k_done v_done gate_done gate_abs gate_exp gate_ln lg_done g_done g_last e_done to_last prod "
              "kdt_done att_done kdt_ready v_ready kv_done state att_copy att_ready o_done o_out head_gate cleared high_done low_done")
    with ExitStack() as ctx:
        def sb(n, shape):
            return ctx.enter_context(nc.sbuf_tensor(f"{name}_{n}", shape, F32))
        raw = sb("raw", [P, 4, KD * P])
        high, low_w = (ctx.enter_context(nc.sbuf_tensor(f"{name}_{n}", [P, 4, KD * P], F32R)) for n in ("high", "low"))
        gate_h = sb("gate_h", [GATE_RANK + 1, P])
        v, vm = sb("v", [P, NB, GLA_DV]), sb("vm", [META, GLA_DV])
        ab, abm, lg, lgm = sb("ab", [P, SEQ]), sb("abm", [META, P]), sb("lg", [P, SEQ]), sb("lgm", [META, P])
        glast = sb("glast", [P, 9])
        e_pos, e_neg, e_last = sb("e_pos", [P, L]), sb("e_neg", [P, L]), sb("e_last", [P, L])
        qe, qn, ke, kn, kd = (sb(n, [P, L]) for n in ("qe", "qn", "ke", "kn", "kd"))
        kdt, kdtm = sb("kdt", [P, NB, P]), sb("kdtm", [META, P])
        att, attm = sb("att", [P, NB, P]), sb("attm", [META, META])
        S = sb("S", [P, 8, GLA_DV])
        B = k.banks
        ident, tri = k.const("ident"), k.const("tri16")
        causal = k.const("causal").bitcast(U32)
        two = "p (h n) -> p h n"

        halves = (slice(0, CH), slice(CH, P))

        def state_bank(c):
            if c == 0:
                return B[:, 1, 0:256]
            bank, at = 4 + 2 * ((c - 1) % 2) + (c - 1) // 4, ((c - 1) // 2 % 2) * 256
            return B[:, bank, at:at + 256]

        with nc.Block() as block:
            @block.sync
            def _(sp):
                with sp.Fori(0, GLA_HEADS) as h:
                    sp.wait_ge(v_done, h + 1)
                    for to, source, arrived in ((raw[:, 0, :], wq, q_in), (raw[:, 1, :], wk, k_in),
                                                (raw[:, 2:4, :].rearrange("p c n -> p (c n)"), wv, v_in)):
                        sp.dma_start(to, source[bass.ds(h, 1)].rearrange("a p n -> (a p) n")).then_inc(arrived, 16)

            @block.gpsimd
            def _(pool):
                with pool.Fori(0, GLA_HEADS) as h:
                    pool.wait_ge(gate_done, h + 1)
                    nc.gpsimd.tensor_copy(gate_h[:], gate_w[:, bass.ds(h * P, P)]).then_inc(head_gate, 1)

            @block.tensor
            def _(pe):
                pe.sem_inc(v_done, 1)
                pe.sem_inc(gate_done, 1)
                with pe.Fori(0, GLA_HEADS) as h:
                    pe.wait_ge(o_out, h * 3 + 3)
                    for i, sem in enumerate((q_done, k_done)):
                        pe.wait_ge(low_done, h * 4 + i + 1)
                        for c in range(KD):
                            for j in range(2):
                                last = product3(nc, B[:, 2 * i + j, 0:264], [a[:, i, c * P:(c + 1) * P] for a in (high, low_w)],
                                                [a[:, c, j * 264:j * 264 + 264] for a in hn], c == 0, c == KD - 1)
                        last.then_inc(sem, 1)
                    pe.wait_ge(low_done, h * 4 + 4)
                    wv_pair = [a[:, 2:4, :].rearrange("p a (c n) -> p (a c) n", n=GLA_DV) for a in (high, low_w)]
                    for b in range(NB + 1):
                        cols = block_cols(b) if b < NB else slice(0, P)
                        to = B[:, 4 + b // 2, (b % 2) * 256:(b % 2) * 256 + 256] if b < NB else B[:, 7, 0:256]
                        for c in range(KD):
                            last = product3(nc, to, [a[:, c, cols] for a in hn], [a[:, c, :] for a in wv_pair],
                                            c == 0, c == KD - 1)
                    last.then_inc(v_done, 1)
                    pe.wait_ge(head_gate, h + 1)
                    pe.wait_ge(v_ready, h * 2 + 2)
                    for b in range(NB):
                        nc.tensor.matmul(B[:, 6, b * P:(b + 1) * P], low[:, block_cols(b)], gate_h[:], start=True, stop=True)
                    nc.tensor.matmul(B[0:META, 7, 256:384], low[:, 0:META], gate_h[:], start=True, stop=True
                                     ).then_inc(gate_done, 1)
                    pe.wait_ge(lg_done, h * 2 + 2)
                    for b in range(NB):
                        nc.tensor.matmul(B[:, 6, b * P:(b + 1) * P], lg[:, b * P:(b + 1) * P], tri, start=True, stop=True)
                    nc.tensor.matmul(B[:, 7, 384:400], lgm[:], tri[0:META, 0:META], start=True, stop=True
                                     ).then_inc(g_done, 1)
                    pe.wait_ge(prod, h * 5 + 5)
                    for b in range(NB):
                        nc.tensor.transpose(B[:, 0, b * P:(b + 1) * P], kd[:, block_cols(b)], ident)
                    nc.tensor.transpose(B[0:META, 1, 0:P], kd[:, 0:META], ident).then_inc(kdt_done, 1)
                    for c in range(1, 9):
                        b, half = (c - 1) // 2, (c - 1) % 2
                        for at, kk, qq in ((0, kn, qe), (256, ke, qn)):
                            nc.tensor.matmul(B[half * CH:half * CH + CH, 2, at + b * CH:at + b * CH + CH],
                                             kk[:, chunk_cols(c)], qq[:, chunk_cols(c)], start=True, stop=True)
                    nc.tensor.matmul(B[0:META, 3, 0:META], kn[:, 0:META], qe[:, 0:META], start=True, stop=True)
                    nc.tensor.matmul(B[0:META, 3, META:2 * META], ke[:, 0:META], qn[:, 0:META], start=True, stop=True
                                     ).then_inc(att_done, 1)
                    pe.wait_ge(v_ready, h * 2 + 2)
                    pe.wait_ge(kdt_ready, h * 2 + 2)
                    for c in range(8):
                        b, half = (c - 1) // 2, (c - 1) % 2
                        rows = slice(0, META) if c == 0 else slice(half * CH, half * CH + CH)
                        nc.tensor.matmul(state_bank(c),
                                         kdtm[:] if c == 0 else kdt[rows, b, :], vm[:] if c == 0 else v[rows, b, :],
                                         start=True, stop=True).then_inc(kv_done, 1)
                    pe.wait_ge(att_ready, h * 3 + 3)
                    for j in range(2):
                        nc.tensor.matmul(B[:, 3, 64 + META * j:64 + META * j + META], vm[:, j * P:(j + 1) * P], attm[:],
                                         start=True, stop=True)
                    for b in range(NB):
                        for j in range(2):
                            nc.tensor.matmul(B[:, j, b * P:(b + 1) * P], v[:, b, j * P:(j + 1) * P], att[:, b, :],
                                             start=True, stop=False)
                            for c in (1 + 2 * b, 2 + 2 * b):
                                if j == 0:
                                    pe.wait_ge(state, h * 8 + c)
                                last = nc.tensor.matmul(B[:, j, (c - 1) * CH:c * CH], S[:, c - 1, j * P:(j + 1) * P],
                                                        qe[:, chunk_cols(c)], start=False, stop=(c % 2 == 0))
                    last.then_inc(o_done, 1)

            @block.scalar
            def _(act):
                act.sem_inc(o_out, 3)
                with act.Fori(0, GLA_HEADS) as h:
                    act.wait_ge(v_done, h + 2)
                    nc.scalar.activation(v[:].rearrange("p (a b) n -> p a (b n)", b=2), B[:, 4:6, :], ACT.Copy).then_inc(v_ready, 1)
                    nc.scalar.activation(vm[:], B[0:META, 7, 0:256], ACT.Copy).then_inc(v_ready, 1)
                    act.wait_ge(gate_done, h + 2)
                    nc.scalar.activation(ab[:], B[:, 6, :], ACT.Abs).then_inc(gate_abs, 1)
                    nc.scalar.activation(abm[:], B[0:META, 7, 256:384], ACT.Abs).then_inc(gate_abs, 1)
                    act.wait_ge(gate_abs, h * 2 + 2)
                    nc.scalar.activation(ab[:], ab[:], ACT.Exp, scale=-1.0).then_inc(gate_exp, 1)
                    nc.scalar.activation(abm[:], abm[:], ACT.Exp, scale=-1.0).then_inc(gate_exp, 1)
                    act.wait_ge(gate_exp, h * 2 + 2)
                    nc.scalar.activation(ab[:], ab[:], ACT.Ln, bias=1.0).then_inc(gate_ln, 1)
                    nc.scalar.activation(abm[:], abm[:], ACT.Ln, bias=1.0).then_inc(gate_ln, 1)
                    act.wait_ge(g_last, h * 2 + 2)
                    for e, sign in ((e_pos, 1.0), (e_neg, -1.0)):
                        nc.scalar.activation(e[:, META:L], B[:, 6, :], ACT.Exp, scale=sign).then_inc(e_done, 1)
                        nc.scalar.activation(e[:, 0:META], B[:, 7, 384:400], ACT.Exp, scale=sign).then_inc(e_done, 1)
                    for c in range(9):
                        g = B[:, 7, 384:400] if c == 0 else B[:, 6, (c - 1) * CH:c * CH]
                        nc.scalar.activation(e_last[:, chunk_cols(c)], g, ACT.Exp, bias=glast[:, c:c + 1], scale=-1.0
                                             ).then_inc(to_last, 1)
                    act.wait_ge(kdt_done, h + 1)
                    nc.scalar.activation(kdt[:].rearrange("p b n -> p (b n)"), B[:, 0, :], ACT.Copy).then_inc(kdt_ready, 1)
                    nc.scalar.activation(kdtm[:], B[0:META, 1, 0:P], ACT.Copy).then_inc(kdt_ready, 1)
                    act.wait_ge(o_done, h + 1)
                    for j in range(2):
                        nc.scalar.activation(o[:, bass.ds(h * 2 + j, 1), META:L].rearrange("p a n -> p (a n)"), B[:, j, :],
                                             ACT.Copy).then_inc(o_out, 1)
                    nc.scalar.activation(o[:, bass.ds(h * 2, 2), 0:META],
                                         B[:, 3, 64:64 + 2 * META].rearrange("p (a n) -> p a n", a=2), ACT.Copy).then_inc(o_out, 1)

            @block.vector
            def _(dve):
                nc.vector.memset(att[:], 0.0).then_inc(cleared, 1)
                dve.wait_ge(cleared, 1)
                with dve.Fori(0, GLA_HEADS) as h:
                    for i in range(4):
                        dve.wait_ge((q_in, k_in, v_in, v_in)[i], h * 16 + 16)
                        dve.wait_ge(v_done, h + 1)
                        nc.vector.tensor_copy(high[:, i, :], raw[:, i, :]).then_inc(high_done, 1)
                        dve.wait_ge(high_done, h * 4 + i + 1)
                        nc.vector.tensor_tensor(low_w[:, i, :], raw[:, i, :], high[:, i, :].bitcast(F32), ALU.subtract
                                                ).then_inc(low_done, 1)
                    dve.wait_ge(gate_ln, h * 2 + 2)
                    nc.vector.scalar_tensor_tensor(lg[:], B[:, 6, :], 0.0, ab[:], ALU.min, ALU.subtract).then_inc(lg_done, 1)
                    nc.vector.scalar_tensor_tensor(lgm[:], B[0:META, 7, 256:384], 0.0, abm[:], ALU.min, ALU.subtract
                                                   ).then_inc(lg_done, 1)
                    dve.wait_ge(g_done, h + 1)
                    nc.vector.tensor_copy(glast[:, 0:1], B[:, 7, 399:400]).then_inc(g_last, 1)
                    nc.vector.tensor_copy(glast[:, 1:9], B[:, 6, CH - 1:SEQ:CH]).then_inc(g_last, 1)
                    dve.wait_ge(q_done, h + 1)
                    dve.wait_ge(k_done, h + 1)
                    dve.wait_ge(e_done, h * 4 + 4)
                    for to, bank, sc, e in ((qe, 0, SC, e_pos), (qn, 0, SC, e_neg), (kn, 2, 1.0, e_neg), (ke, 2, 1.0, e_pos),
                                            (kd, 2, 1.0, e_last)):
                        if e is e_last:
                            dve.wait_ge(to_last, h * 9 + 9)
                        nc.vector.scalar_tensor_tensor(to[:].rearrange(two, h=2), B[:, bank:bank + 2, 0:264], sc,
                                                       e[:].rearrange(two, h=2), ALU.mult, ALU.mult).then_inc(prod, 1)
                    dve.wait_ge(att_done, h + 1)
                    for r in halves:
                        nc.vector.tensor_copy(att[r, :, r], B[r, 2, 256:512].rearrange("p (b n) -> p b n", b=NB)).then_inc(att_copy, 1)
                    nc.vector.tensor_copy(attm[:], B[0:META, 3, META:2 * META]).then_inc(att_copy, 1)
                    dve.wait_ge(att_copy, h * 3 + 3)
                    dve.wait_ge(kv_done, h * 8 + 8)
                    nc.vector.tensor_copy(S[:, 0, :], state_bank(0)).then_inc(state, 1)
                    for r in halves:
                        nc.vector.copy_predicated(att[r, :, r], causal[r, :].rearrange("p (b n) -> p b n", b=NB),
                                                  B[r, 2, 0:256].rearrange("p (b n) -> p b n", b=NB)).then_inc(att_ready, 1)
                    nc.vector.copy_predicated(attm[:], causal[0:META, 0:META], B[0:META, 3, 0:META]).then_inc(att_ready, 1)
                    for c in range(1, 8):
                        dve.wait_ge(state, h * 8 + c)
                        kv = state_bank(c)
                        nc.vector.scalar_tensor_tensor(S[:, c, :], S[:, c - 1, :], e_pos[:, META + c * CH - 1:META + c * CH],
                                                       kv, ALU.mult, ALU.add).then_inc(state, 1)


def ssd_prep_phase(k, name, dt, bias, a_log, acum, e_acum, to_end, e_total, e_total_m):
    nc = k.nc
    B = k.banks
    (biased, abs_done, u_done, v, neg, sums, diff, e_diff, exps) = k.sems(
        name, "biased abs_done u_done v neg sums diff e_diff exps")
    n = (NB + 1) * SSD_HEADS
    nx = NB * SSD_HEADS
    with ExitStack() as ctx:
        def sb(nm):
            return ctx.enter_context(nc.sbuf_tensor(f"{name}_{nm}", [P, n], F32))
        x, u, t, z, z2, p, ea, a = (sb(nm) for nm in ("x", "u", "t", "z", "z2", "p", "ea", "a"))
        flat = "p b n -> p (b n)"
        dt_f = dt[:].rearrange(flat)
        to_end_f, acum_f = to_end[:].rearrange(flat), acum[:].rearrange(flat)
        with nc.Block() as block:
            @block.vector
            def _(dve):
                done = [0]

                def step(ins):
                    ins.then_inc(v, 1)
                    done[0] += 1
                    dve.wait_ge(v, done[0])
                nc.vector.tensor_tensor(x[:].rearrange("p (b n) -> p b n", n=SSD_HEADS), dt[:],
                                        bias[:].unsqueeze(1).to_broadcast([P, NB + 1, SSD_HEADS]), ALU.add).then_inc(biased, 1)
                dve.wait_ge(u_done, 1)
                step(nc.vector.tensor_scalar(t[:], u[:], 2.0, None, ALU.add))
                step(nc.vector.reciprocal(t[:], t[:]))
                step(nc.vector.tensor_tensor(z[:], u[:], t[:], ALU.mult))
                step(nc.vector.tensor_tensor(z2[:], z[:], z[:], ALU.mult))
                step(nc.vector.tensor_scalar(p[:], z2[:], 1.0 / 15, None, ALU.mult))
                for c in (13, 11, 9, 7, 5, 3):
                    step(nc.vector.scalar_tensor_tensor(p[:], p[:], 1.0 / c, z2[:], ALU.add, ALU.mult))
                step(nc.vector.scalar_tensor_tensor(p[:], p[:], 1.0, z[:], ALU.add, ALU.mult))
                step(nc.vector.tensor_scalar(p[:], p[:], 2.0, None, ALU.mult))
                step(nc.vector.scalar_tensor_tensor(dt_f, x[:], 0.0, p[:], ALU.max, ALU.add))
                dve.wait_ge(exps, 1)
                nc.vector.scalar_tensor_tensor(a[:].rearrange("p (b n) -> p b n", n=SSD_HEADS), dt[:], -1.0,
                                               ea[:, 0:SSD_HEADS].unsqueeze(1).to_broadcast([P, NB + 1, SSD_HEADS]),
                                               ALU.mult, ALU.mult).then_inc(neg, 1)
                step(nc.vector.memset(to_end[:, NB, :], 0.0))
                step(nc.vector.memset(acum[:, NB, :], 0.0))
                dve.wait_ge(sums, 1)
                step(nc.vector.tensor_copy(acum_f[:, 0:nx], B[:, 0, 0:nx]))
                step(nc.vector.tensor_copy(acum_f[0:META, nx:n], B[0:META, 0, nx:n]))
                nc.vector.tensor_tensor(to_end_f[:, 0:nx], B[:, 1, 0:nx], acum_f[:, 0:nx], ALU.subtract).then_inc(diff, 1)
                nc.vector.tensor_tensor(to_end_f[0:META, nx:n], B[0:META, 1, nx:n], acum_f[0:META, nx:n],
                                        ALU.subtract).then_inc(diff, 1)
                dve.wait_ge(e_diff, 1)
                step(nc.vector.tensor_tensor(to_end_f, to_end_f, dt_f, ALU.mult))

            @block.scalar
            def _(act):
                act.wait_ge(biased, 1)
                nc.scalar.activation(u[:], x[:], ACT.Abs).then_inc(abs_done, 1)
                act.wait_ge(abs_done, 1)
                nc.scalar.activation(u[:], u[:], ACT.Exp, scale=-1.0).then_inc(u_done, 1)
                nc.scalar.activation(ea[:, 0:SSD_HEADS], a_log[:], ACT.Exp).then_inc(exps, 1)
                act.wait_ge(diff, 2)
                nc.scalar.activation(to_end_f, to_end_f, ACT.Exp).then_inc(e_diff, 1)
                nc.scalar.activation(e_acum[:].rearrange(flat), acum_f, ACT.Exp).then_inc(exps, 1)
                for half in range(2):
                    nc.scalar.activation(e_total[:, half].rearrange(flat), B[:, 2 + half, 0:nx], ACT.Exp).then_inc(exps, 1)
                nc.scalar.activation(e_total_m[:], B[:, 4, 0:SSD_HEADS], ACT.Exp).then_inc(exps, 1)

            @block.tensor
            def _(pe):
                pe.wait_ge(neg, 1)
                m = slice(nx, n)
                nc.tensor.matmul(B[:, 0, 0:nx], k.const("tri"), a[:, 0:nx], start=True, stop=True)
                nc.tensor.matmul(B[0:META, 0, m], k.const("tri")[0:META, 0:META], a[0:META, m], start=True, stop=True)
                nc.tensor.matmul(B[:, 1, 0:nx], k.const("same"), a[:, 0:nx], start=True, stop=True)
                nc.tensor.matmul(B[0:META, 1, m], k.const("ones")[0:META, 0:META], a[0:META, m], start=True, stop=True)
                for half in range(2):
                    nc.tensor.matmul(B[:, 2 + half, 0:nx], k.const(f"half{half}"), a[:, 0:nx], start=True, stop=True)
                nc.tensor.matmul(B[:, 4, 0:SSD_HEADS], k.const("ones")[0:META, :], a[0:META, m], start=True, stop=True
                                 ).then_inc(sums, 1)


def ssd_phase(k, name, hn, w_xbc, conv, skip, dt, acum, e_acum, to_end, e_total, e_total_m, y, spare):
    nc = k.nc
    B = k.banks
    T, H, HD = 6, SSD_HPG, SSD_HD
    w_in = k.sems(name, "w_in0 w_in1 w_in2")
    (high_done, low_done, params, product, raw_out, tap, act_done, skipped, x_turned, x_used, b_turned, b_out, cb_done, diag, row_done,
     diff, absd, seg, m_ready, kv_done, decayed, state, inter_scaled, y_done, y_tok, y_turned, y_out, passed, passed_pool) = k.sems(
        name, "high_done low_done params product raw_out tap act_done skipped x_turned x_used b_turned b_out cb_done diag row_done "
              "diff absd seg m_ready kv_done decayed state inter_scaled y_done y_tok y_turned y_out passed passed_pool")
    with ExitStack() as ctx:
        def sb(n, shape):
            return ctx.enter_context(nc.sbuf_tensor(f"{name}_{n}", shape, F32))
        raw_w = sb("raw_w", [P, 3, KD * P])
        high, low_w = (ctx.enter_context(nc.sbuf_tensor(f"{name}_{n}", [P, 2, KD * P], F32R)) for n in ("high", "low"))
        cw, dg = sb("cw", [P, T, 5]), sb("dg", [P, 4])
        xd, raw, acc = spare[:, 0:4, :], spare[:, 4:6, :], spare[:, 6:8, :]
        xc = sb("xc", [P, T, L])
        xdt, xend = sb("xdt", [P, NB + 1, H * HD]), sb("xend", [P, NB + 1, H * HD])
        bt = sb("bt", [P, NB + 1, P])
        X, E, M = sb("X", [P, H * HD]), sb("E", [P, 2, H * HD]), sb("M", [P, NB + 1, H * HD])
        S, decay = sb("S", [P, 4, H * HD]), sb("decay", [P, H * HD])
        yt = sb("yt", [P, 2, H * HD])
        ident = k.const("ident")
        diag64 = k.const("diag64")

        def heads(a, n=HD):
            return a.rearrange("p (r t) -> p r t", t=n)

        def of(a, r, b, g, n=HD):
            m = r.stop - r.start
            return a[r, b, bass.ds(g * H, H)].unsqueeze(2).to_broadcast([m, H, n])

        full, meta = slice(0, P), slice(0, META)
        with nc.Block() as block:
            @block.sync
            def _(sp):
                with sp.Fori(0, SSD_GROUPS) as g:
                    for j in range(T):
                        sp.wait_ge(low_done, g * T + j + 1)
                        sp.dma_start(raw_w[:, j % 3, :], w_xbc[bass.ds(g * T + j, 1)].rearrange("a p n -> (a p) n")
                                     ).then_inc(w_in[j % 3], 16)

            @block.gpsimd
            def _(pool):
                with pool.Fori(0, SSD_GROUPS) as g:
                    pool.wait_ge(y_out, g * 5 + 1)
                    pool.wait_ge(tap, g * 24 + 1)
                    nc.gpsimd.tensor_copy(cw[:], conv[:, bass.ds(g, 1)].rearrange("p a t n -> p (a t) n")).then_inc(params, 1)
                    nc.gpsimd.tensor_copy(dg[:], skip[:, bass.ds(g * 4, 4)]).then_inc(params, 1)
                    for b in range(NB + 1):
                        r, n = (full, HD) if b < NB else (meta, META)
                        pool.wait_ge(row_done, g * 5 + b + 1)
                        nc.gpsimd.tensor_tensor(heads(X[r, 0:H * n], n), of(acum, r, b, g, n),
                                                diag64[r, 0:n].unsqueeze(1).to_broadcast([r.stop, H, n]), ALU.mult
                                                ).then_inc(diag, 1)
                    pool.wait_ge(params, g * 2 + 2)
                    for j in range(4):
                        pool.wait_ge(act_done, g * T + j + 1)
                        pool.sem_inc(passed_pool, 1)
                        nc.gpsimd.tensor_scalar(xd[:, j, :], xc[:, j, :], dg[:, j:j + 1], None, ALU.mult).then_inc(skipped, 1)

            @block.tensor
            def _(pe):
                pe.sem_inc(product, 2)
                pe.sem_inc(row_done, 1)
                with pe.Fori(0, SSD_GROUPS) as g:
                    for j in range(T):
                        pe.wait_ge(low_done, g * T + j + 4)
                        if j < 3:
                            pe.wait_ge(y_out, g * 5 + 1)
                        else:
                            pe.wait_ge(raw_out, g * T + j - 2)
                        for c in range(KD):
                            for i in range(2):
                                last = product3(nc, B[:, 2 * (j % 3) + i, 0:264],
                                                [a[:, j % 2, c * P:(c + 1) * P] for a in (high, low_w)],
                                                [a[:, c, i * 264:i * 264 + 264] for a in hn], c == 0, c == KD - 1)
                        last.then_inc(product, 1)
                    pe.wait_ge(raw_out, g * T + T)
                    pe.wait_ge(act_done, g * T + T)
                    for b in range(NB):
                        nc.tensor.transpose(B[:, 0, b * P:(b + 1) * P], xc[:, 4, block_cols(b)], ident)
                    last = nc.tensor.transpose(B[meta, 2, 0:P], xc[:, 4, meta], ident).then_inc(b_turned, 1)
                    for c in range(1, 9):
                        b, half = (c - 1) // 2, (c - 1) % 2
                        nc.tensor.matmul(B[half * CH:half * CH + CH, 3, b * CH:b * CH + CH], xc[:, 4, chunk_cols(c)],
                                         xc[:, 5, chunk_cols(c)], start=True, stop=True)
                    nc.tensor.matmul(B[meta, 3, 256:256 + META], xc[:, 4, meta], xc[:, 5, meta], start=True, stop=True
                                     ).then_inc(cb_done, 1)
                    for b in range(NB + 1):
                        r = full if b < NB else meta
                        if b >= 2:
                            pe.wait_ge(x_used, g * 10 + 2 * (b - 1))
                        for j in range(4):
                            last = nc.tensor.transpose(B[r, 6 + b % 2, j * P:(j + 1) * P],
                                                       xc[:, j, block_cols(b) if b < NB else meta], ident)
                        last.then_inc(x_turned, 1)
                    for b in range(NB + 1):
                        r, n = (full, HD) if b < NB else (meta, META)
                        pe.wait_ge(diag, g * 5 + b + 1)
                        if b >= 2:
                            pe.wait_ge(diff, g * 5 + b - 1)
                        pe.sem_inc(passed, 1)
                        nc.tensor.matmul(B[r, 4 + b % 2, 0:H * n], k.const("same")[r, r] if b < NB else k.const("ones")[r, r],
                                         X[r, 0:H * n], start=True, stop=True).then_inc(row_done, 1)

                    def state_part(c):
                        b, half = (c - 1) // 2, (c - 1) % 2
                        rr = meta if c == 0 else slice(half * CH, half * CH + CH)
                        if c >= 2:
                            pe.wait_ge(state, g * 8 + c - 1)
                        nc.tensor.matmul(B[:, 6 + c % 2, :], bt[rr, NB if c == 0 else b, :], xend[rr, NB if c == 0 else b, :],
                                         start=True, stop=True).then_inc(kv_done, 1)

                    pe.wait_ge(x_used, g * 10 + 10)
                    pe.wait_ge(b_out, g * 2 + 2)
                    state_part(0)
                    for b in range(NB + 1):
                        r = full if b < NB else meta
                        pe.wait_ge(m_ready, g * 5 + b + 1)
                        if b > 0:
                            pe.wait_ge(y_tok, g * 5 + b)
                        pe.sem_inc(passed, 1)
                        for i in range(2 if b < NB else 1):
                            rr = slice(i * CH, i * CH + CH) if b < NB else meta
                            n = CH if b < NB else META
                            for h in range(H):
                                last = nc.tensor.matmul(B[rr, 0, h * HD:(h + 1) * HD], M[rr, b, h * n:(h + 1) * n],
                                                        xdt[rr, b, h * HD:(h + 1) * HD], start=True, stop=True)
                        if b < NB:
                            for i in range(2):
                                c = 1 + 2 * b + i
                                pe.wait_ge(state, g * 8 + c)
                                last = nc.tensor.matmul(B[i * CH:i * CH + CH, 1, :], xc[:, 5, chunk_cols(c)],
                                                        S[:, (c - 1) % 4, :], start=True, stop=True)
                                if c < 8:
                                    if i == 0:
                                        state_part(c)
                        last.then_inc(y_done, 1)
                        if b < NB - 1:
                            state_part(2 + 2 * b)
                        pe.wait_ge(y_tok, g * 5 + b + 1)
                        if b >= 2:
                            pe.wait_ge(y_out, g * 5 + b)
                        if b == 0:
                            pe.wait_ge(diff, g * 5 + 5)
                        pe.sem_inc(passed, 1)
                        for j in range(4):
                            n = P if b < NB else META
                            last = nc.tensor.transpose(B[:, 4 + b % 2, j * n:(j + 1) * n], yt[r, b % 2, j * P:(j + 1) * P],
                                                       ident[r, r])
                        last.then_inc(y_turned, 1)

            @block.scalar
            def _(act):
                with act.Fori(0, SSD_GROUPS) as g:
                    def silu(j):
                        act.wait_ge(tap, g * 24 + 4 * (j + 1) + 1)
                        nc.scalar.activation(xc[:, j, :], acc[:, j % 2, :], ACT.Silu).then_inc(act_done, 1)
                    for j in range(T):
                        act.wait_ge(product, g * T + j + 3)
                        if j >= 2:
                            act.wait_ge(tap, g * 24 + 4 * (j - 1) + 1)
                        nc.scalar.activation(raw[:, j % 2, :].rearrange("p (h n) -> p h n", h=2),
                                             B[:, 2 * (j % 3):2 * (j % 3) + 2, 0:264], ACT.Copy).then_inc(raw_out, 1)
                        if j > 0:
                            silu(j - 1)
                    silu(T - 1)
                    act.wait_ge(b_turned, g + 1)
                    nc.scalar.activation(bt[:, 0:NB, :].rearrange("p b n -> p (b n)"), B[:, 0, :], ACT.Copy).then_inc(b_out, 1)
                    nc.scalar.activation(bt[meta, NB, :], B[meta, 2, 0:P], ACT.Copy).then_inc(b_out, 1)
                    for b in range(NB + 1):
                        r, n = (full, HD) if b < NB else (meta, META)
                        act.wait_ge(diff, g * 5 + b + 1)
                        nc.scalar.activation(E[r, b % 2, 0:H * n], E[r, b % 2, 0:H * n], ACT.Abs).then_inc(absd, 1)
                        act.wait_ge(absd, g * 5 + b + 1)
                        nc.scalar.activation(E[r, b % 2, 0:H * n], E[r, b % 2, 0:H * n], ACT.Exp, scale=-1.0).then_inc(seg, 1)

            @block.vector
            def _(dve):
                dve.sem_inc(tap, 1)
                dve.sem_inc(low_done, 3)
                dve.sem_inc(y_out, 1)
                with dve.Fori(0, SSD_GROUPS) as g:
                    def split(j):
                        dve.wait_ge(w_in[j % 3], g * 32 + (16 * (j // 3) + 16))
                        dve.wait_ge(product, g * T + j + 1)
                        nc.vector.tensor_copy(high[:, j % 2, :], raw_w[:, j % 3, :]).then_inc(high_done, 1)
                        dve.wait_ge(high_done, g * T + j + 1)
                        nc.vector.tensor_tensor(low_w[:, j % 2, :], raw_w[:, j % 3, :], high[:, j % 2, :].bitcast(F32),
                                                ALU.subtract).then_inc(low_done, 1)

                    def convolve(j):
                        dve.wait_ge(raw_out, g * T + j + 1)
                        if j >= 2:
                            dve.wait_ge(act_done, g * T + j - 1)
                        x, to = raw[:, j % 2, :], acc[:, j % 2, :]
                        nc.vector.tensor_scalar(to, x, cw[:, j, 3:4], cw[:, j, 4:5], ALU.mult, ALU.add).then_inc(tap, 1)
                        for s in (1, 2, 3):
                            dve.wait_ge(tap, g * 24 + 4 * j + s + 1)
                            nc.vector.scalar_tensor_tensor(to[:, s:L], x[:, 0:L - s], cw[:, j, 3 - s:4 - s], to[:, s:L],
                                                           ALU.mult, ALU.add).then_inc(tap, 1)
                    split(0)
                    split(1)
                    dve.wait_ge(params, g * 2 + 2)
                    for j in range(T):
                        if j + 2 < T:
                            split(j + 2)
                        convolve(j)
                    for b in range(NB + 1):
                        r = full if b < NB else meta
                        dve.wait_ge(x_turned, g * 5 + b + 1)
                        for to, by in ((xdt, dt), (xend, to_end)):
                            nc.vector.tensor_tensor(heads(to[r, b, :]), heads(B[r, 6 + b % 2, :]), of(by, r, b, g), ALU.mult
                                                    ).then_inc(x_used, 1)

                    def weights(b):
                        r, n = (full, HD) if b < NB else (meta, META)
                        dve.wait_ge(seg, g * 5 + b + 1)
                        if b == 0:
                            dve.wait_ge(cb_done, g + 1)
                        cb = B[r, 3, b * CH:b * CH + CH] if b < NB else B[r, 3, 256:256 + META]
                        nc.vector.tensor_tensor(heads(M[r, b, 0:H * n], n), heads(E[r, b % 2, 0:H * n], n),
                                                cb.unsqueeze(1).to_broadcast([r.stop, H, n]), ALU.mult).then_inc(m_ready, 1)
                    for b in range(NB + 1):
                        r, n = (full, HD) if b < NB else (meta, META)
                        if b >= 2:
                            weights(b - 2)
                            dve.wait_ge(m_ready, g * 5 + b - 1)
                        dve.wait_ge(row_done, g * 5 + b + 2)
                        nc.vector.tensor_tensor(heads(E[r, b % 2, 0:H * n], n), heads(B[r, 4 + b % 2, 0:H * n], n),
                                                of(acum, r, b, g, n), ALU.subtract).then_inc(diff, 1)
                    weights(NB - 1)
                    weights(NB)

                    def new_state(c):
                        b, half = (c - 1) // 2, (c - 1) % 2
                        dve.wait_ge(kv_done, g * 8 + c + 1)
                        if c == 0:
                            nc.vector.tensor_copy(S[:, 0, :], B[:, 6, :]).then_inc(state, 1)
                            return
                        dve.wait_ge(state, g * 8 + c)
                        by = e_total[:, half, b, bass.ds(g * H, H)].unsqueeze(2).to_broadcast([P, H, HD])
                        nc.vector.tensor_tensor(heads(decay[:]), heads(S[:, (c - 1) % 4, :]), by, ALU.mult).then_inc(decayed, 1)
                        dve.wait_ge(decayed, g * 7 + c)
                        nc.vector.tensor_tensor(S[:, c % 4, :], decay[:], B[:, 6 + c % 2, :], ALU.add).then_inc(state, 1)
                    new_state(0)
                    for b in range(NB + 1):
                        r, n = (full, P) if b < NB else (meta, META)
                        if b < NB:
                            new_state(1 + 2 * b)
                        dve.wait_ge(y_done, g * 5 + b + 1)
                        if b < NB:
                            nc.vector.tensor_tensor(heads(yt[r, b % 2, :]), heads(B[r, 1, :]), of(e_acum, r, b, g), ALU.mult
                                                    ).then_inc(inter_scaled, 1)
                            dve.wait_ge(inter_scaled, g * 4 + b + 1)
                            nc.vector.tensor_tensor(yt[r, b % 2, :], yt[r, b % 2, :], B[r, 0, :], ALU.add).then_inc(y_tok, 1)
                        else:
                            nc.vector.tensor_copy(yt[r, b % 2, :], B[r, 0, :]).then_inc(y_tok, 1)
                        if b < NB - 1:
                            new_state(2 + 2 * b)
                        dve.wait_ge(skipped, g * 4 + 4)
                        dve.wait_ge(y_turned, g * 5 + b + 1)
                        cols = block_cols(b) if b < NB else meta
                        nc.vector.tensor_tensor(y[:, bass.ds(g * 4, 4), cols], xd[:, :, cols],
                                                B[:, 4 + b % 2, 0:4 * n].rearrange("p (j n) -> p j n", j=4), ALU.add
                                                ).then_inc(y_out, 1)


def route_phase(k, name, q, keys, chosen):
    nc = k.nc
    B = k.banks
    H, SIDES = PEER_HEADS, 2 * PEER_HEADS
    LOW = -3.0e38
    q_block, scored, v, passed, exp_done, turned, out_done = k.sems(name, "q_block scored v passed exp_done turned out_done")
    STEPS = 5 * (SIDES + H) + 14
    with ExitStack() as ctx:
        def sb(n, shape, dt=F32):
            return ctx.enter_context(nc.sbuf_tensor(f"{name}_{n}", shape, dt))
        qb = sb("qb", [P, SIDES, P])
        rest = sb("rest", [P, SIDES, KEYS])
        top, idx, idxf = sb("top", [P, SIDES, TOPK]), sb("idx", [P, SIDES, TOPK], U32), sb("idxf", [P, SIDES, TOPK])
        cand, crest = sb("cand", [P, H, TOPK * TOPK]), sb("crest", [P, H, TOPK * TOPK])
        best, pos = sb("best", [P, H, TOPK]), sb("pos", [P, H, TOPK], U32)
        parts, partsf = sb("parts", [P, 2, H * TOPK], U32), sb("partsf", [P, 2, H * TOPK])
        hot = sb("hot", [P, H * TOPK, TOPK])
        picked = sb("picked", [P, 3, H * TOPK])
        total = sb("total", [P, H])
        weights = picked[:, 2, :].rearrange("p (h n) -> p h n", h=H)
        iota16 = k.const("iota16")
        with nc.Block() as block:
            @block.scalar
            def _(act):
                act.sem_inc(out_done, 1)
                with act.Fori(0, NB) as b:
                    act.wait_ge(scored, b + 1)
                    nc.scalar.activation(qb[:], q[:, :, bass.ds(b * P, P)], ACT.Copy).then_inc(q_block, 1)
                    act.wait_ge(exp_done, b * 2 + 1)
                    nc.scalar.activation(weights, weights, ACT.Exp).then_inc(exp_done, 1)
                    act.wait_ge(turned, b + 1)
                    nc.scalar.activation(chosen[:, :, bass.ds(b * P, P)], B[:, 4, 0:3 * P].rearrange("p (a n) -> p a n", a=3),
                                         ACT.Copy).then_inc(out_done, 1)

            @block.tensor
            def _(pe):
                pe.sem_inc(scored, 1)
                with pe.Fori(0, NB) as b:
                    pe.wait_ge(q_block, b + 1)
                    pe.wait_ge(out_done, b + 1)
                    for r in range(SIDES):
                        last = nc.tensor.matmul(B[:, r // 4, (r % 4) * KEYS:(r % 4 + 1) * KEYS], qb[:, r, :], keys[:, r, :],
                                                start=True, stop=True)
                    last.then_inc(scored, 1)
                    pe.wait_ge(v, b * STEPS + STEPS)
                    for j in range(3):
                        last = nc.tensor.transpose(B[:, 4, j * P:(j + 1) * P], picked[:, j, :], k.const("ident"))
                    last.then_inc(turned, 1)

            @block.vector
            def _(dve):
                with dve.Fori(0, NB) as b:
                    done = [0]

                    def step(ins):
                        ins.then_inc(v, 1)
                        done[0] += 1

                    def settle():
                        dve.wait_ge(v, b * STEPS + done[0])
                        dve.sem_inc(passed, 1)

                    def sixteen(rows, values, spare_values, top_of, index_of):
                        for r in range(rows):
                            step(nc.vector.max(top_of(r)[:, 0:8], values(r)))
                        settle()
                        for r in range(rows):
                            step(nc.vector.max_index(index_of(r)[:, 0:8], top_of(r)[:, 0:8], values(r)))
                            step(nc.vector.match_replace(spare_values(r), top_of(r)[:, 0:8], values(r), LOW))
                        settle()
                        for r in range(rows):
                            step(nc.vector.max(top_of(r)[:, 8:16], spare_values(r)))
                        settle()
                        for r in range(rows):
                            step(nc.vector.max_index(index_of(r)[:, 8:16], top_of(r)[:, 8:16], spare_values(r)))
                        settle()
                    dve.wait_ge(scored, b + 2)
                    dve.sem_inc(passed, 1)
                    sixteen(SIDES, lambda r: B[:, r // 4, (r % 4) * KEYS:(r % 4 + 1) * KEYS], lambda r: rest[:, r, :],
                            lambda r: top[:, r, :], lambda r: idx[:, r, :])
                    step(nc.vector.tensor_copy(idxf[:], idx[:]))
                    square = [P, H, TOPK, TOPK]
                    step(nc.vector.tensor_tensor(cand[:].rearrange("p h (a c) -> p h a c", a=TOPK),
                                                 top[:, 0::2, :].unsqueeze(3).to_broadcast(square),
                                                 top[:, 1::2, :].unsqueeze(2).to_broadcast(square), ALU.add))
                    settle()
                    sixteen(H, lambda r: cand[:, r, :], lambda r: crest[:, r, :], lambda r: best[:, r, :], lambda r: pos[:, r, :])
                    dve.wait_ge(out_done, b + 1)
                    nc.vector.tensor_tensor(weights, best[:], best[:, :, 0:1].to_broadcast([P, H, TOPK]), ALU.subtract
                                            ).then_inc(exp_done, 1)
                    pos_f = pos[:].rearrange("p h n -> p (h n)")
                    step(nc.vector.tensor_scalar(parts[:, 0, :], pos_f, 4, None, ALU.logical_shift_right))
                    step(nc.vector.tensor_scalar(parts[:, 1, :], pos_f, 15, None, ALU.bitwise_and))
                    settle()
                    step(nc.vector.tensor_copy(partsf[:], parts[:]))
                    settle()
                    for side in range(2):
                        step(nc.vector.tensor_tensor(hot[:], partsf[:, side, :].unsqueeze(2).to_broadcast([P, P, TOPK]),
                                                     iota16.unsqueeze(1).to_broadcast([P, P, TOPK]), ALU.is_equal))
                        settle()
                        h4 = hot[:].rearrange("p (h n) a -> p h n a", h=H)
                        step(nc.vector.tensor_tensor(h4, h4, idxf[:, side::2, :].unsqueeze(2).to_broadcast(square), ALU.mult))
                        settle()
                        step(nc.vector.tensor_reduce(picked[:, side, :], hot[:], AX, ALU.add))
                        settle()
                    dve.wait_ge(exp_done, b * 2 + 2)
                    step(nc.vector.tensor_reduce(total[:], weights, AX, ALU.add))
                    settle()
                    step(nc.vector.reciprocal(total[:], total[:]))
                    settle()
                    step(nc.vector.tensor_tensor(weights, weights, total[:].unsqueeze(2).to_broadcast([P, H, TOPK]), ALU.mult))
                    assert done[0] == STEPS, done


def spread_phase(k, name, chosen, w_dram):
    nc = k.nc
    B = k.banks
    T = 4
    hot_done, product, copied = k.sems(name, "hot_done product copied")
    stored = k.sems(name, "stored0 stored1")
    with ExitStack() as ctx:
        def sb(n, shape):
            return ctx.enter_context(nc.sbuf_tensor(f"{name}_{n}", shape, F32))
        cols, rws = sb("cols", [P, 2, T, P]), sb("rows", [P, 2, T, P])
        out = [sb(f"out{i}", [P, KEYS, P]) for i in range(2)]
        iota = k.const("iota")
        turns = P // (2 * T)
        with nc.Block() as block:
            @block.vector
            def _(dve):
                for b in range(NB):
                    with dve.Fori(0, turns) as i:
                        for j in range(2):
                            dve.wait_ge(product, b * 2 * turns + i * 2 + (j + 1))
                            for t in range(T):
                                at = bass.ds(b * P + i * 2 * T + (j * T + t), 1)
                                nc.vector.tensor_scalar(cols[:, j, t, :], iota, chosen[:, 1, at], None, ALU.is_equal)
                                last = nc.vector.tensor_scalar(rws[:, j, t, :], iota, chosen[:, 0, at], chosen[:, 2, at],
                                                               ALU.is_equal, ALU.mult)
                            last.then_inc(hot_done, 1)

            @block.tensor
            def _(pe):
                pe.sem_inc(product, 2)
                for b in range(NB):
                    with pe.Fori(0, turns) as i:
                        for j in range(2):
                            pe.wait_ge(hot_done, b * 2 * turns + i * 2 + (j + 1))
                            pe.wait_ge(copied, b * 2 * turns + i * 2 + (j + 1))
                            for t in range(T):
                                last = nc.tensor.matmul(B[:, j, t * P:(t + 1) * P], cols[:, j, t, :], rws[:, j, t, :],
                                                        start=True, stop=True)
                            last.then_inc(product, 1)

            @block.scalar
            def _(act):
                act.sem_inc(copied, 2)
                for b in range(NB):
                    if b >= 2:
                        act.wait_ge(stored[b % 2], 64)
                    with act.Fori(0, turns) as i:
                        for j in range(2):
                            act.wait_ge(product, b * 2 * turns + i * 2 + (j + 3))
                            nc.scalar.activation(out[b % 2][:, :, bass.ds(i * 2 * T + j * T, T)],
                                                 B[:, j, :].rearrange("p (t n) -> p n t", t=T), ACT.Copy).then_inc(copied, 1)

            @block.sync
            def _(sp):
                for b in range(NB):
                    sp.wait_ge(copied, 2 + (b + 1) * 2 * turns)
                    for part in range(4):
                        r = slice(part * 32, (part + 1) * 32)
                        sp.dma_start(w_dram[r, :, b * P:(b + 1) * P].rearrange("i j n -> j i n"), out[b % 2][:, r, :]
                                     ).then_inc(stored[b % 2], 16)
                for s in stored:
                    sp.wait_ge(s, 128)


def expert_phase(k, name, hb, u, v, w_dram, acc):
    nc = k.nc
    B = k.banks
    G, SET, LAG = GROUP, GROUP // 2, 2
    TURNS = KEYS // G
    (u_done, gelu, a_full, a_high, a_ready, v_done, added, u_high, u_low, v_high, v_low) = k.sems(
        name, "u_done gelu a_full a_high a_ready v_done added u_high u_low v_high v_low")
    u_in, w_in = (k.sems(name, " ".join(f"{n}_in{r}" for r in range(RING))) for n in "uw")
    v_in = k.sems(name, "v_in0 v_in1")
    with ExitStack() as ctx:
        def sb(n, shape, dt=F32):
            return ctx.enter_context(nc.sbuf_tensor(f"{name}_{n}", shape, dt))
        us, ws, vs = sb("us", [P, RING, KD * P]), sb("ws", [P, RING, SEQ]), sb("vs", [P, 2, D])
        uh, ul = sb("uh", [P, 2, KD * P], F32R), sb("ul", [P, 2, KD * P], F32R)
        vh, vl = sb("vh", [P, G, D], F32R), sb("vl", [P, G, D], F32R)
        A = sb("A", [P, 2, SEQ])
        ah, al = sb("ah", [P, G, SEQ], F32R), sb("al", [P, G, SEQ], F32R)

        def run(engine, turn, end):
            for t in range(G):
                turn(0, t, True)
            with engine.Fori(1, TURNS) as g:
                for t in range(G):
                    turn(g, t, False)
            end()

        def lagging(part, g, t, first):
            if t >= LAG:
                part(g, t - LAG)
            elif not first:
                part(g - 1, t - LAG + G)

        def last_lagging(part):
            for t in range(G - LAG, G):
                part(TURNS - 1, t)

        with nc.Block() as block:
            @block.sync
            def _(sp):
                def others(g, t):
                    sp.wait_ge(a_ready, g * G + (t + 1))
                    sp.dma_start(ws[:, t % RING, :], w_dram[bass.ds(g * G + t, 1)].rearrange("a p n -> (a p) n")
                                 ).then_inc(w_in[t % RING], 16)
                    sp.wait_ge(v_low, g * G + (t + 1))
                    sp.dma_start(vs[:, t % 2, :], v[bass.ds((g * G + t) * P, P), :]).then_inc(v_in[t % 2], 16)

                def turn(g, t, first):
                    sp.wait_ge(u_low, g * G + (t + 1))
                    sp.dma_start(us[:, t % RING, :], u[bass.ds(g * G + t, 1)].rearrange("a p n -> (a p) n")
                                 ).then_inc(u_in[t % RING], 16)
                    lagging(others, g, t, first)
                run(sp, turn, lambda: last_lagging(others))

            @block.tensor
            def _(pe):
                pe.sem_inc(u_done, 2)
                pe.sem_inc(v_done, 2 * KD)

                def v_part(g, s, c):
                    if c == 0:
                        pe.wait_ge(v_low, g * G + (s * SET + SET + 2))
                        pe.wait_ge(a_ready, g * G + (s * SET + SET + RING))
                    pe.wait_ge(added, g * 2 * KD + (s * KD + c + 1))
                    for j in range(SET):
                        t = s * SET + j
                        last = product3(nc, B[:, 4 + c % 4, :], [a[:, t, c * P:(c + 1) * P] for a in (vh, vl)],
                                        [a[:, t, :] for a in (ah, al)], j == 0, j == SET - 1)
                    last.then_inc(v_done, 1)

                def turn(g, t, first):
                    pe.wait_ge(u_low, g * G + (t + 1 + RING))
                    pe.wait_ge(gelu, g * G + (t + 1))
                    for c in range(KD):
                        last = product3(nc, B[:, t % RING, :], [a[:, t % 2, c * P:(c + 1) * P] for a in (uh, ul)],
                                        [a[:, c, :] for a in hb], c == 0, c == KD - 1)
                    last.then_inc(u_done, 1)
                    for c in (2 * (t % SET), 2 * (t % SET) + 1):
                        if t >= SET:
                            v_part(g, 0, c)
                        elif not first:
                            v_part(g - 1, 1, c)

                def end():
                    for c in range(KD):
                        v_part(TURNS - 1, 1, c)
                run(pe, turn, end)

            @block.scalar
            def _(act):
                act.sem_inc(gelu, RING)

                def others(g, t):
                    act.wait_ge(u_done, g * G + (t + 3))
                    act.wait_ge(a_ready, g * G + (t + 3))
                    nc.scalar.activation(A[:, t % 2, :], B[:, t % RING, :], ACT.Gelu_apprx_tanh).then_inc(gelu, 1)
                    act.wait_ge(a_full, g * G + (t + 1))
                    act.wait_ge(v_done, g * 2 * KD + (t // SET * KD + KD))
                    nc.scalar.activation(ah[:, t, :], A[:, t % 2, :], ACT.Copy).then_inc(a_high, 1)
                    act.wait_ge(v_in[t % 2], g * 64 + (16 * (t // 2) + 16))
                    nc.scalar.activation(vh[:, t, :], vs[:, t % 2, :], ACT.Copy).then_inc(v_high, 1)

                def turn(g, t, first):
                    act.wait_ge(u_in[t % RING], g * 32 + (16 * (t // RING) + 16))
                    act.wait_ge(u_done, g * G + (t + 1))
                    nc.scalar.activation(uh[:, t % 2, :], us[:, t % RING, :], ACT.Copy).then_inc(u_high, 1)
                    lagging(others, g, t, first)
                run(act, turn, lambda: last_lagging(others))

            @block.gpsimd
            def _(pool):
                pool.sem_inc(u_low, RING)
                pool.sem_inc(v_low, 2)

                def others(g, t):
                    pool.wait_ge(v_high, g * G + (t + 1))
                    nc.gpsimd.tensor_tensor(vl[:, t, :], vs[:, t % 2, :], vh[:, t, :].bitcast(F32), ALU.subtract
                                            ).then_inc(v_low, 1)

                def turn(g, t, first):
                    pool.wait_ge(u_high, g * G + (t + 1))
                    nc.gpsimd.tensor_tensor(ul[:, t % 2, :], us[:, t % RING, :], uh[:, t % 2, :].bitcast(F32), ALU.subtract
                                            ).then_inc(u_low, 1)
                    lagging(others, g, t, first)
                run(pool, turn, lambda: last_lagging(others))

            @block.vector
            def _(dve):
                dve.sem_inc(a_ready, RING)
                dve.sem_inc(added, 4)

                def add(g, s, c, first):
                    dve.wait_ge(v_done, g * 2 * KD + (s * KD + c + 1 + 2 * KD))
                    if not first:
                        dve.wait_ge(added, g * 2 * KD + (s * KD + c - 3))
                    nc.vector.tensor_tensor(acc[:, c, :], acc[:, c, :], B[:, 4 + c % 4, :], ALU.add).then_inc(added, 1)

                def turn(g, t, first):
                    dve.wait_ge(gelu, g * G + (t + 1 + RING))
                    dve.wait_ge(w_in[t % RING], g * 32 + (16 * (t // RING) + 16))
                    nc.vector.tensor_tensor(A[:, t % 2, :], A[:, t % 2, :], ws[:, t % RING, :], ALU.mult).then_inc(a_full, 1)
                    dve.wait_ge(a_high, g * G + (t + 1))
                    nc.vector.tensor_tensor(al[:, t, :], A[:, t % 2, :], ah[:, t, :].bitcast(F32), ALU.subtract
                                            ).then_inc(a_ready, 1)
                    for c in (2 * (t % SET), 2 * (t % SET) + 1):
                        if t >= SET:
                            add(g, 0, c, first)
                        elif not first:
                            add(g - 1, 1, c, False)

                def end():
                    for c in range(KD):
                        add(TURNS - 1, 1, c, False)
                run(dve, turn, end)


def keys_values_phase(k, name, x, w_dram, key, value):
    nc = k.nc
    B = k.banks
    done, out, high_done, low_done = k.sems(name, "done out high_done low_done")
    w_in = k.sems(name, "w_in0 w_in1")
    W = 2 * P
    PARTS = w_dram.shape[2] // W
    with ExitStack() as ctx:
        raw = ctx.enter_context(nc.sbuf_tensor(f"{name}_raw", [P, 2, KD, W], F32))
        w = [ctx.enter_context(nc.sbuf_tensor(f"{name}_{n}", [P, 2, KD, W], F32R)) for n in ("high", "low")]
        with nc.Block() as block:
            @block.sync
            def _(sp):
                for j in range(PARTS):
                    if j >= 2:
                        sp.wait_ge(low_done, j - 1)
                    sp.dma_start(raw[:, j % 2], w_dram[:, :, j * W:(j + 1) * W]).then_inc(w_in[j % 2], 16)

            @block.vector
            def _(dve):
                for j in range(PARTS):
                    dve.wait_ge(w_in[j % 2], 16 * (j // 2) + 16)
                    if j >= 2:
                        dve.wait_ge(done, j)
                    nc.vector.tensor_copy(w[0][:, j % 2], raw[:, j % 2]).then_inc(high_done, 1)
                    dve.wait_ge(high_done, j + 1)
                    nc.vector.tensor_tensor(w[1][:, j % 2], raw[:, j % 2], w[0][:, j % 2].bitcast(F32), ALU.subtract
                                            ).then_inc(low_done, 1)

            @block.tensor
            def _(pe):
                pe.wait_ge(low_done, 1)
                for c in range(KD):
                    last = product3(nc, B[:, 0, :], [a[:, 0, c, 0:P] for a in w], [a[:, c, :] for a in x], c == 0, c == KD - 1)
                last.then_inc(done, 1)
                for j in range(PARTS):
                    pe.wait_ge(low_done, j + 1)
                    n, a0 = (P, P) if j == 0 else (W, 0)
                    for b in range(NB):
                        for c in range(KD):
                            to = B[:, 1 + 2 * j + b // 2, (b % 2) * n:(b % 2) * n + n]
                            last = product3(nc, to, [a[:, c, b * P:(b + 1) * P] for a in x],
                                            [a[:, j % 2, c, a0:a0 + n] for a in w], c == 0, c == KD - 1)
                    last.then_inc(done, 1)

            @block.scalar
            def _(act):
                act.wait_ge(done, 1)
                nc.scalar.activation(key[:], B[:, 0, :], ACT.Copy).then_inc(out, 1)
                for j in range(PARTS):
                    act.wait_ge(done, j + 2)
                    n, at = (P, 0) if j == 0 else (W, P + (j - 1) * W)
                    for half in range(2):
                        nc.scalar.activation(value[:, 2 * half:2 * half + 2, at:at + n],
                                             B[:, 1 + 2 * j + half, 0:2 * n].rearrange("p (b n) -> p b n", b=2), ACT.Copy
                                             ).then_inc(out, 1)


def attention_phase(k, name, q, key, value, sinks, out):
    nc = k.nc
    B = k.banks
    SC = A_HD ** -0.5
    (q_tile, scored, masked, max_done, exp_done, inv, normed, turned, turned_out, o_done, o_out, sunk) = k.sems(
        name, "q_tile scored masked max_done exp_done inv normed turned turned_out o_done o_out sunk")
    UNITS = [(kv, b) for b in range(NB) for kv in range(KV_HEADS)]
    N = len(UNITS)
    with ExitStack() as ctx:
        def sb(n, shape):
            return ctx.enter_context(nc.sbuf_tensor(f"{name}_{n}", shape, F32))
        qt = sb("qt", [P, SEQ])
        sc, pr, pt = sb("sc", [P, 2, 1 + 2 * P]), sb("pr", [P, 2, 1 + 2 * P]), sb("pt", [P, 2, 2 * P])
        nmax, total, rinv = sb("nmax", [P, N]), sb("total", [P, N]), sb("rinv", [P, N])
        band, ident = k.const("band"), k.const("ident")

        def width(b):
            return 2 * P if b else P
        with nc.Block() as block:
            @block.gpsimd
            def _(pool):
                with pool.Fori(0, 4) as t:
                    pool.wait_ge(scored, t * N + 1)
                    nc.gpsimd.tensor_copy(qt[:], q[:, bass.ds(t, 1), :].rearrange("p a n -> p (a n)")).then_inc(q_tile, 1)

            @block.tensor
            def _(pe):
                pe.sem_inc(scored, 1)
                with pe.Fori(0, 4) as t:
                    def scores(u):
                        kv, b = UNITS[u]
                        r = slice(kv * A_HD, kv * A_HD + A_HD)
                        pe.wait_ge(masked, t * N + u + 1)
                        nc.tensor.matmul(B[:, u % 4, 0:width(b)], qt[r, b * P:(b + 1) * P],
                                         key[r, max(b - 1, 0) * P:(b + 1) * P], start=True, stop=True).then_inc(scored, 1)

                    def turn(u):
                        kv, b = UNITS[u]
                        pe.wait_ge(normed, t * N + u + 1)
                        if u >= 2:
                            pe.wait_ge(turned_out, t * N + u - 1)
                        for j in range(width(b) // P):
                            last = nc.tensor.transpose(B[:, 4 + u % 2, j * P:(j + 1) * P], pr[:, u % 2, 1 + j * P:1 + (j + 1) * P], ident)
                        last.then_inc(turned, 1)

                    def mix(u):
                        kv, b = UNITS[u]
                        pe.wait_ge(turned_out, t * N + u + 1)
                        if u < 2:
                            pe.wait_ge(o_out, t * 2 + 2)
                        n = width(b) // P
                        for j in range(n):
                            last = nc.tensor.matmul(B[kv * A_HD:kv * A_HD + A_HD, 6 + kv, b * P:(b + 1) * P],
                                                    value[:, b - n + 1 + j, kv * A_HD:kv * A_HD + A_HD],
                                                    pt[:, u % 2, j * P:(j + 1) * P], start=(j == 0), stop=(j == n - 1))
                        last.then_inc(o_done, 1)
                    pe.wait_ge(q_tile, t + 1)
                    scores(0)
                    scores(1)
                    for u in range(N):
                        turn(u)
                        if u + 2 < N:
                            scores(u + 2)
                        if u:
                            mix(u - 1)
                    mix(N - 1)

            @block.vector
            def _(dve):
                dve.sem_inc(masked, 4)
                with dve.Fori(0, 4) as t:
                    def scale(u):
                        dve.wait_ge(exp_done, t * N + u + 1)
                        nc.vector.reciprocal(rinv[:, u:u + 1], total[:, u:u + 1]).then_inc(inv, 1)
                        dve.wait_ge(inv, t * N + u + 1)
                        n = 1 + width(UNITS[u][1])
                        nc.vector.tensor_scalar(pr[:, u % 2, 0:n], pr[:, u % 2, 0:n], rinv[:, u:u + 1], None, ALU.mult
                                                ).then_inc(normed, 1)
                    for u, (kv, b) in enumerate(UNITS):
                        n = width(b)
                        if u >= 2:
                            scale(u - 2)
                        nc.vector.tensor_copy(sc[:, u % 2, 0:1], sinks[:, bass.ds(t + 4 * kv, 1)]).then_inc(sunk, 1)
                        dve.wait_ge(scored, t * N + u + 2)
                        nc.vector.scalar_tensor_tensor(sc[:, u % 2, 1:1 + n], B[:, u % 4, 0:n], SC, band[:, 2 * P - n:2 * P],
                                                       ALU.mult, ALU.add).then_inc(masked, 1)
                        dve.wait_ge(sunk, t * N + u + 1)
                        dve.wait_ge(masked, t * N + u + 5)
                        nc.vector.tensor_reduce(nmax[:, u:u + 1], sc[:, u % 2, 0:1 + n], AX, ALU.max, negate=True
                                                ).then_inc(max_done, 1)
                    scale(N - 2)
                    scale(N - 1)

            @block.scalar
            def _(act):
                act.sem_inc(o_out, 2)
                with act.Fori(0, 4) as t:
                    def copy_turned(u):
                        n = width(UNITS[u][1])
                        act.wait_ge(turned, t * N + u + 1)
                        if u >= 2:
                            act.wait_ge(o_done, t * N + u - 1)
                        nc.scalar.activation(pt[:, u % 2, 0:n], B[:, 4 + u % 2, 0:n], ACT.Copy).then_inc(turned_out, 1)
                    for u, (kv, b) in enumerate(UNITS):
                        n = 1 + width(b)
                        if u >= 2:
                            copy_turned(u - 2)
                        act.wait_ge(max_done, t * N + u + 1)
                        nc.scalar.activation(pr[:, u % 2, 0:n], sc[:, u % 2, 0:n], ACT.Exp, bias=nmax[:, u:u + 1],
                                             accum_out=total[:, u:u + 1]).then_inc(exp_done, 1)
                    copy_turned(N - 2)
                    copy_turned(N - 1)
                    act.wait_ge(o_done, t * N + N)
                    for kv in range(KV_HEADS):
                        r = slice(kv * A_HD, kv * A_HD + A_HD)
                        nc.scalar.activation(out[r, bass.ds(t, 1), :].rearrange("p a n -> p (a n)"), B[r, 6 + kv, :], ACT.Copy
                                             ).then_inc(o_out, 1)


def retention_phase(k, name, q, key, value, gate, out):
    nc = k.nc
    B = k.banks
    SC = P ** -0.5
    (rotated, cosd, sind, pair, outer, inner_done, att_ready, turned, copied, kv_done, state, v_head, o_done, o_out,
     mean_done, centred, squared, var_done, root, inv, normed, final) = k.sems(
        name, "rotated cosd sind pair outer inner_done att_ready turned copied kv_done state v_head o_done o_out "
              "mean_done centred squared var_done root inv normed final")
    with ExitStack() as ctx:
        def sb(n, shape):
            return ctx.enter_context(nc.sbuf_tensor(f"{name}_{n}", shape, F32))
        tc, ts = sb("tc", [P, 2, SEQ]), sb("ts", [P, 2, SEQ])
        qp, kp, qx, kz = (sb(n, [P, SEQ]) for n in ("qp", "kp", "qx", "kz"))
        att, kzt, vh = sb("att", [P, SEQ]), sb("kzt", [P, SEQ]), sb("vh", [P, NB, P])
        S = sb("S", [P, NB, P])
        o, cent, sq, std, eps = sb("o", [P, SEQ]), sb("cent", [P, SEQ]), sb("sq", [P, SEQ]), sb("std", [P, SEQ]), sb("eps", [P, 1])
        cos, sin, ones, ident = k.const("cos"), k.const("sin"), k.const("ones"), k.const("ident")
        blocks = "p (b n) -> p b n"

        def head(a, h):
            return a[:, bass.ds(h, 1), :].rearrange("p a n -> p (a n)")

        def table(name, h):
            a, _ = CONST2_AT[name]
            return k.consts2[:, bass.ds(h * P + a, P)].unsqueeze(1).to_broadcast([P, NB, P])
        with nc.Block() as block:
            @block.tensor
            def _(pe):
                with pe.Fori(0, R_HEADS) as h:
                    pe.wait_ge(final, h + 1)
                    nc.tensor.matmul(B[:, 0, :], k.const("rot"), head(q, h), start=True, stop=True)
                    nc.tensor.matmul(B[:, 1, :], k.const("rot"), head(key, h), start=True, stop=True).then_inc(rotated, 1)
                    pe.wait_ge(pair, h * 2 + 2)
                    for b in range(NB):
                        s = slice(b * P, (b + 1) * P)
                        last = nc.tensor.matmul(B[:, 2, s], kp[:, s], qp[:, s], start=True, stop=True)
                    last.then_inc(inner_done, 1)
                    pe.wait_ge(outer, h * 2 + 2)
                    for b in range(NB):
                        s = slice(b * P, (b + 1) * P)
                        last = nc.tensor.transpose(B[:, 3, s], kz[:, s], ident)
                    last.then_inc(turned, 1)
                    pe.wait_ge(copied, h + 1)
                    pe.wait_ge(v_head, h + 1)
                    for b in range(NB - 1):
                        s = slice(b * P, (b + 1) * P)
                        last = nc.tensor.matmul(B[:, 4, s], kzt[:, s], vh[:, b, :], start=True, stop=True)
                    last.then_inc(kv_done, 1)
                    pe.wait_ge(att_ready, h + 1)
                    for b in range(NB):
                        s = slice(b * P, (b + 1) * P)
                        last = nc.tensor.matmul(B[:, 5, s], vh[:, b, :], att[:, s], start=True, stop=(b == 0))
                        if b:
                            pe.wait_ge(state, h * 3 + b)
                            last = nc.tensor.matmul(B[:, 5, s], S[:, b, :], qx[:, s], start=False, stop=True)
                    last.then_inc(o_done, 1)
                    pe.wait_ge(o_out, h + 1)
                    nc.tensor.matmul(B[:, 6, :], ones, o[:], start=True, stop=True).then_inc(mean_done, 1)
                    pe.wait_ge(squared, h + 1)
                    nc.tensor.matmul(B[:, 7, :], ones, sq[:], start=True, stop=True).then_inc(var_done, 1)

            @block.gpsimd
            def _(pool):
                with pool.Fori(0, R_HEADS) as h:
                    pool.wait_ge(final, h + 1)
                    nc.gpsimd.tensor_copy(vh[:], value[:, :, bass.ds(h * P + P, P)]).then_inc(v_head, 1)

            @block.scalar
            def _(act):
                with act.Fori(0, R_HEADS) as h:
                    act.wait_ge(turned, h + 1)
                    nc.scalar.activation(kzt[:], B[:, 3, :], ACT.Copy).then_inc(copied, 1)
                    act.wait_ge(o_done, h + 1)
                    nc.scalar.activation(o[:], B[:, 5, :], ACT.Copy).then_inc(o_out, 1)
                    act.wait_ge(centred, h + 1)
                    nc.scalar.activation(sq[:], cent[:], ACT.Square).then_inc(squared, 1)
                    act.wait_ge(var_done, h + 1)
                    nc.scalar.activation(std[:], B[:, 7, :], ACT.Sqrt, bias=eps[:, 0:1], scale=1.0 / P).then_inc(root, 1)

            @block.vector
            def _(dve):
                nc.vector.memset(eps[:], EPS).then_inc(final, 1)
                with dve.Fori(0, R_HEADS) as h:
                    for i, (x, sc) in enumerate(((q, 1.0), (key, SC))):
                        nc.vector.scalar_tensor_tensor(tc[:, i, :], head(x, h), sc, cos, ALU.mult, ALU.mult).then_inc(cosd, 1)
                    dve.wait_ge(rotated, h + 1)
                    for i, sc in enumerate((1.0, SC)):
                        nc.vector.scalar_tensor_tensor(ts[:, i, :], B[:, i, :], sc, sin, ALU.mult, ALU.mult).then_inc(sind, 1)
                    dve.wait_ge(cosd, h * 2 + 2)
                    dve.wait_ge(sind, h * 2 + 2)
                    for i, to in enumerate((qp, kp)):
                        nc.vector.tensor_tensor(to[:], tc[:, i, :], ts[:, i, :], ALU.add).then_inc(pair, 1)
                    dve.wait_ge(pair, h * 2 + 2)
                    for to, x, by in ((kz, kp, "zeta"), (qx, qp, "xi")):
                        nc.vector.tensor_tensor(to[:].rearrange(blocks, b=NB), x[:].rearrange(blocks, b=NB), table(by, h), ALU.mult
                                                ).then_inc(outer, 1)
                    dve.wait_ge(inner_done, h + 1)
                    nc.vector.tensor_tensor(att[:].rearrange(blocks, b=NB), B[:, 2, :].rearrange(blocks, b=NB), table("dintra", h),
                                            ALU.mult).then_inc(att_ready, 1)
                    dve.wait_ge(kv_done, h + 1)
                    nc.vector.tensor_copy(S[:, 1, :], B[:, 4, 0:P]).then_inc(state, 1)
                    for b in (2, 3):
                        dve.wait_ge(state, h * 3 + b - 1)
                        decay = k.consts2[:, bass.ds(h + CONST2_AT["decay"][0], 1)]
                        nc.vector.scalar_tensor_tensor(S[:, b, :], S[:, b - 1, :], decay, B[:, 4, (b - 1) * P:b * P],
                                                       ALU.mult, ALU.add).then_inc(state, 1)
                    dve.wait_ge(mean_done, h + 1)
                    nc.vector.scalar_tensor_tensor(cent[:], B[:, 6, :], -1.0 / P, o[:], ALU.mult, ALU.add).then_inc(centred, 1)
                    dve.wait_ge(root, h + 1)
                    nc.vector.reciprocal(std[:], std[:]).then_inc(inv, 1)
                    dve.wait_ge(inv, h + 1)
                    nc.vector.tensor_tensor(cent[:], cent[:], std[:], ALU.mult).then_inc(normed, 1)
                    dve.wait_ge(normed, h + 1)
                    nc.vector.tensor_tensor(head(out, h), cent[:], head(gate, h), ALU.mult).then_inc(final, 1)


def gated_conv_phase(k, name, x, w_dram, taps, y):
    nc = k.nc
    B = k.banks
    product, tap, gelu, y_full, y_high, y_done, high_done, low_done = k.sems(
        name, "product tap gelu y_full y_high y_done high_done low_done")
    w_in = k.sems(name, "w_in0 w_in1 w_in2 w_in3")
    with ExitStack() as ctx:
        def sb(n, shape, dt=F32):
            return ctx.enter_context(nc.sbuf_tensor(f"{name}_{n}", shape, dt))
        raw = sb("raw", [P, RING, KD * P])
        w = [sb(n, [P, 2, KD * P], F32R) for n in ("high", "low")]
        conv, ge = sb("conv", [P, RING, SEQ]), sb("ge", [P, 2, SEQ])
        with nc.Block() as block:
            @block.sync
            def _(sp):
                with sp.Fori(0, 2 * FT // RING) as g:
                    for r in range(RING):
                        sp.wait_ge(low_done, g * RING + (r + 1))
                        sp.dma_start(raw[:, r, :], w_dram[bass.ds(g * RING + r, 1)].rearrange("a p n -> (a p) n")).then_inc(w_in[r], 16)

            @block.tensor
            def _(pe):
                pe.sem_inc(product, 2)
                with pe.Fori(0, 2 * FT // RING) as g:
                    for r in range(RING):
                        pe.wait_ge(low_done, g * RING + (r + 1 + RING))
                        pe.wait_ge(tap, g * 3 * RING + (3 * r + 3))
                        for c in range(KD):
                            last = product3(nc, B[:, r, :], [a[:, r % 2, c * P:(c + 1) * P] for a in w], [a[:, c, :] for a in x],
                                            c == 0, c == KD - 1)
                        last.then_inc(product, 1)

            @block.vector
            def _(dve):
                dve.sem_inc(tap, 3 * RING)
                dve.sem_inc(y_done, 2)
                with dve.Fori(0, 2 * FT // RING) as g:
                    for r in range(RING):
                        dve.wait_ge(product, g * RING + (r + 3))
                        dve.wait_ge(y_done, g * 2 + (r // 2 + 1))
                        to, a = conv[:, r, :], B[:, r, :]

                        def weight(j):
                            return taps[:, bass.ds(g * RING + r, 1), j:j + 1].rearrange("p a n -> p (a n)")
                        nc.vector.tensor_scalar(to, a, weight(2), weight(3), ALU.mult, ALU.add).then_inc(tap, 1)
                        for s in (1, 2):
                            dve.wait_ge(tap, g * 3 * RING + (3 * r + s + 3 * RING))
                            nc.vector.scalar_tensor_tensor(to[:, s:SEQ], a[:, 0:SEQ - s], weight(2 - s), to[:, s:SEQ],
                                                           ALU.mult, ALU.add).then_inc(tap, 1)
                        if r % 2 == 1:
                            dve.wait_ge(gelu, g * 2 + (r // 2 + 1))
                            dve.wait_ge(tap, g * 3 * RING + (3 * r + 3 + 3 * RING))
                            nc.vector.tensor_tensor(conv[:, r, :], ge[:, r // 2, :], conv[:, r, :], ALU.mult).then_inc(y_full, 1)
                            dve.wait_ge(y_high, g * 2 + (r // 2 + 1))
                            high, low = (a[:, bass.ds(g * 2 + r // 2, 1), :].rearrange("p a n -> p (a n)") for a in y)
                            nc.vector.tensor_tensor(low, conv[:, r, :], high.bitcast(F32), ALU.subtract).then_inc(y_done, 1)

            @block.gpsimd
            def _(pool):
                pool.sem_inc(low_done, RING)
                with pool.Fori(0, 2 * FT // RING) as g:
                    for r in range(RING):
                        pool.wait_ge(high_done, g * RING + (r + 1))
                        nc.gpsimd.tensor_tensor(w[1][:, r % 2, :], raw[:, r, :], w[0][:, r % 2, :].bitcast(F32), ALU.subtract
                                                ).then_inc(low_done, 1)

            @block.scalar
            def _(act):
                def split(g, r):
                    act.wait_ge(w_in[r], g * 16 + 16)
                    act.wait_ge(product, g * RING + (r + 1))
                    nc.scalar.activation(w[0][:, r % 2, :], raw[:, r, :], ACT.Copy).then_inc(high_done, 1)
                def gelu_part(g, f):
                    act.wait_ge(tap, g * 3 * RING + (6 * f + 3 + 3 * RING))
                    act.wait_ge(y_done, g * 2 + (f + 1))
                    nc.scalar.activation(ge[:, f, :], conv[:, 2 * f, :], ACT.Gelu_apprx_tanh).then_inc(gelu, 1)

                def high_part(g, f):
                    act.wait_ge(y_full, g * 2 + (f + 1))
                    nc.scalar.activation(y[0][:, bass.ds(g * 2 + f, 1), :].rearrange("p a n -> p (a n)"), conv[:, 2 * f + 1, :],
                                         ACT.Copy).then_inc(y_high, 1)

                def turn(g, first):
                    for r in range(RING):
                        split(g, r)
                        if r < 2 and first:
                            continue
                        part = high_part if r % 2 else gelu_part
                        part(g, 0) if r >= 2 else part(g - 1, 1)
                turn(0, True)
                with act.Fori(1, 2 * FT // RING) as g:
                    turn(g, False)
                gelu_part(2 * FT // RING - 1, 1)
                high_part(2 * FT // RING - 1, 1)


def tiled(w, width=P):
    kk, m = w.shape
    return np.ascontiguousarray(w.reshape(kk // P, P, m // width, width).transpose(2, 1, 0, 3)).reshape(m // width, P, -1)


def rows(w):
    return np.ascontiguousarray(w.reshape(-1, P, w.shape[1]).transpose(1, 0, 2))


def column(v):
    return np.ascontiguousarray(v.reshape(-1, P).T)


def layout(a):
    i = {}
    h0 = np.concatenate([a["meta_tokens"], a["x"][0]], 0)
    i["h0"] = rows(np.ascontiguousarray(h0.T))
    i["consts"], i["consts2"] = constants()
    w = a["w_in"][0]
    cut = np.cumsum([512, 512, 1024, 1024, 16, 2048, 3072, 32, 1024, 1024])
    q, kk, v, g_out, low, z, xbc, dt, ga, gb = np.split(w, cut[:-1], axis=1)
    i["wq"], i["wk"], i["wv"] = tiled(q), tiled(kk), tiled(v, GLA_DV)
    i["w_gout"], i["w_z"], i["w_ga"], i["w_gb"] = tiled(g_out), tiled(z), tiled(ga), tiled(gb)
    i["w_low"], i["w_dt"] = rows(low), rows(dt)
    i["gate_w"] = np.concatenate([a["gla_w_gate2"][0], a["gla_b_gate"]], 0)
    c0 = SSD_GROUPS * 512
    group = [np.concatenate([np.arange(g * 512, (g + 1) * 512), c0 + np.arange(g * P, (g + 1) * P),
                             c0 + 512 + np.arange(g * P, (g + 1) * P)]) for g in range(SSD_GROUPS)]
    order = np.concatenate(group)
    i["w_xbc"] = tiled(xbc[:, order])
    taps = np.concatenate([a["ssd_conv_w"][0], a["ssd_conv_b"]], 0)[:, order]
    i["conv"] = np.ascontiguousarray(taps.reshape(5, SSD_GROUPS, 6, P).transpose(3, 1, 2, 0))
    every = lambda v: np.ascontiguousarray(np.broadcast_to(v, (P, v.shape[-1])))
    i["dt_bias"], i["a_log"] = every(a["ssd_dt_bias"]), every(a["ssd_a_log"])
    i["skip"] = column(np.repeat(a["ssd_d"][0], SSD_HD))
    i["ssd_norm"] = column(a["ssd_norm_w"][0])
    i["w_up_gla"], i["w_up_ssd"], i["w_out"] = tiled(a["w_up_gla"][0]), tiled(a["w_up_ssd"][0]), tiled(a["w_out"][0])
    i["ln_ffn"], i["ln_final"] = column(a["ln_ffn_w"][0]), column(a["ln_final_w"])
    i["w_q"] = tiled(a["peer_w_q"][0])
    i["keys"] = np.ascontiguousarray(a["peer_sub_keys"][0].reshape(2 * PEER_HEADS, KEYS, P).transpose(2, 0, 1))
    i["u"], i["v"] = tiled(a["peer_u"][0].T), a["peer_v"][0]
    w2 = a["w_in_2"][0]
    qa, ka, va, qr, kr, vr, gr = np.split(w2, np.cumsum([512, 128, 128, 512, 512, 512]), axis=1)
    pairs = np.concatenate([np.concatenate([np.arange(t * 64, t * 64 + 64), np.arange((t + 4) * 64, (t + 4) * 64 + 64)])
                            for t in range(4)])
    i["w_qk2"] = tiled(np.concatenate([qa[:, pairs], qr, kr], 1))
    i["w_gr"] = tiled(gr)
    i["w_kv2"] = rows(np.concatenate([ka, va, vr], 1))
    i["sinks"] = every(a["attn_sinks_2"])
    i["w_out2"] = tiled(np.concatenate([a["w_out_2"][0][:512][pairs], a["w_out_2"][0][512:]], 0))
    for n in ("mix_pre_norm_2", "mix_post_norm_2", "ffn_pre_norm_2", "ffn_post_norm_2"):
        i[n] = column(a[n][0])
    both = np.concatenate([np.concatenate([np.arange(f * P, f * P + P), D_FF + np.arange(f * P, f * P + P)]) for f in range(FT)])
    i["w_up2"], i["w_down2"] = tiled(a["w_up_2"][0][:, both]), tiled(a["w_down_2"][0])
    taps2 = np.concatenate([a["conv_w_2"][0], a["conv_b_2"]], 0)[:, both]
    i["taps2"] = np.ascontiguousarray(taps2.reshape(4, 2 * FT, P).transpose(2, 1, 0))
    i["ln_mix"] = column(a["ln_mix_w"][0])
    i["gla_norm"] = column(np.tile(a["gla_norm_w"][0], GLA_HEADS))
    return i


def pair_of(nc, ctx, name, tiles, n):
    return [ctx.enter_context(nc.sbuf_tensor(f"{name}_{part}", [P, tiles, n], F32R)) for part in ("high", "low")]


def first_mixer(k, d, h):
    nc = k.nc
    with ExitStack() as ctx:
        def sb(n, shape):
            return ctx.enter_context(nc.sbuf_tensor(n, shape, F32))
        mixed = sb("mixed", [P, KD, L])
        hn = pair_of(nc, ctx, "hn", KD, L)
        ln_mix, gla_norm, ssd_norm = sb("ln_mix", [P, KD]), sb("gla_norm", [P, KD]), sb("ssd_norm", [P, 2 * KD])
        gate_w, low = sb("gate_w", [GATE_RANK + 1, 512]), sb("low", [GATE_RANK + 1, L])
        with ExitStack() as scan:
            def sb2(n, shape):
                return scan.enter_context(nc.sbuf_tensor(n, shape, F32))
            dt = sb2("dt", [P, NB + 1, SSD_HEADS])
            acum, e_acum, to_end = (sb2(n, [P, NB + 1, SSD_HEADS]) for n in ("acum", "e_acum", "to_end"))
            e_total, e_total_m = sb2("e_total", [P, 2, NB, SSD_HEADS]), sb2("e_total_m", [P, SSD_HEADS])
            dt_bias, a_log = sb2("dt_bias", [P, SSD_HEADS]), sb2("a_log", [P, SSD_HEADS])
            conv, skip = sb2("conv", [P, SSD_GROUPS, 6, 5]), sb2("skip", [P, 2 * KD])
            with ExitStack() as inner:
                hn_full = inner.enter_context(nc.sbuf_tensor("hn_full", [P, KD, L], F32))
                w_low = inner.enter_context(nc.sbuf_tensor("w_low", [P, KD, GATE_RANK], F32))
                w_dt = inner.enter_context(nc.sbuf_tensor("w_dt", [P, KD, SSD_HEADS], F32))
                load_phase(k, "load1", [(h[:], d["h0"]), (k.consts[:], d["consts"])] + [
                    (t[:], d[n]) for t, n in ((ln_mix, "ln_mix"), (gla_norm, "gla_norm"), (ssd_norm, "ssd_norm"), (w_low, "w_low"),
                                              (w_dt, "w_dt"), (gate_w, "gate_w"), (dt_bias, "dt_bias"), (a_log, "a_log"),
                                              (conv, "conv"), (skip, "skip"))])
                norm_phase(k, "ln1", h, hn_full, ln_mix, 1, KD, L)
                small_products_phase(k, "small", hn_full, w_low, low, w_dt, dt)
                split_phase(k, "ln1_split", hn_full, hn, KD)
            y = sb2("y", [P, 2 * KD, L])
            ssd_prep_phase(k, "prep", dt, dt_bias, a_log, acum, e_acum, to_end, e_total, e_total_m)
            ssd_phase(k, "ssd", hn, d["w_xbc"], conv, skip, dt, acum, e_acum, to_end, e_total, e_total_m, y, mixed)
            product_phase(k, "z", d["w_z"], hn, KD, 2 * KD, L, "times_silu", dst=y)
            norm_phase(k, "ssd_n", y, y, ssd_norm, SSD_GROUPS, 4, L)
            y_pair = pair_of(nc, scan, "y", KD, L)
            for half in range(2):
                split_phase(k, f"y_split{half}", y[:, half * KD:(half + 1) * KD, :], y_pair, KD)
                product_phase(k, f"ups{half}", d["w_up_ssd"], y_pair, KD, KD, L, "add" if half else "copy", dst=mixed, at=half * D)
            product_phase(k, "gb", d["w_gb"], hn, KD, KD, L, "times_gate", dst=mixed)
        k.reset_sems()
        o = sb("o", [P, KD, L])
        gla_phase(k, "gla", hn, low, gate_w, d["wq"], d["wk"], d["wv"], o)
        norm_phase(k, "gla_n", o, o, gla_norm, GLA_HEADS, 2, L)
        product_phase(k, "gout", d["w_gout"], hn, KD, KD, L, "times_silu", dst=o)
        pair = pair_of(nc, ctx, "mixer", KD, L)
        split_phase(k, "o_split", o, pair, KD)
        product_phase(k, "upg", d["w_up_gla"], pair, KD, KD, L, "copy", dst=o)
        product_phase(k, "ga", d["w_ga"], hn, KD, KD, L, "gate_add", dst=mixed, other=o)
        split_phase(k, "mixed_split", mixed, pair, KD)
        product_phase(k, "out1", d["w_out"], pair, KD, KD, L, "add", dst=h)


def first_experts(k, d, hx):
    nc = k.nc
    with ExitStack() as ctx:
        def sb(n, shape):
            return ctx.enter_context(nc.sbuf_tensor(n, shape, F32))
        hb, chosen = pair_of(nc, ctx, "hb", KD, SEQ), sb("chosen", [P, 3, SEQ])
        ln_final = sb("ln_final", [P, KD])
        with ExitStack() as inner:
            ln_ffn = inner.enter_context(nc.sbuf_tensor("ln_ffn", [P, KD], F32))
            q = inner.enter_context(nc.sbuf_tensor("peer_q", [P, 2 * PEER_HEADS, SEQ], F32))
            keys = inner.enter_context(nc.sbuf_tensor("keys", [P, 2 * PEER_HEADS, KEYS], F32))
            load_phase(k, "load2", [(ln_ffn[:], d["ln_ffn"]), (ln_final[:], d["ln_final"]), (keys[:], d["keys"])])
            norm_phase(k, "ln2", hx, q, ln_ffn, 1, KD, SEQ)
            split_phase(k, "hb_split", q, hb, KD)
            product_phase(k, "pq", d["w_q"], hb, KD, 2 * PEER_HEADS, SEQ, "copy", dst=q)
            route_phase(k, "route", q, keys, chosen)
        w_dram = nc.dram_tensor("expert_weights", (KEYS, KEYS, SEQ), F32, kind="Internal").ap()
        spread_phase(k, "spread", chosen, w_dram)
        expert_phase(k, "experts", hb, d["u"], d["v"], w_dram, hx)
        norm_phase(k, "ln3", hx, hx, ln_final, 1, KD, SEQ)


def second_block(k, d, x2):
    nc = k.nc
    with ExitStack() as ctx:
        def sb(n, shape):
            return ctx.enter_context(nc.sbuf_tensor(n, shape, F32))
        x3 = sb("x3", [P, KD, SEQ])
        norms = [sb(f"norm{i}", [P, KD]) for i in range(4)]
        taps = sb("taps", [P, 2 * FT, 4])
        with ExitStack() as inner:
            def sb2(n, shape):
                return inner.enter_context(nc.sbuf_tensor(n, shape, F32))
            k.consts2, sinks = sb2("consts2", [P, CONST2_N]), sb2("sinks", [P, A_HEADS])
            pair = pair_of(nc, inner, "mixer2", KD, SEQ)
            mix = sb2("mix2", [P, KD, SEQ])
            qk = sb2("qk", [P, 12, SEQ])
            gate = sb2("gate", [P, R_HEADS, SEQ])
            key, value = sb2("key", [P, SEQ]), sb2("value", [P, NB, 5 * P])
            load_phase(k, "load3", [(norms[j][:], d[n]) for j, n in enumerate(
                ("mix_pre_norm_2", "mix_post_norm_2", "ffn_pre_norm_2", "ffn_post_norm_2"))] + [
                (k.consts2[:], d["consts2"]), (sinks[:], d["sinks"]), (taps[:], d["taps2"])])
            norm_phase(k, "ln4", x2, mix, norms[0], 1, KD, SEQ)
            split_phase(k, "ln4_split", mix, pair, KD)
            product_phase(k, "qk2", d["w_qk2"], pair, KD, 12, SEQ, "copy", dst=qk)
            product_phase(k, "gr", d["w_gr"], pair, KD, R_HEADS, SEQ, "silu", dst=gate)
            keys_values_phase(k, "kv2", pair, d["w_kv2"], key, value)
            attention_phase(k, "attn", qk, key, value, sinks, mix)
            retention_phase(k, "ret", qk[:, 4:8, :], qk[:, 8:12, :], value, gate, mix[:, 4:8, :])
            split_phase(k, "mix_split", mix, pair, KD)
            product_phase(k, "out2", d["w_out2"], pair, KD, KD, SEQ, "copy", dst=x3)
        norm_phase(k, "ln5", x3, x3, norms[1], 1, KD, SEQ, add=x2)
        y_pair = pair_of(nc, ctx, "y_ff", FT, SEQ)
        with ExitStack() as inner:
            pair = pair_of(nc, inner, "ffn", KD, SEQ)
            norm_phase(k, "ln6", x3, x2, norms[2], 1, KD, SEQ)
            split_phase(k, "ln6_split", x2, pair, KD)
            gated_conv_phase(k, "up", pair, d["w_up2"], taps, y_pair)
        product_phase(k, "down", d["w_down2"], y_pair, FT, KD, SEQ, "copy", dst=x2)
        norm_phase(k, "ln7", x2, x2, norms[3], 1, KD, SEQ, add=x3)


def program(nc, d, out):
    with ExitStack() as ctx:
        k = Core(nc, ctx)
        h = ctx.enter_context(nc.sbuf_tensor("h", [P, KD, L], F32))
        first_mixer(k, d, h)
        k.reset_sems()
        x2 = h[:, :, META:L]
        first_experts(k, d, x2)
        k.reset_sems()
        second_block(k, d, x2)
        store_phase(k, "store", out, x2)


def kernel(**inputs):
    import concourse.bacc as bacc
    from concourse.bass_utils import run_bass_kernel_spmd as run
    nc = bacc.Bacc("TRN2", target_bir_lowering=False, num_devices=1)
    arrays = layout({n: np.asarray(v) for n, v in inputs.items()})
    d = {n: nc.dram_tensor(f"in_{n}", v.shape, mybir.dt.from_np(v.dtype), kind="ExternalInput").ap() for n, v in arrays.items()}
    out = nc.dram_tensor("out_dram", (P, KD, SEQ), F32, kind="ExternalOutput").ap()
    program(nc, d, out)
    r = run(nc, [{f"in_{n}": v for n, v in arrays.items()}], core_ids=[0])
    y = r.results[0]["out_dram"]
    return np.ascontiguousarray(y.transpose(2, 1, 0)).reshape(1, SEQ, D)
```

```python
from contextlib import ExitStack

import numpy as np
import concourse.bass as bass
from concourse import mybir

F32 = mybir.dt.float32
F32R = mybir.dt.float32r
U32 = mybir.dt.uint32
ALU = mybir.AluOpType
ACT = mybir.ActivationFunctionType
AX = mybir.AxisListType.X

P = 128
D = 1024
KD = D // P
SEQ = 512
META = 16
L = META + SEQ
NB = SEQ // P
CH = 64
EPS = 1e-6
RING = 4

GLA_HEADS, GLA_DK, GLA_DV, GATE_RANK = 4, 128, 256, 16
SSD_GROUPS, SSD_HPG, SSD_HD = 4, 8, 64
SSD_HEADS = SSD_GROUPS * SSD_HPG
PEER_HEADS, KEYS, TOPK = 8, 128, 16
GROUP = 8
A_HEADS, A_HD, KV_HEADS = 8, 64, 2
R_HEADS = 4
D_FF = 2816
FT = D_FF // P

CONST_W = {"ident": 128, "ones": 128, "tri": 128, "tri16": 128, "same": 128, "half0": 128, "half1": 128, "diag64": 64, "iota": 128, "iota16": 16,
           "causal": 256}
CONST2_W = {"decay": R_HEADS, "band": 256, "rot": 128, "dintra": 512, "xi": 512, "zeta": 512, "cos": 512, "sin": 512}


def places(widths):
    at, out = 0, {}
    for n, w in widths.items():
        out[n] = (at, at + w)
        at += w
    return out


CONST_AT, CONST2_AT = places(CONST_W), places(CONST2_W)
CONST_N, CONST2_N = sum(CONST_W.values()), sum(CONST2_W.values())


def constants():
    c = {}
    i = np.arange(P)
    chunk = i // CH
    same = (chunk[:, None] == chunk[None, :]).astype(np.float32)
    c["ident"] = np.eye(P)
    c["ones"] = np.ones((P, P))
    c["half0"] = np.broadcast_to(chunk[:, None] == 0, (P, P))
    c["half1"] = np.broadcast_to(chunk[:, None] == 1, (P, P))
    c["tri"] = same * (i[:, None] <= i[None, :])
    c["tri16"] = c["tri"] / 16.0
    c["same"] = same
    c["diag64"] = (i[:, None] % CH == np.arange(CH)[None, :])
    c["iota"] = np.broadcast_to(i[None, :], (P, P))
    c["iota16"] = np.broadcast_to(np.arange(16)[None, :], (P, 16))
    c["causal"] = np.tile(i[:, None] % CH <= np.arange(CH)[None, :], (1, NB))
    rel = (i[:, None] + P) - np.arange(2 * P)[None, :]
    c["band"] = np.where((rel >= 0) & (rel < P), 0.0, -1e30)
    rot = np.zeros((P, P))
    rot[i[1::2], i[0::2]] = -1.0
    rot[i[0::2], i[1::2]] = 1.0
    c["rot"] = rot
    f = np.float32
    log_gamma = np.log(f(1.0) - np.power(f(2.0), f(-5.0) - np.arange(R_HEADS, dtype=f)))
    r = (i[None, :] - i[:, None]).astype(f)
    c["dintra"] = np.stack([np.where(r >= 0, np.exp(g * np.maximum(r, 0)), 0) for g in log_gamma], 1).reshape(P, -1)
    c["xi"] = np.stack([np.broadcast_to(np.exp(g * (i + f(1))), (P, P)) for g in log_gamma], 1).reshape(P, -1)
    c["zeta"] = np.stack([np.broadcast_to(np.exp(g * (P - f(1) - i)), (P, P)) for g in log_gamma], 1).reshape(P, -1)
    c["decay"] = np.broadcast_to(np.exp(log_gamma * f(P)), (P, R_HEADS))
    angle = np.repeat(f(1.0) / np.power(f(10000.0), np.linspace(0, 1, P // 2, dtype=f)), 2)
    arg = (np.arange(SEQ, dtype=f)[None, :] * angle[:, None]).astype(f)
    c["cos"], c["sin"] = np.cos(arg), np.sin(arg)
    return [np.ascontiguousarray(np.concatenate([np.asarray(c[n], np.float32).reshape(P, ws[n]) for n in ws], 1))
            for ws in (CONST_W, CONST2_W)]


class Core:

    def __init__(self, nc, ctx):
        self.nc, self.ctx = nc, ctx
        self.banks = ctx.enter_context(nc.psum_tensor("banks", [P, 8, 512], F32))
        self.consts = ctx.enter_context(nc.sbuf_tensor("consts", [P, CONST_N], F32))
        self.consts2 = None
        self.in_use = []

    def sems(self, phase, names):
        self.in_use += [self.nc.alloc_semaphore(name=f"{phase}_{n}") for n in names.split()]
        return self.in_use[-len(names.split()):]

    def reset_sems(self):
        with self.nc.Block() as block:
            @block.sync
            def _(sp):
                for s in self.in_use:
                    sp.sem_clear(s)
        for s in self.in_use:
            self.nc.release_semaphore(s)
        self.in_use = []

    def const(self, name):
        if name in CONST2_AT:
            a, b = CONST2_AT[name]
            return self.consts2[:, a:b]
        a, b = CONST_AT[name]
        return self.consts[:, a:b]


def load_phase(k, name, pairs):
    (loaded,) = k.sems(name, "loaded")
    with k.nc.Block() as block:
        @block.sync
        def _(sp):
            for to, source in pairs:
                sp.dma_start(to, source).then_inc(loaded, 16)
            sp.wait_ge(loaded, 16 * len(pairs))


def store_phase(k, name, to, source):
    (stored,) = k.sems(name, "stored")
    with k.nc.Block() as block:
        @block.sync
        def _(sp):
            sp.dma_start(to, source).then_inc(stored, 16)
            sp.wait_ge(stored, 16)


def norm_phase(k, name, src, dst, weight, groups, tiles, n, add=None, mean_of=None):
    nc = k.nc
    halves = 1 if n <= 512 else 2
    w = n // halves
    squared, square_used, summed, root, recip, scaled = k.sems(name, "squared square_used summed root recip scaled")
    with ExitStack() as ctx:
        sq = ctx.enter_context(nc.sbuf_tensor(f"{name}_sq", [P, 2, n], F32))
        std = ctx.enter_context(nc.sbuf_tensor(f"{name}_std", [P, 2, n], F32))
        rstd = ctx.enter_context(nc.sbuf_tensor(f"{name}_rstd", [P, 2, n], F32))
        eps = ctx.enter_context(nc.sbuf_tensor(f"{name}_eps", [P, 1], F32))
        ones = k.const("ones")
        inv = 1.0 / (tiles * P)
        with nc.Block() as block:
            @block.scalar
            def _(act):
                act.wait_ge(scaled, 1)
                for g in range(groups):
                    for t in range(tiles):
                        m = g * tiles + t
                        if m >= 2:
                            act.wait_ge(square_used, m - 1)
                        nc.scalar.activation(sq[:, m % 2, :], src[:, m, :], ACT.Square).then_inc(squared, 1)
                    act.wait_ge(square_used, (g + 1) * tiles)
                    if g >= 2:
                        act.wait_ge(recip, g - 1)
                    nc.scalar.activation(std[:, g % 2, :].rearrange("p (h n) -> p h n", h=halves),
                                         k.banks[:, 2 * (g % 2):2 * (g % 2) + halves, 0:w],
                                         ACT.Sqrt, bias=eps[:, 0:1], scale=inv).then_inc(root, 1)

            @block.tensor
            def _(pe):
                for g in range(groups):
                    for t in range(tiles):
                        m = g * tiles + t
                        pe.wait_ge(squared, m + 1)
                        if t == 0 and g >= 2:
                            pe.wait_ge(root, g - 1)
                        for h in range(halves):
                            last = nc.tensor.matmul(k.banks[:, 2 * (g % 2) + h, 0:w], ones,
                                                    sq[:, m % 2, h * w:(h + 1) * w],
                                                    start=(t == 0), stop=(t == tiles - 1))
                        last.then_inc(square_used, 1)

            @block.vector
            def _(dve):
                nc.vector.memset(eps[:], EPS).then_inc(scaled, 1)
                done = 1
                for g in range(groups):
                    dve.wait_ge(root, g + 1)
                    if g >= 2:
                        dve.wait_ge(scaled, done)
                    nc.vector.reciprocal(rstd[:, g % 2, :], std[:, g % 2, :]).then_inc(recip, 1)
                    dve.wait_ge(recip, g + 1)
                    for t in range(tiles):
                        m = g * tiles + t
                        if weight is None:
                            nc.vector.tensor_tensor(dst[:, m, :], src[:, m, :], rstd[:, g % 2, :],
                                                    ALU.mult).then_inc(scaled, 1)
                        else:
                            nc.vector.scalar_tensor_tensor(dst[:, m, :], src[:, m, :], weight[:, m:m + 1],
                                                           rstd[:, g % 2, :], ALU.mult, ALU.mult).then_inc(scaled, 1)
                        done += 1
                if add is not None:
                    for m in range(groups * tiles):
                        dve.wait_ge(scaled, 2 + m)
                        nc.vector.tensor_tensor(dst[:, m, :], dst[:, m, :], add[:, m, :], ALU.add).then_inc(summed, 1)


def product3(nc, to, w, x, start, stop):
    nc.tensor.matmul(to, w[0], x[0], start=start, stop=False)
    nc.tensor.matmul(to, w[0], x[1], start=False, stop=False)
    return nc.tensor.matmul(to, w[1], x[0], start=False, stop=stop)


def split_phase(k, name, src, pair, tiles):
    nc = k.nc
    high_done, low_done = k.sems(name, "high_done low_done")
    high, low = pair
    with nc.Block() as block:
        @block.scalar
        def _(act):
            for t in range(tiles):
                nc.scalar.activation(high[:, t, :], src[:, t, :], ACT.Copy).then_inc(high_done, 1)

        @block.vector
        def _(dve):
            for t in range(tiles):
                dve.wait_ge(high_done, t + 1)
                nc.vector.tensor_tensor(low[:, t, :], src[:, t, :], high[:, t, :].bitcast(F32), ALU.subtract).then_inc(low_done, 1)


def product_phase(k, name, w_dram, x, kt, mt, n, finish, dst=None, other=None, at=0, source=None):
    nc = k.nc
    halves = 1 if n <= 512 else 2
    w = n // halves
    U = RING
    assert mt % U == 0
    raws = RING if kt <= KD else 2
    per = 4 if halves == 1 else 2
    product, psum_read, gate_out, written, high_done, low_done = k.sems(
        name, "product psum_read gate_out written high_done low_done")
    x_high, x_low, x_low_pool = k.sems(name, "x_high x_low x_low_pool") if source is not None else (None,) * 3
    w_in = k.sems(name, " ".join(f"w_in{r}" for r in range(raws)))
    gated = finish in ("times_silu", "times_gate", "gate_add")
    func = {"silu": ACT.Silu, "times_silu": ACT.Silu, "times_gate": ACT.Sigmoid, "gate_add": ACT.Sigmoid}.get(finish, ACT.Copy)
    with ExitStack() as ctx:
        def sb(nm, shape, dt=F32):
            return ctx.enter_context(nc.sbuf_tensor(f"{name}_{nm}", shape, dt))
        raw = sb("raw", [P, raws, kt * P])
        high, low = sb("high", [P, 2, kt * P], F32R), sb("low", [P, 2, kt * P], F32R)
        temp = sb("t", [P, 2, n]) if gated else None
        temp2 = sb("t2", [P, n]) if finish == "gate_add" else None

        def psum(r):
            return k.banks[:, halves * (r % per):halves * (r % per) + halves, 0:w]

        def tile(a, m):
            return a[:, bass.ds(m, 1), :].rearrange("p a (h n) -> p (a h) n", h=halves)

        def flat(a, m):
            return a[:, bass.ds(m, 1), :].rearrange("p a n -> p (a n)")

        def split_source(engine, op, tiles, done):
            if source is not None:
                for t in tiles:
                    engine.wait_ge(x_high, t + 1)
                    op(x[1][:, t, :], source[:, t, :], x[0][:, t, :].bitcast(F32), ALU.subtract).then_inc(done, 1)

        with nc.Block() as block:
            @block.gpsimd
            def _(pool):
                split_source(pool, nc.gpsimd.tensor_tensor, range(1, kt, 3), x_low_pool)

            @block.sync
            def _(sp):
                with sp.Fori(0, mt // U) as g:
                    for r in range(U):
                        sp.wait_ge(low_done, g * U + (r + 1))
                        sp.dma_start(raw[:, r % raws, :],
                                     w_dram[bass.ds(g * U + r, 1), :, at:at + kt * P].rearrange("a p n -> (a p) n")
                                     ).then_inc(w_in[r % raws], 16)

            @block.tensor
            def _(pe):
                pe.sem_inc(product, 2)
                if source is not None:
                    pe.wait_ge(x_low, kt - len(range(1, kt, 3)))
                    pe.wait_ge(x_low_pool, len(range(1, kt, 3)))
                with pe.Fori(0, mt // U) as g:
                    for r in range(U):
                        pe.wait_ge(low_done, g * U + (r + 1 + raws))
                        pe.wait_ge(psum_read, g * U + (r + 1))
                        for c in range(kt):
                            cols = slice(c * P, (c + 1) * P)
                            for h in range(halves):
                                last = product3(nc, psum(r)[:, h, :], (high[:, r % 2, cols], low[:, r % 2, cols]),
                                                [a[:, c, h * w:(h + 1) * w] for a in x], c == 0, c == kt - 1)
                        last.then_inc(product, 1)

            def split(dve, g, r):
                dve.wait_ge(w_in[r % raws], g * (16 * U // raws) + (16 * (r // raws) + 16))
                dve.wait_ge(product, g * U + (r + 1))
                nc.vector.tensor_copy(high[:, r % 2, :], raw[:, r % raws, :]).then_inc(high_done, 1)
                dve.wait_ge(high_done, g * U + (r + 1))
                nc.vector.tensor_tensor(low[:, r % 2, :], raw[:, r % raws, :], high[:, r % 2, :].bitcast(F32), ALU.subtract
                                        ).then_inc(low_done, 1)

            def finish_tile(dve, g, r):
                m = g * U + r
                if finish == "add":
                    dve.wait_ge(product, m + 3)
                    nc.vector.tensor_tensor(tile(dst, m), tile(dst, m), psum(r), ALU.add).then_inc(psum_read, 1)
                elif gated:
                    dve.wait_ge(psum_read, m + (1 + per))
                    if finish == "gate_add":
                        nc.vector.tensor_tensor(temp2[:], temp[:, r % 2, :], flat(other, m), ALU.mult).then_inc(gate_out, 1)
                        dve.wait_ge(gate_out, m + 3)
                        nc.vector.tensor_tensor(flat(dst, m), flat(dst, m), temp2[:], ALU.add).then_inc(written, 1)
                        dve.wait_ge(written, m + 1)
                    else:
                        nc.vector.tensor_tensor(flat(dst, m), flat(dst, m), temp[:, r % 2, :], ALU.mult).then_inc(gate_out, 1)

            @block.vector
            def _(dve):
                dve.sem_inc(low_done, raws)
                if gated:
                    dve.sem_inc(gate_out, 2)
                if finish == "add":
                    dve.sem_inc(psum_read, per)

                split_source(dve, nc.vector.tensor_tensor, [t for t in range(kt) if t % 3 != 1], x_low)

                def turn(g, first):
                    for r in range(U):
                        split(dve, g, r)
                        if r:
                            finish_tile(dve, g, r - 1)
                        elif not first:
                            finish_tile(dve, g - 1, U - 1)
                turn(0, True)
                if mt > U:
                    with dve.Fori(1, mt // U) as g:
                        turn(g, False)
                finish_tile(dve, mt // U - 1, U - 1)

            @block.scalar
            def _(act):
                if source is not None:
                    for t in range(kt):
                        nc.scalar.activation(x[0][:, t, :], source[:, t, :], ACT.Copy).then_inc(x_high, 1)
                if finish == "add":
                    return
                act.sem_inc(psum_read, per)
                with act.Fori(0, mt // U) as g:
                    for r in range(U):
                        act.wait_ge(product, g * U + (r + 3))
                        if gated:
                            act.wait_ge(gate_out, g * U + (r + 1))
                            nc.scalar.activation(temp[:, r % 2, :].rearrange("p (h n) -> p h n", h=halves), psum(r), func
                                                 ).then_inc(psum_read, 1)
                        else:
                            nc.scalar.activation(tile(dst, g * U + r), psum(r), func).then_inc(psum_read, 1)


def chunk_cols(c):
    return slice(0, META) if c == 0 else slice(META + (c - 1) * CH, META + c * CH)


def block_cols(b):
    return slice(META + b * P, META + (b + 1) * P)


def small_products_phase(k, name, hn, w_low, low, w_dt, dt_raw):
    nc = k.nc
    done, evicted = k.sems(name, "done evicted")
    with nc.Block() as block:
        @block.tensor
        def _(pe):
            for h in range(2):
                for c in range(KD):
                    last = nc.tensor.matmul(k.banks[0:GATE_RANK, h, 0:264], w_low[:, c, :], hn[:, c, h * 264:h * 264 + 264],
                                            start=(c == 0), stop=(c == KD - 1))
            last.then_inc(done, 1)
            for b in range(NB):
                for c in range(KD):
                    nc.tensor.matmul(k.banks[:, 2, b * 32:b * 32 + 32], hn[:, c, block_cols(b)], w_dt[:, c, :],
                                     start=(c == 0), stop=(c == KD - 1))
            for c in range(KD):
                last = nc.tensor.matmul(k.banks[0:META, 3, 0:32], hn[:, c, 0:META], w_dt[:, c, :],
                                        start=(c == 0), stop=(c == KD - 1))
            last.then_inc(done, 1)

        @block.vector
        def _(dve):
            nc.vector.memset(low[:], 1.0).then_inc(evicted, 1)
            nc.vector.memset(dt_raw[:, NB, :], 0.0).then_inc(evicted, 1)
            dve.wait_ge(evicted, 2)
            dve.wait_ge(done, 1)
            nc.vector.tensor_copy(low[0:GATE_RANK, :].rearrange("p (h n) -> p h n", h=2), k.banks[0:GATE_RANK, 0:2, 0:264]
                                  ).then_inc(evicted, 1)
            dve.wait_ge(done, 2)
            nc.vector.tensor_copy(dt_raw[:, 0:NB, :].rearrange("p b n -> p (b n)"), k.banks[:, 2, 0:NB * 32]).then_inc(evicted, 1)
            nc.vector.tensor_copy(dt_raw[0:META, NB, :], k.banks[0:META, 3, 0:32]).then_inc(evicted, 1)


def gla_phase(k, name, hn, low, gate_w, wq, wk, wv, o):
    nc = k.nc
    SC = GLA_DK ** -0.5
    (q_in, k_in, v_in, q_done, k_done, v_done, gate_done, gate_abs, gate_exp, gate_ln, lg_done, g_done, g_last, e_done, to_last,
     prod, kdt_done, att_done, kdt_ready, v_ready, kv_done, state, att_copy, att_ready, o_done, o_out, head_gate, cleared,
     high_done, low_done) = k.sems(
        name, "q_in k_in v_in q_done k_done v_done gate_done gate_abs gate_exp gate_ln lg_done g_done g_last e_done to_last prod "
              "kdt_done att_done kdt_ready v_ready kv_done state att_copy att_ready o_done o_out head_gate cleared high_done low_done")
    with ExitStack() as ctx:
        def sb(n, shape):
            return ctx.enter_context(nc.sbuf_tensor(f"{name}_{n}", shape, F32))
        raw = sb("raw", [P, 4, KD * P])
        high, low_w = (ctx.enter_context(nc.sbuf_tensor(f"{name}_{n}", [P, 4, KD * P], F32R)) for n in ("high", "low"))
        gate_h = sb("gate_h", [GATE_RANK + 1, P])
        v, vm = sb("v", [P, NB, GLA_DV]), sb("vm", [META, GLA_DV])
        ab, abm, lg, lgm = sb("ab", [P, SEQ]), sb("abm", [META, P]), sb("lg", [P, SEQ]), sb("lgm", [META, P])
        glast = sb("glast", [P, 9])
        e_pos, e_neg, e_last = sb("e_pos", [P, L]), sb("e_neg", [P, L]), sb("e_last", [P, L])
        qe, qn, ke, kn, kd = (sb(n, [P, L]) for n in ("qe", "qn", "ke", "kn", "kd"))
        kdt, kdtm = sb("kdt", [P, NB, P]), sb("kdtm", [META, P])
        att, attm = sb("att", [P, NB, P]), sb("attm", [META, META])
        S = sb("S", [P, 8, GLA_DV])
        B = k.banks
        ident, tri = k.const("ident"), k.const("tri16")
        causal = k.const("causal").bitcast(U32)
        two = "p (h n) -> p h n"

        halves = (slice(0, CH), slice(CH, P))

        def state_bank(c):
            if c == 0:
                return B[:, 1, 0:256]
            bank, at = 4 + 2 * ((c - 1) % 2) + (c - 1) // 4, ((c - 1) // 2 % 2) * 256
            return B[:, bank, at:at + 256]

        with nc.Block() as block:
            @block.sync
            def _(sp):
                with sp.Fori(0, GLA_HEADS) as h:
                    sp.wait_ge(v_done, h + 1)
                    for to, source, arrived in ((raw[:, 0, :], wq, q_in), (raw[:, 1, :], wk, k_in),
                                                (raw[:, 2:4, :].rearrange("p c n -> p (c n)"), wv, v_in)):
                        sp.dma_start(to, source[bass.ds(h, 1)].rearrange("a p n -> (a p) n")).then_inc(arrived, 16)

            @block.gpsimd
            def _(pool):
                with pool.Fori(0, GLA_HEADS) as h:
                    pool.wait_ge(gate_done, h + 1)
                    nc.gpsimd.tensor_copy(gate_h[:], gate_w[:, bass.ds(h * P, P)]).then_inc(head_gate, 1)

            @block.tensor
            def _(pe):
                pe.sem_inc(v_done, 1)
                pe.sem_inc(gate_done, 1)
                with pe.Fori(0, GLA_HEADS) as h:
                    pe.wait_ge(o_out, h * 3 + 3)
                    for i, sem in enumerate((q_done, k_done)):
                        pe.wait_ge(low_done, h * 4 + i + 1)
                        for c in range(KD):
                            for j in range(2):
                                last = product3(nc, B[:, 2 * i + j, 0:264], [a[:, i, c * P:(c + 1) * P] for a in (high, low_w)],
                                                [a[:, c, j * 264:j * 264 + 264] for a in hn], c == 0, c == KD - 1)
                        last.then_inc(sem, 1)
                    pe.wait_ge(low_done, h * 4 + 4)
                    wv_pair = [a[:, 2:4, :].rearrange("p a (c n) -> p (a c) n", n=GLA_DV) for a in (high, low_w)]
                    for b in range(NB + 1):
                        cols = block_cols(b) if b < NB else slice(0, P)
                        to = B[:, 4 + b // 2, (b % 2) * 256:(b % 2) * 256 + 256] if b < NB else B[:, 7, 0:256]
                        for c in range(KD):
                            last = product3(nc, to, [a[:, c, cols] for a in hn], [a[:, c, :] for a in wv_pair],
                                            c == 0, c == KD - 1)
                    last.then_inc(v_done, 1)
                    pe.wait_ge(head_gate, h + 1)
                    pe.wait_ge(v_ready, h * 2 + 2)
                    for b in range(NB):
                        nc.tensor.matmul(B[:, 6, b * P:(b + 1) * P], low[:, block_cols(b)], gate_h[:], start=True, stop=True)
                    nc.tensor.matmul(B[0:META, 7, 256:384], low[:, 0:META], gate_h[:], start=True, stop=True
                                     ).then_inc(gate_done, 1)
                    pe.wait_ge(lg_done, h * 2 + 2)
                    for b in range(NB):
                        nc.tensor.matmul(B[:, 6, b * P:(b + 1) * P], lg[:, b * P:(b + 1) * P], tri, start=True, stop=True)
                    nc.tensor.matmul(B[:, 7, 384:400], lgm[:], tri[0:META, 0:META], start=True, stop=True
                                     ).then_inc(g_done, 1)
                    pe.wait_ge(prod, h * 5 + 5)
                    for b in range(NB):
                        nc.tensor.transpose(B[:, 0, b * P:(b + 1) * P], kd[:, block_cols(b)], ident)
                    nc.tensor.transpose(B[0:META, 1, 0:P], kd[:, 0:META], ident).then_inc(kdt_done, 1)
                    for c in range(1, 9):
                        b, half = (c - 1) // 2, (c - 1) % 2
                        for at, kk, qq in ((0, kn, qe), (256, ke, qn)):
                            nc.tensor.matmul(B[half * CH:half * CH + CH, 2, at + b * CH:at + b * CH + CH],
                                             kk[:, chunk_cols(c)], qq[:, chunk_cols(c)], start=True, stop=True)
                    nc.tensor.matmul(B[0:META, 3, 0:META], kn[:, 0:META], qe[:, 0:META], start=True, stop=True)
                    nc.tensor.matmul(B[0:META, 3, META:2 * META], ke[:, 0:META], qn[:, 0:META], start=True, stop=True
                                     ).then_inc(att_done, 1)
                    pe.wait_ge(v_ready, h * 2 + 2)
                    pe.wait_ge(kdt_ready, h * 2 + 2)
                    for c in range(8):
                        b, half = (c - 1) // 2, (c - 1) % 2
                        rows = slice(0, META) if c == 0 else slice(half * CH, half * CH + CH)
                        nc.tensor.matmul(state_bank(c),
                                         kdtm[:] if c == 0 else kdt[rows, b, :], vm[:] if c == 0 else v[rows, b, :],
                                         start=True, stop=True).then_inc(kv_done, 1)
                    pe.wait_ge(att_ready, h * 3 + 3)
                    for j in range(2):
                        nc.tensor.matmul(B[:, 3, 64 + META * j:64 + META * j + META], vm[:, j * P:(j + 1) * P], attm[:],
                                         start=True, stop=True)
                    for b in range(NB):
                        for j in range(2):
                            nc.tensor.matmul(B[:, j, b * P:(b + 1) * P], v[:, b, j * P:(j + 1) * P], att[:, b, :],
                                             start=True, stop=False)
                            for c in (1 + 2 * b, 2 + 2 * b):
                                if j == 0:
                                    pe.wait_ge(state, h * 8 + c)
                                last = nc.tensor.matmul(B[:, j, (c - 1) * CH:c * CH], S[:, c - 1, j * P:(j + 1) * P],
                                                        qe[:, chunk_cols(c)], start=False, stop=(c % 2 == 0))
                    last.then_inc(o_done, 1)

            @block.scalar
            def _(act):
                act.sem_inc(o_out, 3)
                with act.Fori(0, GLA_HEADS) as h:
                    act.wait_ge(v_done, h + 2)
                    nc.scalar.activation(v[:].rearrange("p (a b) n -> p a (b n)", b=2), B[:, 4:6, :], ACT.Copy).then_inc(v_ready, 1)
                    nc.scalar.activation(vm[:], B[0:META, 7, 0:256], ACT.Copy).then_inc(v_ready, 1)
                    act.wait_ge(gate_done, h + 2)
                    nc.scalar.activation(ab[:], B[:, 6, :], ACT.Abs).then_inc(gate_abs, 1)
                    nc.scalar.activation(abm[:], B[0:META, 7, 256:384], ACT.Abs).then_inc(gate_abs, 1)
                    act.wait_ge(gate_abs, h * 2 + 2)
                    nc.scalar.activation(ab[:], ab[:], ACT.Exp, scale=-1.0).then_inc(gate_exp, 1)
                    nc.scalar.activation(abm[:], abm[:], ACT.Exp, scale=-1.0).then_inc(gate_exp, 1)
                    act.wait_ge(gate_exp, h * 2 + 2)
                    nc.scalar.activation(ab[:], ab[:], ACT.Ln, bias=1.0).then_inc(gate_ln, 1)
                    nc.scalar.activation(abm[:], abm[:], ACT.Ln, bias=1.0).then_inc(gate_ln, 1)
                    act.wait_ge(g_last, h * 2 + 2)
                    for e, sign in ((e_pos, 1.0), (e_neg, -1.0)):
                        nc.scalar.activation(e[:, META:L], B[:, 6, :], ACT.Exp, scale=sign).then_inc(e_done, 1)
                        nc.scalar.activation(e[:, 0:META], B[:, 7, 384:400], ACT.Exp, scale=sign).then_inc(e_done, 1)
                    for c in range(9):
                        g = B[:, 7, 384:400] if c == 0 else B[:, 6, (c - 1) * CH:c * CH]
                        nc.scalar.activation(e_last[:, chunk_cols(c)], g, ACT.Exp, bias=glast[:, c:c + 1], scale=-1.0
                                             ).then_inc(to_last, 1)
                    act.wait_ge(kdt_done, h + 1)
                    nc.scalar.activation(kdt[:].rearrange("p b n -> p (b n)"), B[:, 0, :], ACT.Copy).then_inc(kdt_ready, 1)
                    nc.scalar.activation(kdtm[:], B[0:META, 1, 0:P], ACT.Copy).then_inc(kdt_ready, 1)
                    act.wait_ge(o_done, h + 1)
                    for j in range(2):
                        nc.scalar.activation(o[:, bass.ds(h * 2 + j, 1), META:L].rearrange("p a n -> p (a n)"), B[:, j, :],
                                             ACT.Copy).then_inc(o_out, 1)
                    nc.scalar.activation(o[:, bass.ds(h * 2, 2), 0:META],
                                         B[:, 3, 64:64 + 2 * META].rearrange("p (a n) -> p a n", a=2), ACT.Copy).then_inc(o_out, 1)

            @block.vector
            def _(dve):
                nc.vector.memset(att[:], 0.0).then_inc(cleared, 1)
                dve.wait_ge(cleared, 1)
                with dve.Fori(0, GLA_HEADS) as h:
                    for i in range(4):
                        dve.wait_ge((q_in, k_in, v_in, v_in)[i], h * 16 + 16)
                        dve.wait_ge(v_done, h + 1)
                        nc.vector.tensor_copy(high[:, i, :], raw[:, i, :]).then_inc(high_done, 1)
                        dve.wait_ge(high_done, h * 4 + i + 1)
                        nc.vector.tensor_tensor(low_w[:, i, :], raw[:, i, :], high[:, i, :].bitcast(F32), ALU.subtract
                                                ).then_inc(low_done, 1)
                    dve.wait_ge(gate_ln, h * 2 + 2)
                    nc.vector.scalar_tensor_tensor(lg[:], B[:, 6, :], 0.0, ab[:], ALU.min, ALU.subtract).then_inc(lg_done, 1)
                    nc.vector.scalar_tensor_tensor(lgm[:], B[0:META, 7, 256:384], 0.0, abm[:], ALU.min, ALU.subtract
                                                   ).then_inc(lg_done, 1)
                    dve.wait_ge(g_done, h + 1)
                    nc.vector.tensor_copy(glast[:, 0:1], B[:, 7, 399:400]).then_inc(g_last, 1)
                    nc.vector.tensor_copy(glast[:, 1:9], B[:, 6, CH - 1:SEQ:CH]).then_inc(g_last, 1)
                    dve.wait_ge(q_done, h + 1)
                    dve.wait_ge(k_done, h + 1)
                    dve.wait_ge(e_done, h * 4 + 4)
                    for to, bank, sc, e in ((qe, 0, SC, e_pos), (qn, 0, SC, e_neg), (kn, 2, 1.0, e_neg), (ke, 2, 1.0, e_pos),
                                            (kd, 2, 1.0, e_last)):
                        if e is e_last:
                            dve.wait_ge(to_last, h * 9 + 9)
                        nc.vector.scalar_tensor_tensor(to[:].rearrange(two, h=2), B[:, bank:bank + 2, 0:264], sc,
                                                       e[:].rearrange(two, h=2), ALU.mult, ALU.mult).then_inc(prod, 1)
                    dve.wait_ge(att_done, h + 1)
                    for r in halves:
                        nc.vector.tensor_copy(att[r, :, r], B[r, 2, 256:512].rearrange("p (b n) -> p b n", b=NB)).then_inc(att_copy, 1)
                    nc.vector.tensor_copy(attm[:], B[0:META, 3, META:2 * META]).then_inc(att_copy, 1)
                    dve.wait_ge(att_copy, h * 3 + 3)
                    dve.wait_ge(kv_done, h * 8 + 8)
                    nc.vector.tensor_copy(S[:, 0, :], state_bank(0)).then_inc(state, 1)
                    for r in halves:
                        nc.vector.copy_predicated(att[r, :, r], causal[r, :].rearrange("p (b n) -> p b n", b=NB),
                                                  B[r, 2, 0:256].rearrange("p (b n) -> p b n", b=NB)).then_inc(att_ready, 1)
                    nc.vector.copy_predicated(attm[:], causal[0:META, 0:META], B[0:META, 3, 0:META]).then_inc(att_ready, 1)
                    for c in range(1, 8):
                        dve.wait_ge(state, h * 8 + c)
                        kv = state_bank(c)
                        nc.vector.scalar_tensor_tensor(S[:, c, :], S[:, c - 1, :], e_pos[:, META + c * CH - 1:META + c * CH],
                                                       kv, ALU.mult, ALU.add).then_inc(state, 1)


def ssd_prep_phase(k, name, dt, bias, a_log, acum, e_acum, to_end, e_total, e_total_m):
    nc = k.nc
    B = k.banks
    (biased, abs_done, u_done, v, neg, sums, diff, e_diff, exps) = k.sems(
        name, "biased abs_done u_done v neg sums diff e_diff exps")
    n = (NB + 1) * SSD_HEADS
    nx = NB * SSD_HEADS
    with ExitStack() as ctx:
        def sb(nm):
            return ctx.enter_context(nc.sbuf_tensor(f"{name}_{nm}", [P, n], F32))
        x, u, t, z, z2, p, ea, a = (sb(nm) for nm in ("x", "u", "t", "z", "z2", "p", "ea", "a"))
        flat = "p b n -> p (b n)"
        dt_f = dt[:].rearrange(flat)
        to_end_f, acum_f = to_end[:].rearrange(flat), acum[:].rearrange(flat)
        with nc.Block() as block:
            @block.vector
            def _(dve):
                done = [0]

                def step(ins):
                    ins.then_inc(v, 1)
                    done[0] += 1
                    dve.wait_ge(v, done[0])
                nc.vector.tensor_tensor(x[:].rearrange("p (b n) -> p b n", n=SSD_HEADS), dt[:],
                                        bias[:].unsqueeze(1).to_broadcast([P, NB + 1, SSD_HEADS]), ALU.add).then_inc(biased, 1)
                dve.wait_ge(u_done, 1)
                step(nc.vector.tensor_scalar(t[:], u[:], 2.0, None, ALU.add))
                step(nc.vector.reciprocal(t[:], t[:]))
                step(nc.vector.tensor_tensor(z[:], u[:], t[:], ALU.mult))
                step(nc.vector.tensor_tensor(z2[:], z[:], z[:], ALU.mult))
                step(nc.vector.tensor_scalar(p[:], z2[:], 1.0 / 15, None, ALU.mult))
                for c in (13, 11, 9, 7, 5, 3):
                    step(nc.vector.scalar_tensor_tensor(p[:], p[:], 1.0 / c, z2[:], ALU.add, ALU.mult))
                step(nc.vector.scalar_tensor_tensor(p[:], p[:], 1.0, z[:], ALU.add, ALU.mult))
                step(nc.vector.tensor_scalar(p[:], p[:], 2.0, None, ALU.mult))
                step(nc.vector.scalar_tensor_tensor(dt_f, x[:], 0.0, p[:], ALU.max, ALU.add))
                dve.wait_ge(exps, 1)
                nc.vector.scalar_tensor_tensor(a[:].rearrange("p (b n) -> p b n", n=SSD_HEADS), dt[:], -1.0,
                                               ea[:, 0:SSD_HEADS].unsqueeze(1).to_broadcast([P, NB + 1, SSD_HEADS]),
                                               ALU.mult, ALU.mult).then_inc(neg, 1)
                step(nc.vector.memset(to_end[:, NB, :], 0.0))
                step(nc.vector.memset(acum[:, NB, :], 0.0))
                dve.wait_ge(sums, 1)
                step(nc.vector.tensor_copy(acum_f[:, 0:nx], B[:, 0, 0:nx]))
                step(nc.vector.tensor_copy(acum_f[0:META, nx:n], B[0:META, 0, nx:n]))
                nc.vector.tensor_tensor(to_end_f[:, 0:nx], B[:, 1, 0:nx], acum_f[:, 0:nx], ALU.subtract).then_inc(diff, 1)
                nc.vector.tensor_tensor(to_end_f[0:META, nx:n], B[0:META, 1, nx:n], acum_f[0:META, nx:n],
                                        ALU.subtract).then_inc(diff, 1)
                dve.wait_ge(e_diff, 1)
                step(nc.vector.tensor_tensor(to_end_f, to_end_f, dt_f, ALU.mult))

            @block.scalar
            def _(act):
                act.wait_ge(biased, 1)
                nc.scalar.activation(u[:], x[:], ACT.Abs).then_inc(abs_done, 1)
                act.wait_ge(abs_done, 1)
                nc.scalar.activation(u[:], u[:], ACT.Exp, scale=-1.0).then_inc(u_done, 1)
                nc.scalar.activation(ea[:, 0:SSD_HEADS], a_log[:], ACT.Exp).then_inc(exps, 1)
                act.wait_ge(diff, 2)
                nc.scalar.activation(to_end_f, to_end_f, ACT.Exp).then_inc(e_diff, 1)
                nc.scalar.activation(e_acum[:].rearrange(flat), acum_f, ACT.Exp).then_inc(exps, 1)
                for half in range(2):
                    nc.scalar.activation(e_total[:, half].rearrange(flat), B[:, 2 + half, 0:nx], ACT.Exp).then_inc(exps, 1)
                nc.scalar.activation(e_total_m[:], B[:, 4, 0:SSD_HEADS], ACT.Exp).then_inc(exps, 1)

            @block.tensor
            def _(pe):
                pe.wait_ge(neg, 1)
                m = slice(nx, n)
                nc.tensor.matmul(B[:, 0, 0:nx], k.const("tri"), a[:, 0:nx], start=True, stop=True)
                nc.tensor.matmul(B[0:META, 0, m], k.const("tri")[0:META, 0:META], a[0:META, m], start=True, stop=True)
                nc.tensor.matmul(B[:, 1, 0:nx], k.const("same"), a[:, 0:nx], start=True, stop=True)
                nc.tensor.matmul(B[0:META, 1, m], k.const("ones")[0:META, 0:META], a[0:META, m], start=True, stop=True)
                for half in range(2):
                    nc.tensor.matmul(B[:, 2 + half, 0:nx], k.const(f"half{half}"), a[:, 0:nx], start=True, stop=True)
                nc.tensor.matmul(B[:, 4, 0:SSD_HEADS], k.const("ones")[0:META, :], a[0:META, m], start=True, stop=True
                                 ).then_inc(sums, 1)


def ssd_phase(k, name, hn, w_xbc, conv, skip, dt, acum, e_acum, to_end, e_total, e_total_m, y, spare):
    nc = k.nc
    B = k.banks
    T, H, HD = 6, SSD_HPG, SSD_HD
    w_in = k.sems(name, "w_in0 w_in1 w_in2")
    (high_done, low_done, params, product, raw_out, tap, act_done, skipped, x_turned, x_used, b_turned, b_out, cb_done, diag, row_done,
     diff, absd, seg, m_ready, kv_done, decayed, state, inter_scaled, y_done, y_tok, y_turned, y_out, passed, passed_pool) = k.sems(
        name, "high_done low_done params product raw_out tap act_done skipped x_turned x_used b_turned b_out cb_done diag row_done "
              "diff absd seg m_ready kv_done decayed state inter_scaled y_done y_tok y_turned y_out passed passed_pool")
    with ExitStack() as ctx:
        def sb(n, shape):
            return ctx.enter_context(nc.sbuf_tensor(f"{name}_{n}", shape, F32))
        raw_w = sb("raw_w", [P, 3, KD * P])
        high, low_w = (ctx.enter_context(nc.sbuf_tensor(f"{name}_{n}", [P, 2, KD * P], F32R)) for n in ("high", "low"))
        cw, dg = sb("cw", [P, T, 5]), sb("dg", [P, 4])
        xd, raw, acc = spare[:, 0:4, :], spare[:, 4:6, :], spare[:, 6:8, :]
        xc = sb("xc", [P, T, L])
        xdt, xend = sb("xdt", [P, NB + 1, H * HD]), sb("xend", [P, NB + 1, H * HD])
        bt = sb("bt", [P, NB + 1, P])
        X, E, M = sb("X", [P, H * HD]), sb("E", [P, 2, H * HD]), sb("M", [P, NB + 1, H * HD])
        S, decay = sb("S", [P, 4, H * HD]), sb("decay", [P, H * HD])
        yt = sb("yt", [P, 2, H * HD])
        ident = k.const("ident")
        diag64 = k.const("diag64")

        def heads(a, n=HD):
            return a.rearrange("p (r t) -> p r t", t=n)

        def of(a, r, b, g, n=HD):
            m = r.stop - r.start
            return a[r, b, bass.ds(g * H, H)].unsqueeze(2).to_broadcast([m, H, n])

        full, meta = slice(0, P), slice(0, META)
        with nc.Block() as block:
            @block.sync
            def _(sp):
                with sp.Fori(0, SSD_GROUPS) as g:
                    for j in range(T):
                        sp.wait_ge(low_done, g * T + j + 1)
                        sp.dma_start(raw_w[:, j % 3, :], w_xbc[bass.ds(g * T + j, 1)].rearrange("a p n -> (a p) n")
                                     ).then_inc(w_in[j % 3], 16)

            @block.gpsimd
            def _(pool):
                with pool.Fori(0, SSD_GROUPS) as g:
                    pool.wait_ge(y_out, g * 5 + 1)
                    pool.wait_ge(tap, g * 24 + 1)
                    nc.gpsimd.tensor_copy(cw[:], conv[:, bass.ds(g, 1)].rearrange("p a t n -> p (a t) n")).then_inc(params, 1)
                    nc.gpsimd.tensor_copy(dg[:], skip[:, bass.ds(g * 4, 4)]).then_inc(params, 1)
                    for b in range(NB + 1):
                        r, n = (full, HD) if b < NB else (meta, META)
                        pool.wait_ge(row_done, g * 5 + b + 1)
                        nc.gpsimd.tensor_tensor(heads(X[r, 0:H * n], n), of(acum, r, b, g, n),
                                                diag64[r, 0:n].unsqueeze(1).to_broadcast([r.stop, H, n]), ALU.mult
                                                ).then_inc(diag, 1)
                    pool.wait_ge(params, g * 2 + 2)
                    for j in range(4):
                        pool.wait_ge(act_done, g * T + j + 1)
                        pool.sem_inc(passed_pool, 1)
                        nc.gpsimd.tensor_scalar(xd[:, j, :], xc[:, j, :], dg[:, j:j + 1], None, ALU.mult).then_inc(skipped, 1)

            @block.tensor
            def _(pe):
                pe.sem_inc(product, 2)
                pe.sem_inc(row_done, 1)
                with pe.Fori(0, SSD_GROUPS) as g:
                    for j in range(T):
                        pe.wait_ge(low_done, g * T + j + 4)
                        if j < 3:
                            pe.wait_ge(y_out, g * 5 + 1)
                        else:
                            pe.wait_ge(raw_out, g * T + j - 2)
                        for c in range(KD):
                            for i in range(2):
                                last = product3(nc, B[:, 2 * (j % 3) + i, 0:264],
                                                [a[:, j % 2, c * P:(c + 1) * P] for a in (high, low_w)],
                                                [a[:, c, i * 264:i * 264 + 264] for a in hn], c == 0, c == KD - 1)
                        last.then_inc(product, 1)
                    pe.wait_ge(raw_out, g * T + T)
                    pe.wait_ge(act_done, g * T + T)
                    for b in range(NB):
                        nc.tensor.transpose(B[:, 0, b * P:(b + 1) * P], xc[:, 4, block_cols(b)], ident)
                    last = nc.tensor.transpose(B[meta, 2, 0:P], xc[:, 4, meta], ident).then_inc(b_turned, 1)
                    for c in range(1, 9):
                        b, half = (c - 1) // 2, (c - 1) % 2
                        nc.tensor.matmul(B[half * CH:half * CH + CH, 3, b * CH:b * CH + CH], xc[:, 4, chunk_cols(c)],
                                         xc[:, 5, chunk_cols(c)], start=True, stop=True)
                    nc.tensor.matmul(B[meta, 3, 256:256 + META], xc[:, 4, meta], xc[:, 5, meta], start=True, stop=True
                                     ).then_inc(cb_done, 1)
                    for b in range(NB + 1):
                        r = full if b < NB else meta
                        if b >= 2:
                            pe.wait_ge(x_used, g * 10 + 2 * (b - 1))
                        for j in range(4):
                            last = nc.tensor.transpose(B[r, 6 + b % 2, j * P:(j + 1) * P],
                                                       xc[:, j, block_cols(b) if b < NB else meta], ident)
                        last.then_inc(x_turned, 1)
                    for b in range(NB + 1):
                        r, n = (full, HD) if b < NB else (meta, META)
                        pe.wait_ge(diag, g * 5 + b + 1)
                        if b >= 2:
                            pe.wait_ge(diff, g * 5 + b - 1)
                        pe.sem_inc(passed, 1)
                        nc.tensor.matmul(B[r, 4 + b % 2, 0:H * n], k.const("same")[r, r] if b < NB else k.const("ones")[r, r],
                                         X[r, 0:H * n], start=True, stop=True).then_inc(row_done, 1)

                    def state_part(c):
                        b, half = (c - 1) // 2, (c - 1) % 2
                        rr = meta if c == 0 else slice(half * CH, half * CH + CH)
                        if c >= 2:
                            pe.wait_ge(state, g * 8 + c - 1)
                        nc.tensor.matmul(B[:, 6 + c % 2, :], bt[rr, NB if c == 0 else b, :], xend[rr, NB if c == 0 else b, :],
                                         start=True, stop=True).then_inc(kv_done, 1)

                    pe.wait_ge(x_used, g * 10 + 10)
                    pe.wait_ge(b_out, g * 2 + 2)
                    state_part(0)
                    for b in range(NB + 1):
                        r = full if b < NB else meta
                        pe.wait_ge(m_ready, g * 5 + b + 1)
                        if b > 0:
                            pe.wait_ge(y_tok, g * 5 + b)
                        pe.sem_inc(passed, 1)
                        for i in range(2 if b < NB else 1):
                            rr = slice(i * CH, i * CH + CH) if b < NB else meta
                            n = CH if b < NB else META
                            for h in range(H):
                                last = nc.tensor.matmul(B[rr, 0, h * HD:(h + 1) * HD], M[rr, b, h * n:(h + 1) * n],
                                                        xdt[rr, b, h * HD:(h + 1) * HD], start=True, stop=True)
                        if b < NB:
                            for i in range(2):
                                c = 1 + 2 * b + i
                                pe.wait_ge(state, g * 8 + c)
                                last = nc.tensor.matmul(B[i * CH:i * CH + CH, 1, :], xc[:, 5, chunk_cols(c)],
                                                        S[:, (c - 1) % 4, :], start=True, stop=True)
                                if c < 8:
                                    if i == 0:
                                        state_part(c)
                        last.then_inc(y_done, 1)
                        if b < NB - 1:
                            state_part(2 + 2 * b)
                        pe.wait_ge(y_tok, g * 5 + b + 1)
                        if b >= 2:
                            pe.wait_ge(y_out, g * 5 + b)
                        if b == 0:
                            pe.wait_ge(diff, g * 5 + 5)
                        pe.sem_inc(passed, 1)
                        for j in range(4):
                            n = P if b < NB else META
                            last = nc.tensor.transpose(B[:, 4 + b % 2, j * n:(j + 1) * n], yt[r, b % 2, j * P:(j + 1) * P],
                                                       ident[r, r])
                        last.then_inc(y_turned, 1)

            @block.scalar
            def _(act):
                with act.Fori(0, SSD_GROUPS) as g:
                    def silu(j):
                        act.wait_ge(tap, g * 24 + 4 * (j + 1) + 1)
                        nc.scalar.activation(xc[:, j, :], acc[:, j % 2, :], ACT.Silu).then_inc(act_done, 1)
                    for j in range(T):
                        act.wait_ge(product, g * T + j + 3)
                        if j >= 2:
                            act.wait_ge(tap, g * 24 + 4 * (j - 1) + 1)
                        nc.scalar.activation(raw[:, j % 2, :].rearrange("p (h n) -> p h n", h=2),
                                             B[:, 2 * (j % 3):2 * (j % 3) + 2, 0:264], ACT.Copy).then_inc(raw_out, 1)
                        if j > 0:
                            silu(j - 1)
                    silu(T - 1)
                    act.wait_ge(b_turned, g + 1)
                    nc.scalar.activation(bt[:, 0:NB, :].rearrange("p b n -> p (b n)"), B[:, 0, :], ACT.Copy).then_inc(b_out, 1)
                    nc.scalar.activation(bt[meta, NB, :], B[meta, 2, 0:P], ACT.Copy).then_inc(b_out, 1)
                    for b in range(NB + 1):
                        r, n = (full, HD) if b < NB else (meta, META)
                        act.wait_ge(diff, g * 5 + b + 1)
                        nc.scalar.activation(E[r, b % 2, 0:H * n], E[r, b % 2, 0:H * n], ACT.Abs).then_inc(absd, 1)
                        act.wait_ge(absd, g * 5 + b + 1)
                        nc.scalar.activation(E[r, b % 2, 0:H * n], E[r, b % 2, 0:H * n], ACT.Exp, scale=-1.0).then_inc(seg, 1)

            @block.vector
            def _(dve):
                dve.sem_inc(tap, 1)
                dve.sem_inc(low_done, 3)
                dve.sem_inc(y_out, 1)
                with dve.Fori(0, SSD_GROUPS) as g:
                    def split(j):
                        dve.wait_ge(w_in[j % 3], g * 32 + (16 * (j // 3) + 16))
                        dve.wait_ge(product, g * T + j + 1)
                        nc.vector.tensor_copy(high[:, j % 2, :], raw_w[:, j % 3, :]).then_inc(high_done, 1)
                        dve.wait_ge(high_done, g * T + j + 1)
                        nc.vector.tensor_tensor(low_w[:, j % 2, :], raw_w[:, j % 3, :], high[:, j % 2, :].bitcast(F32),
                                                ALU.subtract).then_inc(low_done, 1)

                    def convolve(j):
                        dve.wait_ge(raw_out, g * T + j + 1)
                        if j >= 2:
                            dve.wait_ge(act_done, g * T + j - 1)
                        x, to = raw[:, j % 2, :], acc[:, j % 2, :]
                        nc.vector.tensor_scalar(to, x, cw[:, j, 3:4], cw[:, j, 4:5], ALU.mult, ALU.add).then_inc(tap, 1)
                        for s in (1, 2, 3):
                            dve.wait_ge(tap, g * 24 + 4 * j + s + 1)
                            nc.vector.scalar_tensor_tensor(to[:, s:L], x[:, 0:L - s], cw[:, j, 3 - s:4 - s], to[:, s:L],
                                                           ALU.mult, ALU.add).then_inc(tap, 1)
                    split(0)
                    split(1)
                    dve.wait_ge(params, g * 2 + 2)
                    for j in range(T):
                        if j + 2 < T:
                            split(j + 2)
                        convolve(j)
                    for b in range(NB + 1):
                        r = full if b < NB else meta
                        dve.wait_ge(x_turned, g * 5 + b + 1)
                        for to, by in ((xdt, dt), (xend, to_end)):
                            nc.vector.tensor_tensor(heads(to[r, b, :]), heads(B[r, 6 + b % 2, :]), of(by, r, b, g), ALU.mult
                                                    ).then_inc(x_used, 1)

                    def weights(b):
                        r, n = (full, HD) if b < NB else (meta, META)
                        dve.wait_ge(seg, g * 5 + b + 1)
                        if b == 0:
                            dve.wait_ge(cb_done, g + 1)
                        cb = B[r, 3, b * CH:b * CH + CH] if b < NB else B[r, 3, 256:256 + META]
                        nc.vector.tensor_tensor(heads(M[r, b, 0:H * n], n), heads(E[r, b % 2, 0:H * n], n),
                                                cb.unsqueeze(1).to_broadcast([r.stop, H, n]), ALU.mult).then_inc(m_ready, 1)
                    for b in range(NB + 1):
                        r, n = (full, HD) if b < NB else (meta, META)
                        if b >= 2:
                            weights(b - 2)
                            dve.wait_ge(m_ready, g * 5 + b - 1)
                        dve.wait_ge(row_done, g * 5 + b + 2)
                        nc.vector.tensor_tensor(heads(E[r, b % 2, 0:H * n], n), heads(B[r, 4 + b % 2, 0:H * n], n),
                                                of(acum, r, b, g, n), ALU.subtract).then_inc(diff, 1)
                    weights(NB - 1)
                    weights(NB)

                    def new_state(c):
                        b, half = (c - 1) // 2, (c - 1) % 2
                        dve.wait_ge(kv_done, g * 8 + c + 1)
                        if c == 0:
                            nc.vector.tensor_copy(S[:, 0, :], B[:, 6, :]).then_inc(state, 1)
                            return
                        dve.wait_ge(state, g * 8 + c)
                        by = e_total[:, half, b, bass.ds(g * H, H)].unsqueeze(2).to_broadcast([P, H, HD])
                        nc.vector.tensor_tensor(heads(decay[:]), heads(S[:, (c - 1) % 4, :]), by, ALU.mult).then_inc(decayed, 1)
                        dve.wait_ge(decayed, g * 7 + c)
                        nc.vector.tensor_tensor(S[:, c % 4, :], decay[:], B[:, 6 + c % 2, :], ALU.add).then_inc(state, 1)
                    new_state(0)
                    for b in range(NB + 1):
                        r, n = (full, P) if b < NB else (meta, META)
                        if b < NB:
                            new_state(1 + 2 * b)
                        dve.wait_ge(y_done, g * 5 + b + 1)
                        if b < NB:
                            nc.vector.tensor_tensor(heads(yt[r, b % 2, :]), heads(B[r, 1, :]), of(e_acum, r, b, g), ALU.mult
                                                    ).then_inc(inter_scaled, 1)
                            dve.wait_ge(inter_scaled, g * 4 + b + 1)
                            nc.vector.tensor_tensor(yt[r, b % 2, :], yt[r, b % 2, :], B[r, 0, :], ALU.add).then_inc(y_tok, 1)
                        else:
                            nc.vector.tensor_copy(yt[r, b % 2, :], B[r, 0, :]).then_inc(y_tok, 1)
                        if b < NB - 1:
                            new_state(2 + 2 * b)
                        dve.wait_ge(skipped, g * 4 + 4)
                        dve.wait_ge(y_turned, g * 5 + b + 1)
                        cols = block_cols(b) if b < NB else meta
                        nc.vector.tensor_tensor(y[:, bass.ds(g * 4, 4), cols], xd[:, :, cols],
                                                B[:, 4 + b % 2, 0:4 * n].rearrange("p (j n) -> p j n", j=4), ALU.add
                                                ).then_inc(y_out, 1)


def route_phase(k, name, q, keys, chosen, hb, u, early):
    nc = k.nc
    B = k.banks
    H, SIDES = PEER_HEADS, 2 * PEER_HEADS
    LOW = -3.0e38
    q_block, scored, v, passed, exp_done, turned, out_done, early_done, early_high, early_low, early_gelu = k.sems(
        name, "q_block scored v passed exp_done turned out_done early_done early_high early_low early_gelu")
    u_in = k.sems(name, " ".join(f"u_in{r}" for r in range(RING)))
    stored = k.sems(name, "stored0 stored1")
    STEPS = 5 * (SIDES + H) + 14
    with ExitStack() as ctx:
        def sb(n, shape, dt=F32):
            return ctx.enter_context(nc.sbuf_tensor(f"{name}_{n}", shape, dt))
        qb = sb("qb", [P, SIDES, P])
        rest = sb("rest", [P, SIDES, KEYS])
        top, idx, idxf = sb("top", [P, SIDES, TOPK]), sb("idx", [P, SIDES, TOPK], U32), sb("idxf", [P, SIDES, TOPK])
        cand, crest = sb("cand", [P, H, TOPK * TOPK]), sb("crest", [P, H, TOPK * TOPK])
        best, pos = sb("best", [P, H, TOPK]), sb("pos", [P, H, TOPK], U32)
        parts, partsf = sb("parts", [P, 2, H * TOPK], U32), sb("partsf", [P, 2, H * TOPK])
        hot = sb("hot", [P, H * TOPK, TOPK])
        picked = sb("picked", [P, 3, H * TOPK])
        total = sb("total", [P, H])
        us, A = sb("us", [P, RING, KD * P]), sb("A", [P, 2, SEQ])
        uh, ul = sb("uh", [P, 2, KD * P], F32R), sb("ul", [P, 2, KD * P], F32R)
        weights = picked[:, 2, :].rearrange("p (h n) -> p h n", h=H)
        iota16 = k.const("iota16")
        with nc.Block() as block:
            @block.sync
            def _(sp):
                with sp.Fori(0, NB) as b:
                    for t in range(GROUP):
                        sp.wait_ge(early_low, b * GROUP + (t + 1))
                        sp.dma_start(us[:, t % RING, :], u[bass.ds(b * GROUP + t, 1)].rearrange("a p n -> (a p) n")
                                     ).then_inc(u_in[t % RING], 16)

            @block.gpsimd
            def _(pool):
                pool.sem_inc(early_low, RING)
                with pool.Fori(0, NB) as b:
                    for t in range(GROUP):
                        pool.wait_ge(early_high, b * GROUP + (t + 1))
                        nc.gpsimd.tensor_tensor(ul[:, t % 2, :], us[:, t % RING, :], uh[:, t % 2, :].bitcast(F32), ALU.subtract
                                                ).then_inc(early_low, 1)

            @block.scalar
            def _(act):
                act.sem_inc(out_done, 1)
                act.sem_inc(early_gelu, 2)
                for s in stored:
                    act.sem_inc(s, 16)

                def copy_queries(b):
                    nc.scalar.activation(qb[:], q[:, :, bass.ds(b * P, P)], ACT.Copy).then_inc(q_block, 1)

                def high_part(b, t):
                    act.wait_ge(u_in[t % RING], b * 32 + (16 * (t // RING) + 16))
                    act.wait_ge(early_done, b * GROUP + (t + 1))
                    nc.scalar.activation(uh[:, t % 2, :], us[:, t % RING, :], ACT.Copy).then_inc(early_high, 1)

                def finish(b, t):
                    act.wait_ge(early_done, b * GROUP + (t + 3))
                    act.wait_ge(stored[t % 2], b * 64 + (16 * (t // 2) + 16))
                    nc.scalar.activation(A[:, t % 2, :], B[:, 5 + t % 2, :], ACT.Gelu_apprx_tanh).then_inc(early_gelu, 1)
                    act.wait_ge(early_gelu, b * GROUP + (t + 3))
                    act.dma_start(early[bass.ds(b * GROUP + t, 1)].rearrange("a p n -> (a p) n"), A[:, t % 2, :]
                                  ).then_inc(stored[t % 2], 16)

                def turn(b, more):
                    if more:
                        act.wait_ge(scored, b + 1)
                        copy_queries(b + 1)
                    high_part(b, 0)
                    high_part(b, 1)
                    for t in range(GROUP):
                        if t + 2 < GROUP:
                            high_part(b, t + 2)
                        finish(b, t)
                        if t == GROUP - 2:
                            act.wait_ge(exp_done, b * 2 + 1)
                            nc.scalar.activation(weights, weights, ACT.Exp).then_inc(exp_done, 1)
                    act.wait_ge(turned, b + 1)
                    nc.scalar.activation(chosen[:, :, bass.ds(b * P, P)], B[:, 4, 0:3 * P].rearrange("p (a n) -> p a n", a=3),
                                         ACT.Copy).then_inc(out_done, 1)
                copy_queries(0)
                with act.Fori(0, NB - 1) as b:
                    turn(b, True)
                turn(NB - 1, False)
                for s in stored:
                    act.wait_ge(s, 16 + NB * GROUP // 2 * 16)

            @block.tensor
            def _(pe):
                pe.sem_inc(early_done, 2)

                def score(b):
                    pe.wait_ge(q_block, b + 1)
                    for r in range(SIDES):
                        last = nc.tensor.matmul(B[:, r // 4, (r % 4) * KEYS:(r % 4 + 1) * KEYS], qb[:, r, :], keys[:, r, :],
                                                start=True, stop=True)
                    last.then_inc(scored, 1)

                def turn(b, more):
                    for t in range(GROUP):
                        pe.wait_ge(early_low, b * GROUP + (t + 1 + RING))
                        pe.wait_ge(early_gelu, b * GROUP + (t + 1))
                        for c in range(KD):
                            last = product3(nc, B[:, 5 + t % 2, :], [a[:, t % 2, c * P:(c + 1) * P] for a in (uh, ul)],
                                            [a[:, c, :] for a in hb], c == 0, c == KD - 1)
                        last.then_inc(early_done, 1)
                        if more and t == GROUP // 2 - 1:
                            pe.wait_ge(v, b * STEPS + 3 * SIDES)
                            score(b + 1)
                    pe.wait_ge(v, b * STEPS + STEPS)
                    pe.wait_ge(out_done, b + 1)
                    for j in range(3):
                        last = nc.tensor.transpose(B[:, 4, j * P:(j + 1) * P], picked[:, j, :], k.const("ident"))
                    last.then_inc(turned, 1)
                score(0)
                with pe.Fori(0, NB - 1) as b:
                    turn(b, True)
                turn(NB - 1, False)

            @block.vector
            def _(dve):
                with dve.Fori(0, NB) as b:
                    done = [0]

                    def step(ins):
                        ins.then_inc(v, 1)
                        done[0] += 1

                    def settle():
                        dve.wait_ge(v, b * STEPS + done[0])
                        dve.sem_inc(passed, 1)

                    def sixteen(rows, values, spare_values, top_of, index_of):
                        for r in range(rows):
                            step(nc.vector.max(top_of(r)[:, 0:8], values(r)))
                        settle()
                        for r in range(rows):
                            step(nc.vector.max_index(index_of(r)[:, 0:8], top_of(r)[:, 0:8], values(r)))
                            step(nc.vector.match_replace(spare_values(r), top_of(r)[:, 0:8], values(r), LOW))
                        settle()
                        for r in range(rows):
                            step(nc.vector.max(top_of(r)[:, 8:16], spare_values(r)))
                        settle()
                        for r in range(rows):
                            step(nc.vector.max_index(index_of(r)[:, 8:16], top_of(r)[:, 8:16], spare_values(r)))
                        settle()
                    dve.wait_ge(scored, b + 1)
                    dve.sem_inc(passed, 1)
                    sixteen(SIDES, lambda r: B[:, r // 4, (r % 4) * KEYS:(r % 4 + 1) * KEYS], lambda r: rest[:, r, :],
                            lambda r: top[:, r, :], lambda r: idx[:, r, :])
                    step(nc.vector.tensor_copy(idxf[:], idx[:]))
                    square = [P, H, TOPK, TOPK]
                    step(nc.vector.tensor_tensor(cand[:].rearrange("p h (a c) -> p h a c", a=TOPK),
                                                 top[:, 0::2, :].unsqueeze(3).to_broadcast(square),
                                                 top[:, 1::2, :].unsqueeze(2).to_broadcast(square), ALU.add))
                    settle()
                    sixteen(H, lambda r: cand[:, r, :], lambda r: crest[:, r, :], lambda r: best[:, r, :], lambda r: pos[:, r, :])
                    dve.wait_ge(out_done, b + 1)
                    nc.vector.tensor_tensor(weights, best[:], best[:, :, 0:1].to_broadcast([P, H, TOPK]), ALU.subtract
                                            ).then_inc(exp_done, 1)
                    pos_f = pos[:].rearrange("p h n -> p (h n)")
                    step(nc.vector.tensor_scalar(parts[:, 0, :], pos_f, 4, None, ALU.logical_shift_right))
                    step(nc.vector.tensor_scalar(parts[:, 1, :], pos_f, 15, None, ALU.bitwise_and))
                    settle()
                    step(nc.vector.tensor_copy(partsf[:], parts[:]))
                    settle()
                    for side in range(2):
                        step(nc.vector.tensor_tensor(hot[:], partsf[:, side, :].unsqueeze(2).to_broadcast([P, P, TOPK]),
                                                     iota16.unsqueeze(1).to_broadcast([P, P, TOPK]), ALU.is_equal))
                        settle()
                        h4 = hot[:].rearrange("p (h n) a -> p h n a", h=H)
                        step(nc.vector.tensor_tensor(h4, h4, idxf[:, side::2, :].unsqueeze(2).to_broadcast(square), ALU.mult))
                        settle()
                        step(nc.vector.tensor_reduce(picked[:, side, :], hot[:], AX, ALU.add))
                        settle()
                    dve.wait_ge(exp_done, b * 2 + 2)
                    step(nc.vector.tensor_reduce(total[:], weights, AX, ALU.add))
                    settle()
                    step(nc.vector.reciprocal(total[:], total[:]))
                    settle()
                    step(nc.vector.tensor_tensor(weights, weights, total[:].unsqueeze(2).to_broadcast([P, H, TOPK]), ALU.mult))
                    assert done[0] == STEPS, done


def spread_phase(k, name, chosen, w_dram):
    nc = k.nc
    B = k.banks
    T = 4
    hot_done, product, copied = k.sems(name, "hot_done product copied")
    stored = k.sems(name, "stored0 stored1")
    with ExitStack() as ctx:
        def sb(n, shape):
            return ctx.enter_context(nc.sbuf_tensor(f"{name}_{n}", shape, F32))
        cols, rws = sb("cols", [P, 2, T, P]), sb("rows", [P, 2, T, P])
        out = [sb(f"out{i}", [P, KEYS, P]) for i in range(2)]
        iota = k.const("iota")
        turns = P // (2 * T)
        with nc.Block() as block:
            @block.vector
            def _(dve):
                for b in range(NB):
                    with dve.Fori(0, turns) as i:
                        for j in range(2):
                            dve.wait_ge(product, b * 2 * turns + i * 2 + (j + 1))
                            four = bass.ds(b * P + i * 2 * T + j * T, T)
                            nc.vector.tensor_tensor(cols[:, j], iota.unsqueeze(1).to_broadcast([P, T, P]),
                                                    chosen[:, 1, four].unsqueeze(2).to_broadcast([P, T, P]), ALU.is_equal)
                            for t in range(T):
                                at = bass.ds(b * P + i * 2 * T + (j * T + t), 1)
                                last = nc.vector.tensor_scalar(rws[:, j, t, :], iota, chosen[:, 0, at], chosen[:, 2, at],
                                                               ALU.is_equal, ALU.mult)
                            last.then_inc(hot_done, 1)

            @block.tensor
            def _(pe):
                pe.sem_inc(product, 2)
                for b in range(NB):
                    with pe.Fori(0, turns) as i:
                        for j in range(2):
                            pe.wait_ge(hot_done, b * 2 * turns + i * 2 + (j + 1))
                            pe.wait_ge(copied, b * 2 * turns + i * 2 + (j + 1))
                            for t in range(T):
                                last = nc.tensor.matmul(B[:, j, t * P:(t + 1) * P], cols[:, j, t, :], rws[:, j, t, :],
                                                        start=True, stop=True)
                            last.then_inc(product, 1)

            @block.scalar
            def _(act):
                act.sem_inc(copied, 2)
                for b in range(NB):
                    if b >= 2:
                        act.wait_ge(stored[b % 2], 64)
                    with act.Fori(0, turns) as i:
                        for j in range(2):
                            act.wait_ge(product, b * 2 * turns + i * 2 + (j + 3))
                            nc.scalar.activation(out[b % 2][:, :, bass.ds(i * 2 * T + j * T, T)],
                                                 B[:, j, :].rearrange("p (t n) -> p n t", t=T), ACT.Copy).then_inc(copied, 1)

            @block.sync
            def _(sp):
                for b in range(NB):
                    sp.wait_ge(copied, 2 + (b + 1) * 2 * turns)
                    for part in range(4):
                        r = slice(part * 32, (part + 1) * 32)
                        sp.dma_start(w_dram[r, :, b * P:(b + 1) * P].rearrange("i j n -> j i n"), out[b % 2][:, r, :]
                                     ).then_inc(stored[b % 2], 16)
                for s in stored:
                    sp.wait_ge(s, 128)


def expert_phase(k, name, hb, u, v, w_dram, early, acc):
    nc = k.nc
    B = k.banks
    G, SET, LAG = GROUP, GROUP // 2, 2
    TURNS, EARLY = KEYS // G, early.shape[0] // G
    (u_done, gelu, a_full, a_high, a_ready, v_done, added, u_high, u_low, v_high, v_low) = k.sems(
        name, "u_done gelu a_full a_high a_ready v_done added u_high u_low v_high v_low")
    u_in, w_in = (k.sems(name, " ".join(f"{n}_in{r}" for r in range(RING))) for n in "uw")
    v_in = k.sems(name, "v_in0 v_in1")
    with ExitStack() as ctx:
        def sb(n, shape, dt=F32):
            return ctx.enter_context(nc.sbuf_tensor(f"{name}_{n}", shape, dt))
        us, ws, vs = sb("us", [P, RING, KD * P]), sb("ws", [P, RING, SEQ]), sb("vs", [P, 2, D])
        uh, ul = sb("uh", [P, 2, KD * P], F32R), sb("ul", [P, 2, KD * P], F32R)
        vh, vl = sb("vh", [P, G, D], F32R), sb("vl", [P, G, D], F32R)
        A = sb("A", [P, 2, SEQ])
        ah, al = sb("ah", [P, G, SEQ], F32R), sb("al", [P, G, SEQ], F32R)

        def run(engine, early_turn, turn, end):
            for t in range(G):
                early_turn(0, t, True)
            with engine.Fori(1, EARLY) as g:
                for t in range(G):
                    early_turn(g, t, False)
            with engine.Fori(EARLY, TURNS) as g:
                for t in range(G):
                    turn(g, t, False)
            end()

        def lagging(part, g, t, first):
            if t >= LAG:
                part(g, t - LAG)
            elif not first:
                part(g - 1, t - LAG + G)

        def last_lagging(part):
            for t in range(G - LAG, G):
                part(TURNS - 1, t)

        with nc.Block() as block:
            @block.sync
            def _(sp):
                def others(g, t):
                    sp.wait_ge(a_ready, g * G + (t + 1))
                    sp.dma_start(ws[:, t % RING, :], w_dram[bass.ds(g * G + t, 1)].rearrange("a p n -> (a p) n")
                                 ).then_inc(w_in[t % RING], 16)
                    sp.wait_ge(v_low, g * G + (t + 1))
                    sp.dma_start(vs[:, t % 2, :], v[bass.ds((g * G + t) * P, P), :]).then_inc(v_in[t % 2], 16)

                def early_turn(g, t, first):
                    sp.wait_ge(u_low, g * G + (t + 1))
                    sp.dma_start(us[:, t % RING, 0:SEQ], early[bass.ds(g * G + t, 1)].rearrange("a p n -> (a p) n")
                                 ).then_inc(u_in[t % RING], 16)
                    lagging(others, g, t, first)

                def turn(g, t, first):
                    sp.wait_ge(u_low, g * G + (t + 1))
                    sp.dma_start(us[:, t % RING, :], u[bass.ds(g * G + t, 1)].rearrange("a p n -> (a p) n")
                                 ).then_inc(u_in[t % RING], 16)
                    lagging(others, g, t, first)
                run(sp, early_turn, turn, lambda: last_lagging(others))

            @block.tensor
            def _(pe):
                pe.sem_inc(u_done, 2 + EARLY * G)
                pe.sem_inc(v_done, 2 * KD)

                def v_part(g, s, c):
                    if c == 0:
                        pe.wait_ge(v_low, g * G + (s * SET + SET + 2))
                        pe.wait_ge(a_ready, g * G + (s * SET + SET + RING))
                    pe.wait_ge(added, g * 2 * KD + (s * KD + c + 1))
                    for j in range(SET):
                        t = s * SET + j
                        last = product3(nc, B[:, 4 + c % 4, :], [a[:, t, c * P:(c + 1) * P] for a in (vh, vl)],
                                        [a[:, t, :] for a in (ah, al)], j == 0, j == SET - 1)
                    last.then_inc(v_done, 1)

                def v_parts(g, t, first):
                    for c in (2 * (t % SET), 2 * (t % SET) + 1):
                        if t >= SET:
                            v_part(g, 0, c)
                        elif not first:
                            v_part(g - 1, 1, c)

                def turn(g, t, first):
                    pe.wait_ge(u_low, g * G + (t + 1 + RING))
                    pe.wait_ge(gelu, g * G + (t + 1))
                    for c in range(KD):
                        last = product3(nc, B[:, t % RING, :], [a[:, t % 2, c * P:(c + 1) * P] for a in (uh, ul)],
                                        [a[:, c, :] for a in hb], c == 0, c == KD - 1)
                    last.then_inc(u_done, 1)
                    v_parts(g, t, first)

                def end():
                    for c in range(KD):
                        v_part(TURNS - 1, 1, c)
                run(pe, v_parts, turn, end)

            @block.scalar
            def _(act):
                act.sem_inc(gelu, RING + EARLY * G)
                act.sem_inc(u_high, EARLY * G)

                def split(g, t):
                    act.wait_ge(a_full, g * G + (t + 1))
                    act.wait_ge(v_done, g * 2 * KD + (t // SET * KD + KD))
                    nc.scalar.activation(ah[:, t, :], A[:, t % 2, :], ACT.Copy).then_inc(a_high, 1)
                    act.wait_ge(v_in[t % 2], g * 64 + (16 * (t // 2) + 16))
                    nc.scalar.activation(vh[:, t, :], vs[:, t % 2, :], ACT.Copy).then_inc(v_high, 1)

                def others(g, t):
                    act.wait_ge(u_done, g * G + (t + 3))
                    act.wait_ge(a_ready, g * G + (t + 3))
                    nc.scalar.activation(A[:, t % 2, :], B[:, t % RING, :], ACT.Gelu_apprx_tanh).then_inc(gelu, 1)
                    split(g, t)

                def turn(g, first):
                    for t in range(G):
                        act.wait_ge(u_in[t % RING], g * 32 + (16 * (t // RING) + 16))
                        act.wait_ge(u_done, g * G + (t + 1))
                        nc.scalar.activation(uh[:, t % 2, :], us[:, t % RING, :], ACT.Copy).then_inc(u_high, 1)
                        lagging(others, g, t, first)
                with act.Fori(0, EARLY) as g:
                    for t in range(G):
                        split(g, t)
                turn(EARLY, True)
                with act.Fori(EARLY + 1, TURNS) as g:
                    turn(g, False)
                last_lagging(others)

            @block.gpsimd
            def _(pool):
                pool.sem_inc(u_low, RING)
                pool.sem_inc(v_low, 2)

                def others(g, t):
                    pool.wait_ge(v_high, g * G + (t + 1))
                    nc.gpsimd.tensor_tensor(vl[:, t, :], vs[:, t % 2, :], vh[:, t, :].bitcast(F32), ALU.subtract
                                            ).then_inc(v_low, 1)

                def early_turn(g, t, first):
                    lagging(others, g, t, first)
                    pool.wait_ge(a_full, g * G + (t + 1))
                    pool.sem_inc(u_low, 1)

                def turn(g, t, first):
                    pool.wait_ge(u_high, g * G + (t + 1))
                    nc.gpsimd.tensor_tensor(ul[:, t % 2, :], us[:, t % RING, :], uh[:, t % 2, :].bitcast(F32), ALU.subtract
                                            ).then_inc(u_low, 1)
                    lagging(others, g, t, first)
                run(pool, early_turn, turn, lambda: last_lagging(others))

            @block.vector
            def _(dve):
                dve.sem_inc(a_ready, RING)
                dve.sem_inc(added, 4)

                def add(g, s, c, first):
                    dve.wait_ge(v_done, g * 2 * KD + (s * KD + c + 1 + 2 * KD))
                    if not first:
                        dve.wait_ge(added, g * 2 * KD + (s * KD + c - 3))
                    nc.vector.tensor_tensor(acc[:, c, :], acc[:, c, :], B[:, 4 + c % 4, :], ALU.add).then_inc(added, 1)

                def low_and_adds(g, t, first):
                    dve.wait_ge(a_high, g * G + (t + 1))
                    nc.vector.tensor_tensor(al[:, t, :], A[:, t % 2, :], ah[:, t, :].bitcast(F32), ALU.subtract
                                            ).then_inc(a_ready, 1)
                    for c in (2 * (t % SET), 2 * (t % SET) + 1):
                        if t >= SET:
                            add(g, 0, c, first)
                        elif not first:
                            add(g - 1, 1, c, False)

                def early_turn(g, t, first):
                    dve.wait_ge(u_in[t % RING], g * 32 + (16 * (t // RING) + 16))
                    dve.wait_ge(w_in[t % RING], g * 32 + (16 * (t // RING) + 16))
                    dve.wait_ge(a_ready, g * G + (t + 3))
                    nc.vector.tensor_tensor(A[:, t % 2, :], us[:, t % RING, 0:SEQ], ws[:, t % RING, :], ALU.mult
                                            ).then_inc(a_full, 1)
                    low_and_adds(g, t, first)

                def turn(g, t, first):
                    dve.wait_ge(gelu, g * G + (t + 1 + RING))
                    dve.wait_ge(w_in[t % RING], g * 32 + (16 * (t // RING) + 16))
                    nc.vector.tensor_tensor(A[:, t % 2, :], A[:, t % 2, :], ws[:, t % RING, :], ALU.mult).then_inc(a_full, 1)
                    low_and_adds(g, t, first)

                def end():
                    for c in range(KD):
                        add(TURNS - 1, 1, c, False)
                run(dve, early_turn, turn, end)


def keys_values_phase(k, name, x, w_dram, key, value):
    nc = k.nc
    B = k.banks
    done, out, high_done, low_done = k.sems(name, "done out high_done low_done")
    w_in = k.sems(name, "w_in0 w_in1")
    W = 2 * P
    PARTS = w_dram.shape[2] // W
    with ExitStack() as ctx:
        raw = ctx.enter_context(nc.sbuf_tensor(f"{name}_raw", [P, 2, KD, W], F32))
        w = [ctx.enter_context(nc.sbuf_tensor(f"{name}_{n}", [P, 2, KD, W], F32R)) for n in ("high", "low")]
        with nc.Block() as block:
            @block.sync
            def _(sp):
                for j in range(PARTS):
                    if j >= 2:
                        sp.wait_ge(low_done, j - 1)
                    sp.dma_start(raw[:, j % 2], w_dram[:, :, j * W:(j + 1) * W]).then_inc(w_in[j % 2], 16)

            @block.vector
            def _(dve):
                for j in range(PARTS):
                    dve.wait_ge(w_in[j % 2], 16 * (j // 2) + 16)
                    if j >= 2:
                        dve.wait_ge(done, j)
                    nc.vector.tensor_copy(w[0][:, j % 2], raw[:, j % 2]).then_inc(high_done, 1)
                    dve.wait_ge(high_done, j + 1)
                    nc.vector.tensor_tensor(w[1][:, j % 2], raw[:, j % 2], w[0][:, j % 2].bitcast(F32), ALU.subtract
                                            ).then_inc(low_done, 1)

            @block.tensor
            def _(pe):
                pe.wait_ge(low_done, 1)
                for c in range(KD):
                    last = product3(nc, B[:, 0, :], [a[:, 0, c, 0:P] for a in w], [a[:, c, :] for a in x], c == 0, c == KD - 1)
                last.then_inc(done, 1)
                for j in range(PARTS):
                    pe.wait_ge(low_done, j + 1)
                    n, a0 = (P, P) if j == 0 else (W, 0)
                    for b in range(NB):
                        for c in range(KD):
                            to = B[:, 1 + 2 * j + b // 2, (b % 2) * n:(b % 2) * n + n]
                            last = product3(nc, to, [a[:, c, b * P:(b + 1) * P] for a in x],
                                            [a[:, j % 2, c, a0:a0 + n] for a in w], c == 0, c == KD - 1)
                    last.then_inc(done, 1)

            @block.scalar
            def _(act):
                act.wait_ge(done, 1)
                nc.scalar.activation(key[:], B[:, 0, :], ACT.Copy).then_inc(out, 1)
                for j in range(PARTS):
                    act.wait_ge(done, j + 2)
                    n, at = (P, 0) if j == 0 else (W, P + (j - 1) * W)
                    for half in range(2):
                        nc.scalar.activation(value[:, 2 * half:2 * half + 2, at:at + n],
                                             B[:, 1 + 2 * j + half, 0:2 * n].rearrange("p (b n) -> p b n", b=2), ACT.Copy
                                             ).then_inc(out, 1)


def token_mixers_phase(k, name, q, key, value, sinks, out, rq, rkey, gate, rout):
    nc = k.nc
    B = k.banks
    SC, R_SC = A_HD ** -0.5, P ** -0.5
    (q_tile, scored, masked, max_done, exp_done, inv, normed, turned, turned_out, o_done, o_out, sunk) = k.sems(
        name, "q_tile scored masked max_done exp_done inv normed turned turned_out o_done o_out sunk")
    (rotated, cosd, sind, pair, outer, inner_done, att_ready, kz_turned, kz_copied, kv_done, state, v_head, ro_done, ro_out,
     mean_done, centred, squared, var_done, root, r_inv, r_normed, final) = k.sems(
        name, "rotated cosd sind pair outer inner_done att_ready kz_turned kz_copied kv_done state v_head ro_done ro_out "
              "mean_done centred squared var_done root r_inv r_normed final")
    UNITS = [(kv, b) for b in range(NB) for kv in range(KV_HEADS)]
    N = len(UNITS)
    assert R_HEADS == A_HEADS // KV_HEADS
    with ExitStack() as ctx:
        def sb(n, shape):
            return ctx.enter_context(nc.sbuf_tensor(f"{name}_{n}", shape, F32))
        qt = sb("qt", [P, SEQ])
        sc, pr, pt = sb("sc", [P, 2, 1 + 2 * P]), sb("pr", [P, 2, 1 + 2 * P]), sb("pt", [P, 2, 2 * P])
        nmax, total, rinv = sb("nmax", [P, N]), sb("total", [P, N]), sb("rinv", [P, N])
        tc, ts = sb("tc", [P, 2, SEQ]), sb("ts", [P, 2, SEQ])
        qp, kp, qx, kz = (sb(n, [P, SEQ]) for n in ("qp", "kp", "qx", "kz"))
        att, kzt, vh = sb("att", [P, SEQ]), sb("kzt", [P, SEQ]), sb("vh", [P, NB, P])
        S = sb("S", [P, NB, P])
        o, cent, sq, std, eps = sb("o", [P, SEQ]), sb("cent", [P, SEQ]), sb("sq", [P, SEQ]), sb("std", [P, SEQ]), sb("eps", [P, 1])
        band, ident = k.const("band"), k.const("ident")
        cos, sin, ones = k.const("cos"), k.const("sin"), k.const("ones")
        blocks = "p (b n) -> p b n"

        def width(b):
            return 2 * P if b else P

        def head(a, h):
            return a[:, bass.ds(h, 1), :].rearrange("p a n -> p (a n)")

        def table(name, h):
            a, _ = CONST2_AT[name]
            return k.consts2[:, bass.ds(h * P + a, P)].unsqueeze(1).to_broadcast([P, NB, P])

        def block(b):
            return slice(b * P, (b + 1) * P)
        with nc.Block() as program:
            @program.gpsimd
            def _(pool):
                with pool.Fori(0, R_HEADS) as t:
                    pool.wait_ge(scored, t * N + 1)
                    nc.gpsimd.tensor_copy(qt[:], head(q, t)).then_inc(q_tile, 1)
                    pool.wait_ge(final, t + 1)
                    nc.gpsimd.tensor_copy(vh[:], value[:, :, bass.ds(t * P + P, P)]).then_inc(v_head, 1)

            @program.tensor
            def _(pe):
                pe.sem_inc(scored, 1)
                with pe.Fori(0, R_HEADS) as t:
                    def scores(u):
                        kv, b = UNITS[u]
                        r = slice(kv * A_HD, kv * A_HD + A_HD)
                        pe.wait_ge(masked, t * N + u + 1)
                        nc.tensor.matmul(B[:, u % 2, 0:width(b)], qt[r, block(b)],
                                         key[r, max(b - 1, 0) * P:(b + 1) * P], start=True, stop=True).then_inc(scored, 1)

                    def turn(u):
                        kv, b = UNITS[u]
                        pe.wait_ge(normed, t * N + u + 1)
                        if u >= 2:
                            pe.wait_ge(turned_out, t * N + u - 1)
                        for j in range(width(b) // P):
                            last = nc.tensor.transpose(B[:, 2 + u % 2, block(j)], pr[:, u % 2, 1 + j * P:1 + (j + 1) * P], ident)
                        last.then_inc(turned, 1)

                    def mix(u):
                        kv, b = UNITS[u]
                        pe.wait_ge(turned_out, t * N + u + 1)
                        if u < 1:
                            pe.wait_ge(o_out, t + 1)
                        n = width(b) // P
                        for j in range(n):
                            last = nc.tensor.matmul(B[kv * A_HD:kv * A_HD + A_HD, 4, block(b)],
                                                    value[:, b - n + 1 + j, kv * A_HD:kv * A_HD + A_HD],
                                                    pt[:, u % 2, block(j)], start=(j == 0), stop=(j == n - 1))
                        last.then_inc(o_done, 1)

                    def ret_rotate():
                        pe.wait_ge(root, t + 1)
                        nc.tensor.matmul(B[:, 5, :], k.const("rot"), head(rq, t), start=True, stop=True)
                        nc.tensor.matmul(B[:, 6, :], k.const("rot"), head(rkey, t), start=True, stop=True).then_inc(rotated, 1)

                    def ret_inner():
                        pe.wait_ge(pair, t * 2 + 2)
                        for b in range(NB):
                            last = nc.tensor.matmul(B[:, 7, block(b)], kp[:, block(b)], qp[:, block(b)], start=True, stop=True)
                        last.then_inc(inner_done, 1)
                        pe.wait_ge(outer, t * 2 + 2)
                        for b in range(NB):
                            last = nc.tensor.transpose(B[:, 5, block(b)], kz[:, block(b)], ident)
                        last.then_inc(kz_turned, 1)

                    def ret_keys_values():
                        pe.wait_ge(kz_copied, t + 1)
                        pe.wait_ge(v_head, t + 1)
                        for b in range(NB - 1):
                            last = nc.tensor.matmul(B[:, 6, block(b)], kzt[:, block(b)], vh[:, b, :], start=True, stop=True)
                        last.then_inc(kv_done, 1)

                    def ret_out():
                        pe.wait_ge(att_ready, t + 1)
                        for b in range(NB):
                            last = nc.tensor.matmul(B[:, 7, block(b)], vh[:, b, :], att[:, block(b)], start=True, stop=(b == 0))
                            if b:
                                pe.wait_ge(state, t * 3 + b)
                                last = nc.tensor.matmul(B[:, 7, block(b)], S[:, b, :], qx[:, block(b)], start=False, stop=True)
                        last.then_inc(ro_done, 1)

                    def ret_mean():
                        pe.wait_ge(ro_out, t + 1)
                        nc.tensor.matmul(B[:, 5, :], ones, o[:], start=True, stop=True).then_inc(mean_done, 1)

                    def ret_variance():
                        pe.wait_ge(squared, t + 1)
                        nc.tensor.matmul(B[:, 6, :], ones, sq[:], start=True, stop=True).then_inc(var_done, 1)
                    between = {0: ret_inner, 2: ret_keys_values, 3: ret_out, 4: ret_mean, 5: ret_variance}
                    ret_rotate()
                    pe.wait_ge(q_tile, t + 1)
                    scores(0)
                    scores(1)
                    for u in range(N):
                        turn(u)
                        if u + 2 < N:
                            scores(u + 2)
                        if u:
                            mix(u - 1)
                        if u in between:
                            between[u]()
                    mix(N - 1)

            @program.vector
            def _(dve):
                dve.sem_inc(masked, 2)
                nc.vector.memset(eps[:], EPS).then_inc(final, 1)
                with dve.Fori(0, R_HEADS) as t:
                    def scale(u):
                        dve.wait_ge(exp_done, t * N + u + 1)
                        nc.vector.reciprocal(rinv[:, u:u + 1], total[:, u:u + 1]).then_inc(inv, 1)
                        dve.wait_ge(inv, t * N + u + 1)
                        n = 1 + width(UNITS[u][1])
                        nc.vector.tensor_scalar(pr[:, u % 2, 0:n], pr[:, u % 2, 0:n], rinv[:, u:u + 1], None, ALU.mult
                                                ).then_inc(normed, 1)

                    def ret_rotate():
                        for i, (x, s) in enumerate(((rq, 1.0), (rkey, R_SC))):
                            nc.vector.scalar_tensor_tensor(tc[:, i, :], head(x, t), s, cos, ALU.mult, ALU.mult).then_inc(cosd, 1)
                        dve.wait_ge(rotated, t + 1)
                        for i, s in enumerate((1.0, R_SC)):
                            nc.vector.scalar_tensor_tensor(ts[:, i, :], B[:, 5 + i, :], s, sin, ALU.mult, ALU.mult).then_inc(sind, 1)
                        dve.wait_ge(cosd, t * 2 + 2)
                        dve.wait_ge(sind, t * 2 + 2)
                        for i, to in enumerate((qp, kp)):
                            nc.vector.tensor_tensor(to[:], tc[:, i, :], ts[:, i, :], ALU.add).then_inc(pair, 1)
                        dve.wait_ge(pair, t * 2 + 2)
                        for to, x, by in ((kz, kp, "zeta"), (qx, qp, "xi")):
                            nc.vector.tensor_tensor(to[:].rearrange(blocks, b=NB), x[:].rearrange(blocks, b=NB), table(by, t), ALU.mult
                                                    ).then_inc(outer, 1)

                    def ret_inner():
                        dve.wait_ge(inner_done, t + 1)
                        nc.vector.tensor_tensor(att[:].rearrange(blocks, b=NB), B[:, 7, :].rearrange(blocks, b=NB),
                                                table("dintra", t), ALU.mult).then_inc(att_ready, 1)

                    def ret_states():
                        dve.wait_ge(kv_done, t + 1)
                        nc.vector.tensor_copy(S[:, 1, :], B[:, 6, 0:P]).then_inc(state, 1)
                        for b in (2, 3):
                            dve.wait_ge(state, t * 3 + b - 1)
                            decay = k.consts2[:, bass.ds(t + CONST2_AT["decay"][0], 1)]
                            nc.vector.scalar_tensor_tensor(S[:, b, :], S[:, b - 1, :], decay, B[:, 6, block(b - 1)],
                                                           ALU.mult, ALU.add).then_inc(state, 1)

                    def ret_centre():
                        dve.wait_ge(mean_done, t + 1)
                        nc.vector.scalar_tensor_tensor(cent[:], B[:, 5, :], -1.0 / P, o[:], ALU.mult, ALU.add).then_inc(centred, 1)

                    def ret_finish():
                        dve.wait_ge(root, t + 2)
                        nc.vector.reciprocal(std[:], std[:]).then_inc(r_inv, 1)
                        dve.wait_ge(r_inv, t + 1)
                        nc.vector.tensor_tensor(cent[:], cent[:], std[:], ALU.mult).then_inc(r_normed, 1)
                        dve.wait_ge(r_normed, t + 1)
                        nc.vector.tensor_tensor(head(rout, t), cent[:], head(gate, t), ALU.mult).then_inc(final, 1)
                    after = {0: ret_rotate, 2: ret_inner, 4: ret_states, 6: ret_centre}
                    for u, (kv, b) in enumerate(UNITS):
                        n = width(b)
                        if u >= 2:
                            scale(u - 2)
                        nc.vector.tensor_copy(sc[:, u % 2, 0:1], sinks[:, bass.ds(t + 4 * kv, 1)]).then_inc(sunk, 1)
                        dve.wait_ge(scored, t * N + u + 2)
                        nc.vector.scalar_tensor_tensor(sc[:, u % 2, 1:1 + n], B[:, u % 2, 0:n], SC, band[:, 2 * P - n:2 * P],
                                                       ALU.mult, ALU.add).then_inc(masked, 1)
                        dve.wait_ge(sunk, t * N + u + 1)
                        dve.wait_ge(masked, t * N + u + 3)
                        nc.vector.tensor_reduce(nmax[:, u:u + 1], sc[:, u % 2, 0:1 + n], AX, ALU.max, negate=True
                                                ).then_inc(max_done, 1)
                        if u in after:
                            after[u]()
                    scale(N - 2)
                    scale(N - 1)
                    ret_finish()

            @program.scalar
            def _(act):
                act.sem_inc(o_out, 1)
                act.sem_inc(root, 1)
                with act.Fori(0, R_HEADS) as t:
                    def copy_turned(u):
                        n = width(UNITS[u][1])
                        act.wait_ge(turned, t * N + u + 1)
                        if u >= 2:
                            act.wait_ge(o_done, t * N + u - 1)
                        nc.scalar.activation(pt[:, u % 2, 0:n], B[:, 2 + u % 2, 0:n], ACT.Copy).then_inc(turned_out, 1)

                    def ret_keys():
                        act.wait_ge(kz_turned, t + 1)
                        nc.scalar.activation(kzt[:], B[:, 5, :], ACT.Copy).then_inc(kz_copied, 1)

                    def ret_out():
                        act.wait_ge(ro_done, t + 1)
                        nc.scalar.activation(o[:], B[:, 7, :], ACT.Copy).then_inc(ro_out, 1)

                    def ret_square():
                        act.wait_ge(centred, t + 1)
                        nc.scalar.activation(sq[:], cent[:], ACT.Square).then_inc(squared, 1)

                    def ret_root():
                        act.wait_ge(var_done, t + 1)
                        nc.scalar.activation(std[:], B[:, 6, :], ACT.Sqrt, bias=eps[:, 0:1], scale=1.0 / P).then_inc(root, 1)
                    after = {2: ret_keys, 5: ret_out, 6: ret_square, 7: ret_root}
                    for u, (kv, b) in enumerate(UNITS):
                        n = 1 + width(b)
                        if u >= 2:
                            copy_turned(u - 2)
                        act.wait_ge(max_done, t * N + u + 1)
                        nc.scalar.activation(pr[:, u % 2, 0:n], sc[:, u % 2, 0:n], ACT.Exp, bias=nmax[:, u:u + 1],
                                             accum_out=total[:, u:u + 1]).then_inc(exp_done, 1)
                        if u in after:
                            after[u]()
                    copy_turned(N - 2)
                    copy_turned(N - 1)
                    act.wait_ge(o_done, t * N + N)
                    nc.scalar.activation(head(out, t), B[:, 4, :], ACT.Copy).then_inc(o_out, 1)


def gated_conv_phase(k, name, x, w_dram, taps, y):
    nc = k.nc
    B = k.banks
    product, tap, gelu, y_full, y_high, y_done, high_done, low_done = k.sems(
        name, "product tap gelu y_full y_high y_done high_done low_done")
    w_in = k.sems(name, "w_in0 w_in1 w_in2 w_in3")
    with ExitStack() as ctx:
        def sb(n, shape, dt=F32):
            return ctx.enter_context(nc.sbuf_tensor(f"{name}_{n}", shape, dt))
        raw = sb("raw", [P, RING, KD * P])
        w = [sb(n, [P, 2, KD * P], F32R) for n in ("high", "low")]
        conv, ge = sb("conv", [P, RING, SEQ]), sb("ge", [P, 2, SEQ])
        with nc.Block() as block:
            @block.sync
            def _(sp):
                with sp.Fori(0, 2 * FT // RING) as g:
                    for r in range(RING):
                        sp.wait_ge(low_done, g * RING + (r + 1))
                        sp.dma_start(raw[:, r, :], w_dram[bass.ds(g * RING + r, 1)].rearrange("a p n -> (a p) n")).then_inc(w_in[r], 16)

            @block.tensor
            def _(pe):
                pe.sem_inc(product, 2)
                with pe.Fori(0, 2 * FT // RING) as g:
                    for r in range(RING):
                        pe.wait_ge(low_done, g * RING + (r + 1 + RING))
                        pe.wait_ge(tap, g * 3 * RING + (3 * r + 3))
                        for c in range(KD):
                            last = product3(nc, B[:, r, :], [a[:, r % 2, c * P:(c + 1) * P] for a in w], [a[:, c, :] for a in x],
                                            c == 0, c == KD - 1)
                        last.then_inc(product, 1)

            @block.vector
            def _(dve):
                dve.sem_inc(tap, 3 * RING)
                dve.sem_inc(y_done, 2)
                with dve.Fori(0, 2 * FT // RING) as g:
                    for r in range(RING):
                        dve.wait_ge(product, g * RING + (r + 3))
                        dve.wait_ge(y_done, g * 2 + (r // 2 + 1))
                        to, a = conv[:, r, :], B[:, r, :]

                        def weight(j):
                            return taps[:, bass.ds(g * RING + r, 1), j:j + 1].rearrange("p a n -> p (a n)")
                        nc.vector.tensor_scalar(to, a, weight(2), weight(3), ALU.mult, ALU.add).then_inc(tap, 1)
                        for s in (1, 2):
                            dve.wait_ge(tap, g * 3 * RING + (3 * r + s + 3 * RING))
                            nc.vector.scalar_tensor_tensor(to[:, s:SEQ], a[:, 0:SEQ - s], weight(2 - s), to[:, s:SEQ],
                                                           ALU.mult, ALU.add).then_inc(tap, 1)
                        if r % 2 == 1:
                            dve.wait_ge(gelu, g * 2 + (r // 2 + 1))
                            dve.wait_ge(tap, g * 3 * RING + (3 * r + 3 + 3 * RING))
                            nc.vector.tensor_tensor(conv[:, r, :], ge[:, r // 2, :], conv[:, r, :], ALU.mult).then_inc(y_full, 1)
                            dve.wait_ge(y_high, g * 2 + (r // 2 + 1))
                            high, low = (a[:, bass.ds(g * 2 + r // 2, 1), :].rearrange("p a n -> p (a n)") for a in y)
                            nc.vector.tensor_tensor(low, conv[:, r, :], high.bitcast(F32), ALU.subtract).then_inc(y_done, 1)

            @block.gpsimd
            def _(pool):
                pool.sem_inc(low_done, RING)
                with pool.Fori(0, 2 * FT // RING) as g:
                    for r in range(RING):
                        pool.wait_ge(high_done, g * RING + (r + 1))
                        nc.gpsimd.tensor_tensor(w[1][:, r % 2, :], raw[:, r, :], w[0][:, r % 2, :].bitcast(F32), ALU.subtract
                                                ).then_inc(low_done, 1)

            @block.scalar
            def _(act):
                def split(g, r):
                    act.wait_ge(w_in[r], g * 16 + 16)
                    act.wait_ge(product, g * RING + (r + 1))
                    nc.scalar.activation(w[0][:, r % 2, :], raw[:, r, :], ACT.Copy).then_inc(high_done, 1)
                def gelu_part(g, f):
                    act.wait_ge(tap, g * 3 * RING + (6 * f + 3 + 3 * RING))
                    act.wait_ge(y_done, g * 2 + (f + 1))
                    nc.scalar.activation(ge[:, f, :], conv[:, 2 * f, :], ACT.Gelu_apprx_tanh).then_inc(gelu, 1)

                def high_part(g, f):
                    act.wait_ge(y_full, g * 2 + (f + 1))
                    nc.scalar.activation(y[0][:, bass.ds(g * 2 + f, 1), :].rearrange("p a n -> p (a n)"), conv[:, 2 * f + 1, :],
                                         ACT.Copy).then_inc(y_high, 1)

                def turn(g, first):
                    for r in range(RING):
                        split(g, r)
                        if r < 2 and first:
                            continue
                        part = high_part if r % 2 else gelu_part
                        part(g, 0) if r >= 2 else part(g - 1, 1)
                turn(0, True)
                with act.Fori(1, 2 * FT // RING) as g:
                    turn(g, False)
                gelu_part(2 * FT // RING - 1, 1)
                high_part(2 * FT // RING - 1, 1)


def tiled(w, width=P):
    kk, m = w.shape
    return np.ascontiguousarray(w.reshape(kk // P, P, m // width, width).transpose(2, 1, 0, 3)).reshape(m // width, P, -1)


def rows(w):
    return np.ascontiguousarray(w.reshape(-1, P, w.shape[1]).transpose(1, 0, 2))


def column(v):
    return np.ascontiguousarray(v.reshape(-1, P).T)


def layout(a):
    i = {}
    h0 = np.concatenate([a["meta_tokens"], a["x"][0]], 0)
    i["h0"] = rows(np.ascontiguousarray(h0.T))
    i["consts"], i["consts2"] = constants()
    w = a["w_in"][0]
    cut = np.cumsum([512, 512, 1024, 1024, 16, 2048, 3072, 32, 1024, 1024])
    q, kk, v, g_out, low, z, xbc, dt, ga, gb = np.split(w, cut[:-1], axis=1)
    i["wq"], i["wk"], i["wv"] = tiled(q), tiled(kk), tiled(v, GLA_DV)
    i["w_gout"], i["w_z"], i["w_ga"], i["w_gb"] = tiled(g_out), tiled(z), tiled(ga), tiled(gb)
    i["w_low"], i["w_dt"] = rows(low), rows(dt)
    i["gate_w"] = np.concatenate([a["gla_w_gate2"][0], a["gla_b_gate"]], 0)
    c0 = SSD_GROUPS * 512
    group = [np.concatenate([np.arange(g * 512, (g + 1) * 512), c0 + np.arange(g * P, (g + 1) * P),
                             c0 + 512 + np.arange(g * P, (g + 1) * P)]) for g in range(SSD_GROUPS)]
    order = np.concatenate(group)
    i["w_xbc"] = tiled(xbc[:, order])
    taps = np.concatenate([a["ssd_conv_w"][0], a["ssd_conv_b"]], 0)[:, order]
    i["conv"] = np.ascontiguousarray(taps.reshape(5, SSD_GROUPS, 6, P).transpose(3, 1, 2, 0))
    every = lambda v: np.ascontiguousarray(np.broadcast_to(v, (P, v.shape[-1])))
    i["dt_bias"], i["a_log"] = every(a["ssd_dt_bias"]), every(a["ssd_a_log"])
    i["skip"] = column(np.repeat(a["ssd_d"][0], SSD_HD))
    i["ssd_norm"] = column(a["ssd_norm_w"][0])
    i["w_up_gla"], i["w_up_ssd"], i["w_out"] = tiled(a["w_up_gla"][0]), tiled(a["w_up_ssd"][0]), tiled(a["w_out"][0])
    i["ln_ffn"], i["ln_final"] = column(a["ln_ffn_w"][0]), column(a["ln_final_w"])
    i["w_q"] = tiled(a["peer_w_q"][0])
    i["keys"] = np.ascontiguousarray(a["peer_sub_keys"][0].reshape(2 * PEER_HEADS, KEYS, P).transpose(2, 0, 1))
    i["u"], i["v"] = tiled(a["peer_u"][0].T), a["peer_v"][0]
    w2 = a["w_in_2"][0]
    qa, ka, va, qr, kr, vr, gr = np.split(w2, np.cumsum([512, 128, 128, 512, 512, 512]), axis=1)
    pairs = np.concatenate([np.concatenate([np.arange(t * 64, t * 64 + 64), np.arange((t + 4) * 64, (t + 4) * 64 + 64)])
                            for t in range(4)])
    i["w_qk2"] = tiled(np.concatenate([qa[:, pairs], qr, kr], 1))
    i["w_gr"] = tiled(gr)
    i["w_kv2"] = rows(np.concatenate([ka, va, vr], 1))
    i["sinks"] = every(a["attn_sinks_2"])
    i["w_out2"] = tiled(np.concatenate([a["w_out_2"][0][:512][pairs], a["w_out_2"][0][512:]], 0))
    for n in ("mix_pre_norm_2", "mix_post_norm_2", "ffn_pre_norm_2", "ffn_post_norm_2"):
        i[n] = column(a[n][0])
    both = np.concatenate([np.concatenate([np.arange(f * P, f * P + P), D_FF + np.arange(f * P, f * P + P)]) for f in range(FT)])
    i["w_up2"], i["w_down2"] = tiled(a["w_up_2"][0][:, both]), tiled(a["w_down_2"][0])
    taps2 = np.concatenate([a["conv_w_2"][0], a["conv_b_2"]], 0)[:, both]
    i["taps2"] = np.ascontiguousarray(taps2.reshape(4, 2 * FT, P).transpose(2, 1, 0))
    i["ln_mix"] = column(a["ln_mix_w"][0])
    i["gla_norm"] = column(np.tile(a["gla_norm_w"][0], GLA_HEADS))
    return i


def pair_of(nc, ctx, name, tiles, n):
    return [ctx.enter_context(nc.sbuf_tensor(f"{name}_{part}", [P, tiles, n], F32R)) for part in ("high", "low")]


def first_mixer(k, d, h):
    nc = k.nc
    with ExitStack() as ctx:
        def sb(n, shape):
            return ctx.enter_context(nc.sbuf_tensor(n, shape, F32))
        mixed = sb("mixed", [P, KD, L])
        hn = pair_of(nc, ctx, "hn", KD, L)
        ln_mix, gla_norm, ssd_norm = sb("ln_mix", [P, KD]), sb("gla_norm", [P, KD]), sb("ssd_norm", [P, 2 * KD])
        gate_w, low = sb("gate_w", [GATE_RANK + 1, 512]), sb("low", [GATE_RANK + 1, L])
        with ExitStack() as scan:
            def sb2(n, shape):
                return scan.enter_context(nc.sbuf_tensor(n, shape, F32))
            dt = sb2("dt", [P, NB + 1, SSD_HEADS])
            acum, e_acum, to_end = (sb2(n, [P, NB + 1, SSD_HEADS]) for n in ("acum", "e_acum", "to_end"))
            e_total, e_total_m = sb2("e_total", [P, 2, NB, SSD_HEADS]), sb2("e_total_m", [P, SSD_HEADS])
            dt_bias, a_log = sb2("dt_bias", [P, SSD_HEADS]), sb2("a_log", [P, SSD_HEADS])
            conv, skip = sb2("conv", [P, SSD_GROUPS, 6, 5]), sb2("skip", [P, 2 * KD])
            with ExitStack() as inner:
                hn_full = inner.enter_context(nc.sbuf_tensor("hn_full", [P, KD, L], F32))
                w_low = inner.enter_context(nc.sbuf_tensor("w_low", [P, KD, GATE_RANK], F32))
                w_dt = inner.enter_context(nc.sbuf_tensor("w_dt", [P, KD, SSD_HEADS], F32))
                load_phase(k, "load1", [(h[:], d["h0"]), (k.consts[:], d["consts"])] + [
                    (t[:], d[n]) for t, n in ((ln_mix, "ln_mix"), (gla_norm, "gla_norm"), (ssd_norm, "ssd_norm"), (w_low, "w_low"),
                                              (w_dt, "w_dt"), (gate_w, "gate_w"), (dt_bias, "dt_bias"), (a_log, "a_log"),
                                              (conv, "conv"), (skip, "skip"))])
                norm_phase(k, "ln1", h, hn_full, ln_mix, 1, KD, L)
                small_products_phase(k, "small", hn_full, w_low, low, w_dt, dt)
                split_phase(k, "ln1_split", hn_full, hn, KD)
            y = sb2("y", [P, 2 * KD, L])
            ssd_prep_phase(k, "prep", dt, dt_bias, a_log, acum, e_acum, to_end, e_total, e_total_m)
            ssd_phase(k, "ssd", hn, d["w_xbc"], conv, skip, dt, acum, e_acum, to_end, e_total, e_total_m, y, mixed)
            product_phase(k, "z", d["w_z"], hn, KD, 2 * KD, L, "times_silu", dst=y)
            norm_phase(k, "ssd_n", y, y, ssd_norm, SSD_GROUPS, 4, L)
            y_pair = pair_of(nc, scan, "y", KD, L)
            for half in range(2):
                product_phase(k, f"ups{half}", d["w_up_ssd"], y_pair, KD, KD, L, "add" if half else "copy", dst=mixed,
                              at=half * D, source=y[:, half * KD:(half + 1) * KD, :])
            product_phase(k, "gb", d["w_gb"], hn, KD, KD, L, "times_gate", dst=mixed)
        k.reset_sems()
        o = sb("o", [P, KD, L])
        gla_phase(k, "gla", hn, low, gate_w, d["wq"], d["wk"], d["wv"], o)
        norm_phase(k, "gla_n", o, o, gla_norm, GLA_HEADS, 2, L)
        product_phase(k, "gout", d["w_gout"], hn, KD, KD, L, "times_silu", dst=o)
        pair = pair_of(nc, ctx, "mixer", KD, L)
        product_phase(k, "upg", d["w_up_gla"], pair, KD, KD, L, "copy", dst=o, source=o)
        product_phase(k, "ga", d["w_ga"], hn, KD, KD, L, "gate_add", dst=mixed, other=o)
        product_phase(k, "out1", d["w_out"], pair, KD, KD, L, "add", dst=h, source=mixed)


def first_experts(k, d, hx):
    nc = k.nc
    with ExitStack() as ctx:
        def sb(n, shape):
            return ctx.enter_context(nc.sbuf_tensor(n, shape, F32))
        hb, chosen = pair_of(nc, ctx, "hb", KD, SEQ), sb("chosen", [P, 3, SEQ])
        ln_final = sb("ln_final", [P, KD])
        early = nc.dram_tensor("early_experts", (NB * GROUP, P, SEQ), F32, kind="Internal").ap()
        with ExitStack() as inner:
            ln_ffn = inner.enter_context(nc.sbuf_tensor("ln_ffn", [P, KD], F32))
            q = inner.enter_context(nc.sbuf_tensor("peer_q", [P, 2 * PEER_HEADS, SEQ], F32))
            keys = inner.enter_context(nc.sbuf_tensor("keys", [P, 2 * PEER_HEADS, KEYS], F32))
            load_phase(k, "load2", [(ln_ffn[:], d["ln_ffn"]), (ln_final[:], d["ln_final"]), (keys[:], d["keys"])])
            norm_phase(k, "ln2", hx, q, ln_ffn, 1, KD, SEQ)
            product_phase(k, "pq", d["w_q"], hb, KD, 2 * PEER_HEADS, SEQ, "copy", dst=q, source=q)
            route_phase(k, "route", q, keys, chosen, hb, d["u"], early)
        w_dram = nc.dram_tensor("expert_weights", (KEYS, KEYS, SEQ), F32, kind="Internal").ap()
        spread_phase(k, "spread", chosen, w_dram)
        expert_phase(k, "experts", hb, d["u"], d["v"], w_dram, early, hx)
        norm_phase(k, "ln3", hx, hx, ln_final, 1, KD, SEQ)


def second_block(k, d, x2):
    nc = k.nc
    with ExitStack() as ctx:
        def sb(n, shape):
            return ctx.enter_context(nc.sbuf_tensor(n, shape, F32))
        x3 = sb("x3", [P, KD, SEQ])
        norms = [sb(f"norm{i}", [P, KD]) for i in range(4)]
        taps = sb("taps", [P, 2 * FT, 4])
        with ExitStack() as inner:
            def sb2(n, shape):
                return inner.enter_context(nc.sbuf_tensor(n, shape, F32))
            k.consts2, sinks = sb2("consts2", [P, CONST2_N]), sb2("sinks", [P, A_HEADS])
            pair = pair_of(nc, inner, "mixer2", KD, SEQ)
            mix = sb2("mix2", [P, KD, SEQ])
            qk = sb2("qk", [P, 12, SEQ])
            gate = sb2("gate", [P, R_HEADS, SEQ])
            key, value = sb2("key", [P, SEQ]), sb2("value", [P, NB, 5 * P])
            load_phase(k, "load3", [(norms[j][:], d[n]) for j, n in enumerate(
                ("mix_pre_norm_2", "mix_post_norm_2", "ffn_pre_norm_2", "ffn_post_norm_2"))] + [
                (k.consts2[:], d["consts2"]), (sinks[:], d["sinks"]), (taps[:], d["taps2"])])
            norm_phase(k, "ln4", x2, mix, norms[0], 1, KD, SEQ)
            product_phase(k, "qk2", d["w_qk2"], pair, KD, 12, SEQ, "copy", dst=qk, source=mix)
            product_phase(k, "gr", d["w_gr"], pair, KD, R_HEADS, SEQ, "silu", dst=gate)
            keys_values_phase(k, "kv2", pair, d["w_kv2"], key, value)
            token_mixers_phase(k, "mixers", qk, key, value, sinks, mix, qk[:, 4:8, :], qk[:, 8:12, :], gate, mix[:, 4:8, :])
            product_phase(k, "out2", d["w_out2"], pair, KD, KD, SEQ, "copy", dst=x3, source=mix)
        norm_phase(k, "ln5", x3, x3, norms[1], 1, KD, SEQ, add=x2)
        y_pair = pair_of(nc, ctx, "y_ff", FT, SEQ)
        with ExitStack() as inner:
            pair = pair_of(nc, inner, "ffn", KD, SEQ)
            norm_phase(k, "ln6", x3, x2, norms[2], 1, KD, SEQ)
            split_phase(k, "ln6_split", x2, pair, KD)
            gated_conv_phase(k, "up", pair, d["w_up2"], taps, y_pair)
        product_phase(k, "down", d["w_down2"], y_pair, FT, KD, SEQ, "copy", dst=x2)
        norm_phase(k, "ln7", x2, x2, norms[3], 1, KD, SEQ, add=x3)


def program(nc, d, out):
    with ExitStack() as ctx:
        k = Core(nc, ctx)
        h = ctx.enter_context(nc.sbuf_tensor("h", [P, KD, L], F32))
        first_mixer(k, d, h)
        k.reset_sems()
        x2 = h[:, :, META:L]
        first_experts(k, d, x2)
        k.reset_sems()
        second_block(k, d, x2)
        store_phase(k, "store", out, x2)


def kernel(**inputs):
    import concourse.bacc as bacc
    from concourse.bass_utils import run_bass_kernel_spmd as run
    nc = bacc.Bacc("TRN2", target_bir_lowering=False, num_devices=1)
    arrays = layout({n: np.asarray(v) for n, v in inputs.items()})
    d = {n: nc.dram_tensor(f"in_{n}", v.shape, mybir.dt.from_np(v.dtype), kind="ExternalInput").ap() for n, v in arrays.items()}
    out = nc.dram_tensor("out_dram", (P, KD, SEQ), F32, kind="ExternalOutput").ap()
    program(nc, d, out)
    r = run(nc, [{f"in_{n}": v for n, v in arrays.items()}], core_ids=[0])
    y = r.results[0]["out_dram"]
    return np.ascontiguousarray(y.transpose(2, 1, 0)).reshape(1, SEQ, D)
```
